# Optimizing a Trainium2 kernel written in Bass

```python
import math
import jax
import jax.numpy as jnp
from jax import lax
import numpy as np

D_MODEL = 1024
BATCH = 1
SEQ = 256
DEPTH = 2
DEC_BATCH = 8
DEC_SEQ = 1
PAST_LEN = 256
PAGE_SIZE = 128

N_EVEN = (DEPTH + 1) // 2
N_ODD = DEPTH // 2
CONV_W = 4
LRU_W = D_MODEL // 2
LRU_BLOCKS = 8
LRU_BW = LRU_W // LRU_BLOCKS
RG_C = 8.0
H_B = 4
DH_B = D_MODEL // (4 * H_B)
ATT_W = H_B * 2 * DH_B
Q_BLOCK = 128
IN_E = 2 * LRU_W + 3 * ATT_W
MIX_E = LRU_W + ATT_W
DK_C = 128
DV_C = 128
H_C = D_MODEL // DK_C
QKV_C = H_C * (2 * DK_C + DV_C)
IN_O = QKV_C + H_C * DV_C + 2 * H_C
CHUNK = 64
D_FF = 2816
N_EXPERTS = 8
TOP_K = 2
D_FF_E = 3584
EPS = 1e-6
NEG_INF = -1e30

kernel_name = "hybrid_rglru_diffattn_gdn_moe_step"

def rmsnorm(x, g):
    xf = x.astype(jnp.float32)
    y = xf * lax.rsqrt(jnp.mean(xf * xf, axis=-1, keepdims=True) + EPS)
    return (y * g.astype(jnp.float32)).astype(x.dtype)

def l2norm(x):
    xf = x.astype(jnp.float32)
    return xf * lax.rsqrt(jnp.sum(xf * xf, axis=-1, keepdims=True) + EPS)

def swiglu(h, wg, wu, wd):
    return (jax.nn.silu(h @ wg) * (h @ wu)) @ wd

def causal_conv(x, buf, w, b=None):
    T = x.shape[1]
    xp = jnp.concatenate([buf.astype(x.dtype), x], axis=1)
    y = xp[:, 0:T] * w[0]
    for j in range(1, CONV_W):
        y = y + xp[:, j:j + T] * w[j]
    if b is not None:
        y = y + b
    return y, xp[:, T:]

def rg_lru(x, h0, wx, bx, wa, ba, lam):
    B, T, _ = x.shape
    xf = x.astype(jnp.float32)
    xb = xf.reshape(B, T, LRU_BLOCKS, LRU_BW)
    gate_x = jax.nn.sigmoid(jnp.einsum('btnc,ncd->btnd', xb, wx.astype(jnp.float32)).reshape(B, T, LRU_W) + bx.astype(jnp.float32))
    gate_a = jax.nn.sigmoid(jnp.einsum('btnc,ncd->btnd', xb, wa.astype(jnp.float32)).reshape(B, T, LRU_W) + ba.astype(jnp.float32))
    log_a = -RG_C * gate_a * jax.nn.softplus(-lam.astype(jnp.float32))
    a = jnp.exp(log_a)
    b = jnp.sqrt(-jnp.expm1(2.0 * log_a)) * (gate_x * xf)
    b = b.at[:, 0].add(a[:, 0] * h0.astype(jnp.float32))
    _, h = lax.associative_scan(lambda l, r: (l[0] * r[0], r[0] * l[1] + r[1]), (a, b), axis=1)
    return h, h[:, -1]

def diff_softmax_mix(q1, q2, k1, k2, v, mask, lam):
    scale = DH_B ** -0.5
    s1 = jnp.einsum('bqhd,bkhd->bhqk', q1, k1).astype(jnp.float32) * scale
    s2 = jnp.einsum('bqhd,bkhd->bhqk', q2, k2).astype(jnp.float32) * scale
    s1 = jnp.where(mask, s1, NEG_INF)
    s2 = jnp.where(mask, s2, NEG_INF)
    p = jax.nn.softmax(s1, axis=-1) - lam * jax.nn.softmax(s2, axis=-1)
    return jnp.einsum('bhqk,bkhe->bqhe', p.astype(v.dtype), v)

def diff_attention_prompt(q1, q2, k1, k2, v, lam):
    B, T, H, d = q1.shape
    nb = T // Q_BLOCK

    def blk(a):
        return a.reshape((B, nb, Q_BLOCK) + a.shape[2:]).swapaxes(0, 1)

    qpos = jnp.arange(T).reshape(nb, Q_BLOCK)
    kpos = jnp.arange(T)

    def body(args):
        q1b, q2b, qp = args
        return diff_softmax_mix(q1b, q2b, k1, k2, v, kpos[None, :] <= qp[:, None], lam)

    o = lax.map(body, (blk(q1), blk(q2), qpos))
    return o.swapaxes(0, 1).reshape(B, T, H, 2 * d)

def even_mixer(h, conv_buf, h0, past_k, past_v, lam_init, w_in, conv_w, conv_b, lru_wx, lru_bx, lru_wa, lru_ba, lru_lambda,
               g_q, g_k, lam_q1, lam_k1, lam_q2, lam_k2, subln_g, w_out):
    B, T, _ = h.shape
    proj = h @ w_in
    gate = proj[..., :LRU_W]
    xr = proj[..., LRU_W:2 * LRU_W]
    q = proj[..., 2 * LRU_W:2 * LRU_W + ATT_W]
    k = proj[..., 2 * LRU_W + ATT_W:2 * LRU_W + 2 * ATT_W]
    v = proj[..., 2 * LRU_W + 2 * ATT_W:]
    xc, conv_new = causal_conv(xr, conv_buf, conv_w, conv_b)
    hs, h_last = rg_lru(xc, h0, lru_wx, lru_bx, lru_wa, lru_ba, lru_lambda)
    y_a = jax.nn.gelu(gate) * hs.astype(h.dtype)
    q = rmsnorm(q.reshape(B, T, H_B, 2, DH_B), g_q)
    k = rmsnorm(k.reshape(B, T, H_B, 2, DH_B), g_k)
    k_rows = k.reshape(B, T, H_B, 2 * DH_B)
    v_rows = v.reshape(B, T, H_B, 2 * DH_B)
    f32 = jnp.float32
    lam = (jnp.exp(jnp.sum(lam_q1.astype(f32) * lam_k1.astype(f32)))
           - jnp.exp(jnp.sum(lam_q2.astype(f32) * lam_k2.astype(f32))) + lam_init)
    if past_k is None:
        o = diff_attention_prompt(q[..., 0, :], q[..., 1, :], k[..., 0, :], k[..., 1, :], v_rows, lam)
    else:
        P = past_k.shape[1]
        k_all = jnp.concatenate([past_k.astype(k_rows.dtype), k_rows], axis=1)
        v_all = jnp.concatenate([past_v.astype(v_rows.dtype), v_rows], axis=1)
        qpos = P + jnp.arange(T)
        kpos = jnp.arange(P + T)
        o = diff_softmax_mix(q[..., 0, :], q[..., 1, :], k_all[..., :DH_B], k_all[..., DH_B:], v_all,
                             kpos[None, :] <= qpos[:, None], lam)
    o = rmsnorm(o, subln_g) * (1.0 - lam_init)
    y = jnp.concatenate([y_a, o.reshape(B, T, ATT_W)], axis=-1) @ w_out
    return y, k_rows, v_rows, conv_new, h_last

def gated_delta_chunked(q, k, v, g, beta, s0):
    B, T, H, _ = q.shape
    n = -(-T // CHUNK)
    pad = n * CHUNK - T

    def to_chunks(a):
        a = jnp.pad(a.astype(jnp.float32), [(0, 0), (0, pad)] + [(0, 0)] * (a.ndim - 2))
        a = a.reshape((B, n, CHUNK) + a.shape[2:])
        return jnp.moveaxis(a, 3, 2)

    q, k, v, g, beta = (to_chunks(a) for a in (q, k, v, g, beta))
    DV = v.shape[-1]
    G = jnp.cumsum(g, axis=-1)
    idx = jnp.arange(CHUNK)
    incl = idx[:, None] >= idx[None, :]
    strict = idx[:, None] > idx[None, :]
    diff = G[..., :, None] - G[..., None, :]
    decay = jnp.where(incl, jnp.exp(jnp.where(incl, diff, 0.0)), 0.0)
    kb = k * beta[..., None]
    A = jnp.where(strict, jnp.einsum('bnhid,bnhjd->bnhij', kb, k) * decay, 0.0)
    rhs = jnp.concatenate([v * beta[..., None], kb * jnp.exp(G)[..., None]], axis=-1)
    sol = lax.linalg.triangular_solve(A + jnp.eye(CHUNK, dtype=jnp.float32), rhs,
                                      left_side=True, lower=True, unit_diagonal=True)
    u, w = sol[..., :DV], sol[..., DV:]
    qk = jnp.einsum('bnhid,bnhjd->bnhij', q, k) * decay
    q_dec = q * jnp.exp(G)[..., None]
    k_dec = k * jnp.exp(G[..., -1:] - G)[..., None]
    g_end = jnp.exp(G[..., -1])
    xs = tuple(jnp.moveaxis(a, 1, 0) for a in (u, w, qk, q_dec, k_dec, g_end))

    def step(S, xs_i):
        u_i, w_i, qk_i, qd_i, kd_i, ge_i = xs_i
        v_new = u_i - jnp.einsum('bhcd,bhde->bhce', w_i, S)
        o_i = jnp.einsum('bhcd,bhde->bhce', qd_i, S) + jnp.einsum('bhij,bhje->bhie', qk_i, v_new)
        S = S * ge_i[..., None, None] + jnp.einsum('bhcd,bhce->bhde', kd_i, v_new)
        return S, o_i

    s_fin, o = lax.scan(step, s0.astype(jnp.float32), xs)
    o = jnp.transpose(o, (1, 0, 3, 2, 4)).reshape(B, n * CHUNK, H, DV)[:, :T]
    return o, s_fin

def odd_mixer(h, conv_buf, s0, w_in, conv_w, a_log, dt_bias, onorm_g, w_out):
    B, T, _ = h.shape
    proj = h @ w_in
    qkv = proj[..., :QKV_C]
    z = proj[..., QKV_C:QKV_C + H_C * DV_C]
    b_pre = proj[..., QKV_C + H_C * DV_C:QKV_C + H_C * DV_C + H_C]
    a_pre = proj[..., QKV_C + H_C * DV_C + H_C:]
    qkv, conv_new = causal_conv(qkv, conv_buf, conv_w)
    qkv = jax.nn.silu(qkv)
    q = qkv[..., :H_C * DK_C].reshape(B, T, H_C, DK_C)
    k = qkv[..., H_C * DK_C:2 * H_C * DK_C].reshape(B, T, H_C, DK_C)
    v = qkv[..., 2 * H_C * DK_C:].reshape(B, T, H_C, DV_C)
    q = l2norm(q) * (DK_C ** -0.5)
    k = l2norm(k)
    beta = jax.nn.sigmoid(b_pre.astype(jnp.float32))
    g = -jnp.exp(a_log.astype(jnp.float32)) * jax.nn.softplus(a_pre.astype(jnp.float32) + dt_bias.astype(jnp.float32))
    o, s_new = gated_delta_chunked(q, k, v, g, beta, s0)
    o = rmsnorm(o.astype(h.dtype), onorm_g) * jax.nn.silu(z.reshape(B, T, H_C, DV_C))
    return o.reshape(B, T, H_C * DV_C) @ w_out, conv_new, s_new

def moe_swiglu(h, router_w, wg, wu, wd):
    logits = (h @ router_w).astype(jnp.float32)
    top_v, top_i = lax.top_k(logits, TOP_K)
    gates = jax.nn.softmax(top_v, axis=-1)
    comb = jnp.sum(jax.nn.one_hot(top_i, N_EXPERTS, dtype=jnp.float32) * gates[..., None], axis=-2)
    out = jnp.zeros_like(h)
    for e in range(N_EXPERTS):
        out = out + comb[..., e:e + 1].astype(h.dtype) * swiglu(h, wg[e], wu[e], wd[e])
    return out

def setup_inputs(seed: int = 0) -> dict:
    key = jax.random.key(seed)
    keys = jax.random.split(key, 64)
    cnt = [0]
    f32 = jnp.float32

    def nk():
        cnt[0] += 1
        return keys[cnt[0] - 1]

    def nrm(shape, scale):
        return scale * jax.random.normal(nk(), shape, f32)

    def gain(shape):
        return 1.0 + 0.05 * jax.random.normal(nk(), shape, f32)

    n_pages = PAST_LEN // PAGE_SIZE
    n_pool = (DEC_BATCH * n_pages * 5) // 4
    perm = jax.random.permutation(nk(), n_pool)
    page_table = perm[:DEC_BATCH * n_pages].reshape(DEC_BATCH, n_pages).astype(jnp.int32)
    u = jax.random.uniform(nk(), (N_EVEN, LRU_W), f32, 0.9, 0.999)
    s = u ** (1.0 / RG_C)
    lru_lambda = jnp.log(s) - jnp.log1p(-s)
    a_log = jnp.log(jax.random.uniform(nk(), (N_ODD, H_C), f32, 1.0, 16.0))
    dt = jnp.exp(jax.random.uniform(nk(), (N_ODD, H_C), f32, math.log(1e-3), math.log(1e-1)))
    dt_bias = dt + jnp.log(-jnp.expm1(-dt))
    return {
        "x_prompt": nrm((BATCH, SEQ, D_MODEL), 1.0),
        "x_sample": nrm((DEC_BATCH, DEC_SEQ, D_MODEL), 1.0),
        "cache_k": nrm((N_EVEN, n_pool, PAGE_SIZE, H_B, 2 * DH_B), 1.0),
        "cache_v": nrm((N_EVEN, n_pool, PAGE_SIZE, H_B, 2 * DH_B), 1.0),
        "state_lru_conv": nrm((N_EVEN, DEC_BATCH, CONV_W - 1, LRU_W), 1.0),
        "state_lru_h": nrm((N_EVEN, DEC_BATCH, LRU_W), 0.5),
        "state_delta_conv": nrm((N_ODD, DEC_BATCH, CONV_W - 1, QKV_C), 1.0),
        "state_delta_s": nrm((N_ODD, DEC_BATCH, H_C, DK_C, DV_C), 0.1),
        "page_table": page_table,
        "ln_mix_e": gain((N_EVEN, D_MODEL)),
        "w_in_e": nrm((N_EVEN, D_MODEL, IN_E), D_MODEL ** -0.5),
        "conv_lru_w": nrm((N_EVEN, CONV_W, LRU_W), 0.5),
        "conv_lru_b": nrm((N_EVEN, LRU_W), 0.01),
        "lru_wx": nrm((N_EVEN, LRU_BLOCKS, LRU_BW, LRU_BW), LRU_BW ** -0.5),
        "lru_bx": nrm((N_EVEN, LRU_W), 0.01),
        "lru_wa": nrm((N_EVEN, LRU_BLOCKS, LRU_BW, LRU_BW), LRU_BW ** -0.5),
        "lru_ba": nrm((N_EVEN, LRU_W), 0.01),
        "lru_lambda": lru_lambda,
        "qk_gain_q": gain((N_EVEN, DH_B)),
        "qk_gain_k": gain((N_EVEN, DH_B)),
        "lam_q1": nrm((N_EVEN, DH_B), 0.1),
        "lam_k1": nrm((N_EVEN, DH_B), 0.1),
        "lam_q2": nrm((N_EVEN, DH_B), 0.1),
        "lam_k2": nrm((N_EVEN, DH_B), 0.1),
        "subln_g": gain((N_EVEN, 2 * DH_B)),
        "w_out_e": nrm((N_EVEN, MIX_E, D_MODEL), MIX_E ** -0.5),
        "ln_ffn_e": gain((N_EVEN, D_MODEL)),
        "ffn_wg": nrm((N_EVEN, D_MODEL, D_FF), D_MODEL ** -0.5),
        "ffn_wu": nrm((N_EVEN, D_MODEL, D_FF), D_MODEL ** -0.5),
        "ffn_wd": nrm((N_EVEN, D_FF, D_MODEL), D_FF ** -0.5),
        "ln_mix_o": gain((N_ODD, D_MODEL)),
        "w_in_o": nrm((N_ODD, D_MODEL, IN_O), D_MODEL ** -0.5),
        "conv_delta_w": nrm((N_ODD, CONV_W, QKV_C), 0.5),
        "a_log": a_log,
        "dt_bias": dt_bias,
        "onorm_g": gain((N_ODD, DV_C)),
        "w_out_o": nrm((N_ODD, H_C * DV_C, D_MODEL), (H_C * DV_C) ** -0.5),
        "ln_ffn_o": gain((N_ODD, D_MODEL)),
        "router_w": nrm((N_ODD, D_MODEL, N_EXPERTS), D_MODEL ** -0.5),
        "moe_wg": nrm((N_ODD, N_EXPERTS, D_MODEL, D_FF_E), D_MODEL ** -0.5),
        "moe_wu": nrm((N_ODD, N_EXPERTS, D_MODEL, D_FF_E), D_MODEL ** -0.5),
        "moe_wd": nrm((N_ODD, N_EXPERTS, D_FF_E, D_MODEL), D_FF_E ** -0.5),
    }

def reference(x_prompt, x_sample, cache_k, cache_v, state_lru_conv, state_lru_h, state_delta_conv, state_delta_s,
              page_table, ln_mix_e, w_in_e, conv_lru_w, conv_lru_b, lru_wx, lru_bx, lru_wa, lru_ba, lru_lambda,
              qk_gain_q, qk_gain_k, lam_q1, lam_k1, lam_q2, lam_k2, subln_g, w_out_e, ln_ffn_e, ffn_wg, ffn_wu, ffn_wd,
              ln_mix_o, w_in_o, conv_delta_w, a_log, dt_bias, onorm_g, w_out_o, ln_ffn_o, router_w, moe_wg, moe_wu, moe_wd):
    bp = x_prompt.shape[0]
    bs = x_sample.shape[0]
    past_len = page_table.shape[1] * PAGE_SIZE
    xp, xs = x_prompt, x_sample
    kp_l, vp_l, cp_l, hp_l, dcp_l, dsp_l = [], [], [], [], [], []
    ks_l, vs_l, cs_l, hs_l, dcs_l, dss_l = [], [], [], [], [], []
    for layer in range(DEPTH):
        i = layer // 2
        if layer % 2 == 0:
            lam_init = 0.8 - 0.6 * math.exp(-0.3 * layer)
            we = (w_in_e[i], conv_lru_w[i], conv_lru_b[i], lru_wx[i], lru_bx[i], lru_wa[i], lru_ba[i], lru_lambda[i],
                  qk_gain_q[i], qk_gain_k[i], lam_q1[i], lam_k1[i], lam_q2[i], lam_k2[i], subln_g[i], w_out_e[i])
            past_k = cache_k[i, page_table].reshape(bs, past_len, H_B, 2 * DH_B)
            past_v = cache_v[i, page_table].reshape(bs, past_len, H_B, 2 * DH_B)
            yp, kp, vp, cp, hp = even_mixer(rmsnorm(xp, ln_mix_e[i]), jnp.zeros((bp, CONV_W - 1, LRU_W), xp.dtype),
                                            jnp.zeros((bp, LRU_W), jnp.float32), None, None, lam_init, *we)
            ys, ks, vs, cs, hs = even_mixer(rmsnorm(xs, ln_mix_e[i]), state_lru_conv[i], state_lru_h[i],
                                            past_k, past_v, lam_init, *we)
            xp = xp + yp
            xs = xs + ys
            kp_l.append(kp); vp_l.append(vp); cp_l.append(cp); hp_l.append(hp)
            ks_l.append(ks); vs_l.append(vs); cs_l.append(cs); hs_l.append(hs)
            xp = xp + swiglu(rmsnorm(xp, ln_ffn_e[i]), ffn_wg[i], ffn_wu[i], ffn_wd[i])
            xs = xs + swiglu(rmsnorm(xs, ln_ffn_e[i]), ffn_wg[i], ffn_wu[i], ffn_wd[i])
        else:
            wo = (w_in_o[i], conv_delta_w[i], a_log[i], dt_bias[i], onorm_g[i], w_out_o[i])
            yp, dcp, dsp = odd_mixer(rmsnorm(xp, ln_mix_o[i]), jnp.zeros((bp, CONV_W - 1, QKV_C), xp.dtype),
                                     jnp.zeros((bp, H_C, DK_C, DV_C), jnp.float32), *wo)
            ys, dcs, dss = odd_mixer(rmsnorm(xs, ln_mix_o[i]), state_delta_conv[i], state_delta_s[i], *wo)
            xp = xp + yp
            xs = xs + ys
            dcp_l.append(dcp); dsp_l.append(dsp); dcs_l.append(dcs); dss_l.append(dss)
            xp = xp + moe_swiglu(rmsnorm(xp, ln_ffn_o[i]), router_w[i], moe_wg[i], moe_wu[i], moe_wd[i])
            xs = xs + moe_swiglu(rmsnorm(xs, ln_ffn_o[i]), router_w[i], moe_wg[i], moe_wu[i], moe_wd[i])
    return (xp, xs,
            jnp.stack(kp_l), jnp.stack(vp_l), jnp.stack(cp_l), jnp.stack(hp_l), jnp.stack(dcp_l), jnp.stack(dsp_l),
            jnp.stack(ks_l), jnp.stack(vs_l), jnp.stack(cs_l), jnp.stack(hs_l), jnp.stack(dcs_l), jnp.stack(dss_l))


_drawn_inputs = setup_inputs


def setup_inputs(seed=0):
    import zlib

    import numpy as np

    out = dict(_drawn_inputs(seed))
    spreads = {}
    factors = {'lru_bx': 8.0, 'lru_ba': 4.056, 'lam_k1': 8.0, 'lam_k2': 4.104}
    for name, (base, spread) in spreads.items():
        noise = np.random.default_rng([zlib.crc32(name.encode()), seed]).standard_normal(out[name].shape)
        drawn = base * np.exp(spread * noise) if base else spread * noise
        out[name] = jnp.asarray(drawn.astype(out[name].dtype))
    for name, factor in factors.items():
        out[name] = (out[name] * factor).astype(out[name].dtype)
    return out
```

```python
import math
from contextlib import ExitStack

import concourse.bass as bass
from concourse import mybir

F32 = mybir.dt.float32
I32 = mybir.dt.int32
U32 = mybir.dt.uint32
ACT = mybir.ActivationFunctionType
ALU = mybir.AluOpType
X = mybir.AxisListType.X

P = 128
CHUNK_COLS = 512
SLOTS = 7
EPS = 1e-6
MASKED = -1e30
RG_C = 8.0
LAM_INIT = 0.8 - 0.6 * math.exp(-0.3 * 0)


def program(nc, A, O):
    TP, D = A["x_prompt"].shape[1:]
    TS = A["x_sample"].shape[0]
    T = TP + TS
    KD = D // P
    TT = TP // P
    TOK = [(i * P, P) for i in range(TT)] + [(TP, TS)]
    LW = A["lru_bx"].shape[1]
    NL = LW // P
    HB, E2 = A["cache_k"].shape[3:]
    DH = E2 // 2
    AW = HB * E2
    NP_ = A["page_table"].shape[1]
    NPOOL = A["cache_k"].shape[1]
    CW = A["conv_lru_w"].shape[1]
    HIST = CW - 1
    IN_E = A["w_in_e"].shape[2]
    FF = A["ffn_wg"].shape[2]
    NF = FF // P
    _, _, HC, DK, DV = A["state_delta_s"].shape
    QKV = A["conv_delta_w"].shape[2]
    NQ = QKV // P
    NE = A["router_w"].shape[2]
    FE = A["moe_wg"].shape[3]
    NCH = FE // CHUNK_COLS
    HH = 2 * HB
    NB = TS * HB
    assert D == KD * P and TP == TT * P and TT == 2 and E2 == P and NP_ == 2 and FE % CHUNK_COLS == 0
    TAIL = HIST + TS

    with ExitStack() as ctx:
        def sb(name, shape, dt=F32):
            return ctx.enter_context(nc.sbuf_tensor(name, shape, dt))

        sems, step_at, given = {}, {}, {}

        def sem(name):
            if name not in sems:
                sems[name] = ctx.enter_context(nc.semaphore(name))
            return sems[name]

        def sig(name):
            if name not in step_at:
                return sem(name)
            engine, first, count = step_at[name]
            assert given.get(engine, 0) == first + given.get(name, 0) and given.get(name, 0) < count, (name, given.get(engine, 0), first)
            given[engine] = given.get(engine, 0) + 1
            given[name] = given.get(name, 0) + 1
            return sem(engine)

        def at(name, count=1):
            if name not in step_at:
                return sem(name), count
            engine, first, most = step_at[name]
            assert 0 < count <= most, (name, count)
            return sem(engine), first + count

        def order(engine, *events):
            first = 0
            for name, count in events:
                step_at[name] = (engine, first, count)
                first += count

        order("scalar_steps",
              ("xT_done", KD), ("norm0_sq", 1), ("lam_absexp", 1), ("norm0_root", 1), ("proj_done", IN_E // P),
              ("lru_gates", 2 * NL), ("lru_a", 2), ("gelu", 1), ("lru_root", 1), ("qk_sq", 1), ("qk_root", HH),
              ("lam_exp", 1), ("ktok", 3), ("vtok", 3), ("qs_tok", 1), ("tail_tok", 1), ("ss", 1), ("exps_s", 2),
              ("exps", 2 * HH), ("o_sq", 1), ("o_root", HB), ("norm1_sq", 1), ("norm1_root", 1), ("ffn_sil", NF),
              ("norm2_sq", 1), ("norm2_root", 1), ("beta", 1), ("g_absexp", 1), ("ealog", 1),
              ("dtail", QKV // CHUNK_COLS), ("l2_sq", 2), ("l2_root", 1), ("eG", 1), ("s_egb", 1), ("s_qks", 1),
              ("on_sq", 1), ("on_root", 1), ("norm3_sq", 1), ("norm3_root", 1), ("gate_exp", 1),
              ("xtok", 6), ("htok", 6))
        order("tensor_steps",
              ("par_psum", 1), ("xT_psum", KD), ("norm0_ss", 1), ("proj_psum", IN_E // P), ("lru_gate_psum", 2 * NL),
              ("qk_ss", HH), ("lam_psum", 1), ("ktok_psum", 3), ("vtok_psum", 3), ("qs_psum", 1), ("tail_psum", 1),
              ("hlast_psum", 1), ("qb_psum", TS), ("ss_psum", 1), ("self_psum", 1), ("pT_s_psum", 1),
              ("scores_psum", HH), ("o_ss", HB), ("out_e_psum", KD), ("norm1_ss", 1), ("ffn_d_psum", KD),
              ("dhist_psum", 1), ("norm2_ss", 1), ("ba_psum", 1), ("qkvz_psum", NQ + HC),
              ("dtail_psum", QKV // CHUNK_COLS), ("l2_used", 1), ("l2_ss", 1), ("Gt_psum", 1), ("l2_b", 2 * HC),
              ("s_gb", 1), ("s_qk", 1), ("on_ss", 1), ("on_b", HC), ("out_o_psum", KD), ("norm3_ss", 1),
              ("iota_psum", 1), ("logits_psum", 1), ("xtok_psum", 6), ("htok_psum", 6), ("ranks_psum", 1))
        order("vector_steps",
              ("par_done", 1), ("lam_abs", 1), ("norm0_done", 1), ("xc_done", 1), ("lru_y", 1), ("lru_m", 1),
              ("lru_done", 1), ("qk_done", 1), ("hlast", 1), ("k_pages_used", TS), ("qk_self", 1), ("neg_max_s", 1),
              ("p_s", 1), ("pT_s", 1), ("o_sample", 1), ("scores", HH), ("neg_max", 1), ("probs", HB),
              ("mix_done", 1), ("out_e_added", KD), ("norm1_done", 1), ("ffn_act", NF), ("ffn_added", KD),
              ("norm2_done", 1), ("ba_read", 1), ("g_abs", 1), ("g", 1), ("dconv", NQ), ("Gt", 1), ("l2_inv", 1),
              ("l2_applied", 2 * HC), ("s_prod", 1), ("on_inv", 1), ("on_applied", HC), ("on_done", 1),
              ("out_o_added", KD), ("norm3_done", 1), ("iota", 1), ("top_diff", 1), ("masks", 1), ("ranks", 1))

        ring = sb("weight_ring", [P, SLOTS, KD * CHUNK_COLS])
        ident = sb("ident", [P, P])
        ones = sb("ones", [P, P])
        halves = sb("halves", [P, P])
        half2 = sb("half2", [P, 2])
        le_mask = sb("le_mask", [P, P])
        lt_mask = sb("lt_mask", [P, P])
        causal = sb("causal", [P, 3 * P])
        eps_t = sb("eps_t", [P, 1])
        par = sb("par", [P, P])
        cd = sb("cd", [P, P])
        small = sb("small", [P, 320])
        xT = sb("xT", [P, KD, T])
        hT = sb("hT", [P, KD, T])
        W = 17700
        work = sb("work", [P, W])
        bank = [ctx.enter_context(nc.psum_tensor(f"bank{i}", [P, CHUNK_COLS], F32)) for i in range(8)]

        class Arena:

            def __init__(self):
                self.at = 0

            def take(self, *dims):
                n = math.prod(dims)
                v = work[:, self.at:self.at + n]
                self.at += n
                assert self.at <= W, self.at
                names = "abcd"[:len(dims)]
                if len(dims) > 1:
                    v = v.rearrange(f"p ({' '.join(names)}) -> p {' '.join(names)}", **dict(zip(names, dims)))
                return v

        rows, row = {}, 0
        for name, ap in (("ln_mix_e", A["ln_mix_e"]), ("conv_lru_w", A["conv_lru_w"]), ("conv_lru_b", A["conv_lru_b"]),
                         ("lru_bx", A["lru_bx"]), ("lru_ba", A["lru_ba"]), ("lru_lambda", A["lru_lambda"]),
                         ("ln_ffn_e", A["ln_ffn_e"]), ("ln_mix_o", A["ln_mix_o"]), ("ln_ffn_o", A["ln_ffn_o"]),
                         ("subln_g", A["subln_g"]), ("onorm_g", A["onorm_g"])):
            n = math.prod(ap.shape)
            rows[name] = (row, n // P, ap)
            row += n // P
        r_gq, r_gk, r_lq, r_lk = row, row + 1, row + 2, row + 3
        N_ROWS = row + 4
        N_CD = CW * NQ

        def col(name, i=0):
            return par[:, rows[name][0] + i:rows[name][0] + i + 1]

        sm_at = [0]

        def vec(n):
            v = small[:, sm_at[0]:sm_at[0] + n]
            sm_at[0] += n
            assert sm_at[0] <= 320
            return v

        def cols(ap, c0, n):
            return ap[:, c0:c0 + n].rearrange("(j p) n -> p j n", p=P)

        def chunk_rows(ap, r0, n):
            return ap[r0:r0 + n, :].rearrange("(j p) n -> p j n", p=P)

        dense = []
        place = {}

        def stream_cols(name, ap, total, n):
            c0 = n * CHUNK_COLS
            w = min(CHUNK_COLS, total - c0)
            place[name, n] = len(dense)
            dense.append((cols(ap, c0, w), KD, w))

        for n in range(IN_E // CHUNK_COLS):
            stream_cols("w_in_e", A["w_in_e"][0], IN_E, n)
        for n in range(D // CHUNK_COLS):
            stream_cols("w_out_e", A["w_out_e"][0], D, n)
        NFC = -(-FF // CHUNK_COLS)
        for n in range(NFC):
            stream_cols("ffn_wg", A["ffn_wg"][0], FF, n)
            stream_cols("ffn_wu", A["ffn_wu"][0], FF, n)
        JD = KD * CHUNK_COLS // D
        for n in range(-(-NF // JD)):
            j = min(JD, NF - n * JD)
            place["ffn_wd", n] = len(dense)
            dense.append((chunk_rows(A["ffn_wd"][0], n * JD * P, j * P), j, D))
        NQC = (QKV + D) // CHUNK_COLS
        for n in range(NQC):
            stream_cols("w_in_o", A["w_in_o"][0], QKV + D, n)
        for n in range(D // CHUNK_COLS):
            stream_cols("w_out_o", A["w_out_o"][0], D, n)
        ND = len(dense)

        def slot_view(i, k, w):
            return ring[:, i % SLOTS, 0:k * w].rearrange("p (j n) -> p j n", j=k)

        def chunk(name, n):
            i = place[name, n]
            return slot_view(i, dense[i][1], dense[i][2])

        def wait_chunk(eng, i):
            eng.wait_ge(sig(f"slot{i % SLOTS}_loaded"), 16 * (i // SLOTS + 1))

        a0 = Arena()
        proj = a0.take(IN_E // P, T)
        mixT = proj[:, 0:KD, :]
        inv = a0.take(KD, T)
        pages_kv = a0.take(4, NP_, AW)
        scr = a0.take(3 * D)
        ktok = a0.take(3, AW)
        vtok = a0.take(3, AW)
        lru_w = vtok.rearrange("p a b -> p (a b)")[:, 0:2 * NL * P].rearrange(
            "p (a b c) -> p a b c", a=2, b=NL)
        GATE, XR, Q_, K_, V_ = 0, NL, 2 * NL, 2 * NL + HB, 2 * NL + 2 * HB
        x_tok = scr.rearrange("p (t d) -> p t d", t=3)
        kt_flat = ktok.rearrange("p a b -> p (a b)")
        par_rows, cd_rows = kt_flat[:, 0:P], kt_flat[:, P:2 * P]
        hist_rows = kt_flat[0:TS * HIST, 2 * P:2 * P + LW]
        h0_rows = kt_flat[0:TS, 2 * P + LW:2 * P + 2 * LW]
        kv_flat = pages_kv.rearrange("p a b c -> p (a b c)")
        xc = kv_flat[:, 0:NL * T].rearrange("p (a b) -> p a b", a=NL)
        decay_a = kv_flat[:, NL * T:2 * NL * T].rearrange("p (a b) -> p a b", a=NL)
        gate_x = inv[:, 0:NL, :]
        gate_a = inv[:, NL:2 * NL, :]
        tanh_y = scr[:, 0:NL * T].rearrange("p (a b) -> p a b", a=NL)
        tmp_l = scr[:, NL * T:2 * NL * T].rearrange("p (a b) -> p a b", a=NL)
        hist = vec(NL * TS * HIST).rearrange("p (a b c) -> p a b c", a=NL, b=TS)
        h0 = vec(NL * TS).rearrange("p (a b) -> p a b", a=NL)
        sp8 = vec(NL)
        v_s = [vec(NL) for _ in range(3)]
        lamv = vec(1)
        lam_e = vec(2)
        nlam = vec(1)
        mx = vec(2 * HH)
        ssum = vec(2 * HH)
        rsum = vec(2 * HH)
        subg = vec(1)
        mx_s, ssum_s, rsum_s = vec(2), vec(2), vec(2)
        sc_p = scr[:, 0:HH * 3 * P].rearrange("p (i c) -> p i c", i=HH)
        inv_flat = inv.rearrange("p a b -> p (a b)")
        pT = [inv_flat[:, k * 384:k * 384 + 3 * P] for k in range(2)]
        kv_mul = inv_flat[:, 0:NP_ * AW].rearrange("p (a b) -> p a b", a=NP_)
        qs_tok = inv_flat[0:TS, 1024:1024 + AW]
        tail_tok = inv_flat[0:TAIL, 1536:1536 + LW]
        sc_s = scr[:, 0:NP_ * HH * TS].rearrange("p (g i h b) -> p g i h b", g=NP_, i=2, h=HB)
        qk_s = scr[:, 256:256 + NB].rearrange("p (h b) -> p h b", h=HB)
        NK_S = NP_ * P + 1
        ss = scr[0:NB, 512:512 + 2 * NK_S].rearrange("p (i c) -> p i c", i=2)
        pT_s = scr[:, 1100:1100 + NP_ * NB].rearrange("p (g n) -> p g n", g=NP_)
        pself = scr[:, 1200:1200 + NB]
        osq = scr[:, 1300:1300 + HB * T].rearrange("p (h t) -> p h t", h=HB)
        hl = vec(NL * (TS + 1)).rearrange("p (a b) -> p a b", a=NL)
        hl_tok = scr[0:TS + 1, 2560:2560 + LW]
        act = work[:, 0:NF * T].rearrange("p (a b) -> p a b", a=NF)
        sil = scr[:, 0:2 * T].rearrange("p (a b) -> p a b", a=2)
        pg_sb = sb("page_numbers", [1, TS * NP_], I32)


        def shaped(v, dims):
            names = "abcd"[:len(dims)]
            return v if len(dims) == 1 else v.rearrange(f"p ({' '.join(names)}) -> p {' '.join(names)}", **dict(zip(names, dims)))

        def cut(o, *dims):
            return shaped(work[:, o:o + math.prod(dims)], dims)

        NGROUPS = TT * HC // 4
        NG = 4
        LEVELS = 7
        GRP = NG * P
        INV0 = (IN_E // P) * T
        QKV0 = INV0 + KD * T
        TMP0 = QKV0 + NQ * T
        A_0 = HC * T + HC * P
        B_0 = TMP0 + LEVELS * P
        zT = cut(0, HC, T)
        pre = cut(HC * T, 4, T)
        S_pr = cut(HC * T, HC, P)
        qkvT = cut(QKV0, NQ, T)
        qT, kT, vT = qkvT[:, 0:HC, :], qkvT[:, HC:2 * HC, :], qkvT[:, 2 * HC:3 * HC, :]
        oT = hT
        dhist_rows = work[0:TS * HIST, TMP0:TMP0 + QKV]
        tail_rows = work[0:TAIL, TMP0:TMP0 + QKV]
        tailT = cut(TMP0 + QKV, NQ, TAIL)
        dhist = cut(TMP0 + QKV + NQ * TAIL, NQ, TS, HIST)
        lvl = cut(TMP0, LEVELS, P)
        Gb, EA, QK, Tm = (cut(A_0 + k * GRP, NG, P) for k in range(4))
        Tt, Am, KB, KDc, VB, QD = (cut(B_0 + k * GRP, NG, P) for k in range(6))
        Yb, NW, VN = Gb, Tm, Am
        s_ring = [cut(A_0, TS, P), cut(A_0 + 2 * GRP, TS, P), cut(B_0, TS, P), cut(B_0 + 2 * GRP, TS, P)]
        v_diag = cut(B_0 + 4 * GRP, TS, P)
        assert A_0 + 4 * GRP <= INV0 and B_0 + 6 * GRP <= W and TMP0 + QKV + NQ * (TAIL + TS * HIST) <= W
        gt_mask = sb("gt_mask", [P, P])
        w_ba = sb("w_ba", [P, KD, 2 * HC])
        w_router = sb("w_router", [P, KD, NE])
        alog_b = sb("alog_b", [P, HC])
        dt_b = sb("dt_b", [P, HC])
        NS1 = 600
        sm1 = sb("sm1", [P, NS1])
        sm1_at = [0]

        def vec1(*dims):
            n = math.prod(dims)
            v = sm1[:, sm1_at[0]:sm1_at[0] + n]
            sm1_at[0] += n
            assert sm1_at[0] <= NS1
            return shaped(v, dims)

        NTT = TT + 1
        pick = vec1(4 * HC - 1)
        ba = vec1(NTT, 2 * HC)
        beta = vec1(NTT, HC)
        g_t = vec1(NTT, HC)
        sp_t = [vec1(NTT, HC) for _ in range(3)]
        Gt = vec1(TT, HC)
        eG = vec1(TT, HC)
        bkb = vec1(TT, HC)
        kd_s = vec1(HC)
        ge = vec1(HC)
        gd = vec1(2, HC, TS)
        egb = vec1(2, HC, TS)
        qks = vec1(HC, TS)
        k_row = inv[0:TS, 1, 0:P]
        vn_s = vec1(TS)
        vn_t = vec1(TS)


        NSTEP = FE // CHUNK_COLS
        KF = CHUNK_COLS // P
        CAP = P
        PASSES = -(-T // CAP)
        YC = D // CHUNK_COLS
        acc = cut(0, NTT, D)
        m_act = cut(NTT * D, 2, CHUNK_COLS)
        m_sil = cut(NTT * D + 2 * CHUNK_COLS, 2, CHUNK_COLS)
        assert NTT * D + 4 * CHUNK_COLS <= INV0
        h_tok = cut(QKV0, NTT, D)
        hTe = cut(QKV0 + NTT * D, KD, CAP)
        mo = [QKV0 + NTT * D + KD * CAP]

        def more_of(*dims):
            v = cut(mo[0], *dims)
            mo[0] += math.prod(dims)
            assert mo[0] <= W
            return v

        m_actT = more_of(2, KF, CAP)
        sel = more_of(NTT, CAP)
        selw = more_of(NTT, CAP)
        WT = more_of(T)
        y_e = more_of(D)
        iota = more_of(P)
        logit = more_of(NTT, NE)
        top = more_of(NTT, NE)
        top_i = more_of(NTT, NE).bitcast(U32)
        idx_f = more_of(NTT, 2)
        gates = more_of(NTT, 2)
        comb = more_of(NTT, NE)
        comb2 = more_of(NTT, NE)
        mask = more_of(NTT, NE)
        rank = more_of(NTT, NE)
        count = more_of(1)
        count_i = more_of(1).bitcast(I32)
        spare = more_of(8)
        FAR = 16384.0
        order_e = [("g", 0), ("u", 0)]
        for c in range(1, NSTEP):
            order_e += [("g", c), ("u", c), ("d", c - 1)]
        order_e.append(("d", NSTEP - 1))
        PER = len(order_e)
        assert ND % SLOTS == 0 and PER % SLOTS == 0
        e_at = {k: i for i, k in enumerate(order_e)}

        def e_slot(kind, c):
            k = JD if kind == "d" else KD
            w = D if kind == "d" else CHUNK_COLS
            return slot_view(e_at[kind, c], k, w)

        def wait_e_chunk(eng, it, kind, c):
            i = e_at[kind, c]
            eng.wait_ge(*at(f"slot{i % SLOTS}_loaded", it * (16 * (PER // SLOTS)) + 16 * (ND // SLOTS + i // SLOTS + 1)))

        N_PAR = len(rows) + 11
        OUTS = 8
        block = ctx.enter_context(nc.Block())
        V, SC, PE, GP = nc.vector, nc.scalar, nc.tensor, nc.gpsimd

        @block.sync
        def _(sp):
            for i, (src, k, w) in enumerate(dense):
                if i >= SLOTS:
                    sp.wait_ge(*at("chunk_used", i - SLOTS + 1))
                sp.dma_start(slot_view(i, k, w), src).then_inc(sig(f"slot{i % SLOTS}_loaded"), 16)

            def load_expert(e, it, first):
                for i, (kind, c) in enumerate(order_e):
                    if i >= SLOTS:
                        k, cc = order_e[i - SLOTS]
                        sp.wait_ge(*at(f"moe_{k}", it * NSTEP + cc + 1))
                    elif first:
                        sp.wait_ge(*at("chunk_used", ND - SLOTS + i + 1))
                    else:
                        k, cc = order_e[i - SLOTS + PER]
                        sp.wait_ge(*at(f"moe_{k}", it * NSTEP + (cc + 1 - NSTEP)))
                    if kind == "d":
                        src = A["moe_wd"][0, e, c * CHUNK_COLS:(c + 1) * CHUNK_COLS, :]
                    else:
                        src = A["moe_w" + kind][0, e, :, c * CHUNK_COLS:(c + 1) * CHUNK_COLS]
                    sp.dma_start(e_slot(kind, c), src.rearrange("(j p) n -> p j n", p=P)).then_inc(sig(f"slot{i % SLOTS}_loaded"), 16)

            load_expert(0, 0, True)
            with sp.Fori(1, NE) as e:
                load_expert(e, e, False)
            sp.wait_ge(*at("flag", 1))
            with sp.If(sp.value_load(count_i[0:1, 0:1], min_val=0, max_val=T) > CAP):
                with sp.Fori(1, PASSES) as p:
                    with sp.Fori(0, NE) as e:
                        load_expert(e, p * NE + e, False)
            sp.wait_ge(*at("y_ready", 1))
            sp.dma_start(O["y_prompt"][0].rearrange("(t p) d -> p t d", p=P), acc[:, 0:TT, :]).then_inc(sig("y_written"), 16)
            sp.dma_start(O["y_sample"].rearrange("b t d -> (b t) d"), acc[0:TS, TT, :]).then_inc(sig("y_written"), 16)
            sp.wait_ge(*at("y_written", 32))

        @block.gpsimd
        def _(gp):
            GP.memset(ident[:], 0.0)
            GP.memset(ones[:], 1.0)
            GP.memset(halves[:], 0.0)
            GP.memset(half2[:], 0.0)
            GP.memset(le_mask[:], 1.0)
            GP.memset(lt_mask[:], 1.0)
            GP.memset(gt_mask[:], 1.0)
            GP.memset(sm1[:], 0.0)
            GP.memset(causal[:], 0.0)
            GP.memset(eps_t[:], EPS)
            GP.memset(lru_w, 0.0).then_inc(sig("gp_filled"), 1)
            gp.wait_ge(*at("gp_filled", 1))
            GP.affine_select(out=ident[:], in_=ident[:], compare_op=ALU.not_equal, fill=1.0, base=0,
                             pattern=[[-1, P]], channel_multiplier=1)
            for m, base in ((le_mask, 0), (lt_mask, -1)):
                GP.affine_select(out=m[:], in_=m[:], compare_op=ALU.is_ge, fill=0.0, base=base,
                                 pattern=[[1, P]], channel_multiplier=-1)
            GP.affine_select(out=gt_mask[:], in_=gt_mask[:], compare_op=ALU.is_ge, fill=0.0, base=-1,
                             pattern=[[-1, P]], channel_multiplier=1)
            for c in (0, 2):
                last = GP.affine_select(out=causal[:, c * P:(c + 1) * P], in_=causal[:, c * P:(c + 1) * P],
                                        compare_op=ALU.is_ge, fill=MASKED, base=0, pattern=[[-1, P]], channel_multiplier=1)
            last.then_inc(sig("gp_filled"), 1)
            gp.wait_ge(*at("gp_filled", 2))
            for k in range(2):
                GP.memset(halves[k * DH:(k + 1) * DH, k * DH:(k + 1) * DH], 1.0)
                GP.memset(half2[k * DH:(k + 1) * DH, k:k + 1], 1.0).then_inc(sig("constants"), 1)
            for g, name in enumerate(("lru_wx", "lru_wa")):
                w = A[name][0].rearrange("(t k) c d -> k c t d", k=2)
                for k in range(2):
                    gp.dma_start(lru_w[k * DH:(k + 1) * DH, g, :, k * DH:(k + 1) * DH], w[k])\
                      .then_inc(sig("lru_w_loaded"), 16)
            gp.dma_start(pg_sb[:], A["page_table"].rearrange("(o b) g -> o (b g)", o=1)).then_inc(sig("pages_loaded"), 16)
            gp.wait_ge(*at("pages_loaded", 16))
            gp.wait_ge(*at("lru_done", 1))
            for n in range(2 * TS):
                b, src = n % TS, A["cache_k" if n < TS else "cache_v"]
                if n >= 4:
                    if n - 4 < TS:
                        gp.wait_ge(*at("k_pages_used", n - 3))
                    else:
                        gp.wait_ge(*at("v_pages_used", n - 3 - TS))
                for g in range(NP_):
                    r = gp.value_load(pg_sb[0:1, b * NP_ + g:b * NP_ + g + 1], min_val=0, max_val=NPOOL - 1)
                    gp.dma_start(pages_kv[:, n % 4, g, :], src[0, r].rearrange("t h e -> t (h e)"))\
                      .then_inc(sig(f"kv{n % 4}_loaded"), 16)

            gp.wait_ge(*at("tail_written", 32))
            GP.memset(lvl, 0.0).then_inc(sig("gp_filled"), 1)
            gp.wait_ge(*at("gp_filled", 3))
            for n in range(LEVELS):
                s = 1 << n
                last = GP.memset(lvl[:, n, :].rearrange("p (k c) -> p k c", c=2 * s)[:, :, 0:s], 1.0)
            last.then_inc(sig("gp_filled"), 1)
            for k in range(2):
                gp.wait_ge(*at("gp_filled", 4 + k))
                for n in range(LEVELS):
                    s = 1 << n
                    m = lvl[:, n, :].rearrange("p (k c) -> p k c", c=2 * s)[:, :, 0:s]
                    base, cm = ((-s, 1), (2 * s - 1, -1))[k]
                    last = GP.affine_select(out=m, in_=m, compare_op=ALU.is_ge, fill=0.0, base=base,
                                            pattern=[[-cm * 2 * s, P // (2 * s)], [0, s]], channel_multiplier=cm)
                last.then_inc(sig("gp_filled" if k == 0 else "levels"), 1)
            gp.wait_ge(*at("d_done", 2 * NGROUPS))
            for h in range(HC):
                if h >= 4:
                    gp.wait_ge(*at(f"state{h % 4}_written", 16))
                gp.dma_start(s_ring[h % 4], A["state_delta_s"][0, :, h].rearrange("b d e -> d b e"))\
                  .then_inc(sig(f"state{h % 4}_loaded"), 16)

        def softplus(dve, link, out, z, tmp, abs_sig, exp_sig, sign):
            t, s, s2 = tmp
            V.tensor_scalar(out, z, sign, 0.0, ALU.mult, ALU.max)
            link(V.tensor_scalar(s, z, -1.0, None, ALU.mult))
            V.tensor_tensor(t, s, z, ALU.min).then_inc(sig(abs_sig), 1)
            dve.wait_ge(*at(exp_sig, 1))
            link(V.tensor_scalar(s, t, 2.0, None, ALU.add))
            link(V.reciprocal(s, s))
            link(V.tensor_tensor(s, s, t, ALU.mult))
            link(V.tensor_tensor(s2, s, s, ALU.mult))
            link(V.tensor_scalar(t, s2, 1.0 / 17, 1.0 / 15, ALU.mult, ALU.add))
            for k in (13, 11, 9, 7, 5, 3, 1):
                link(V.tensor_tensor(t, t, s2, ALU.mult))
                link(V.tensor_scalar(t, t, 1.0 / k, None, ALU.add))
            link(V.tensor_tensor(t, t, s, ALU.mult))
            link(V.scalar_tensor_tensor(out, t, 2.0, out, ALU.mult, ALU.add))

        def conv(dve, link, out, x, tap, bias, past, tiles, E, done):
            for t in tiles:
                last = E.tensor_scalar(out[:, t, :], x(t), tap(t, HIST), bias(t), ALU.mult, ALU.add)
            link(last)
            for j in range(HIST - 1, -1, -1):
                back = HIST - j
                for t in tiles:
                    E.scalar_tensor_tensor(out[:, t, back:TP], x(t)[:, 0:TP - back], tap(t, j), out[:, t, back:TP],
                                           ALU.mult, ALU.add)
                    last = E.scalar_tensor_tensor(out[:, t, TP:T], past(t, j), tap(t, j), out[:, t, TP:T], ALU.mult, ALU.add)
                if j:
                    link(last)
            last.then_inc(sig(done), 1)

        def norm_act_squares(eng, n, dep):
            eng.wait_ge(*at(*dep))
            SC.activation(inv[:], xT[:], ACT.Square).then_inc(sig(f"norm{n}_sq"), 1)

        def norm_act_root(eng, n):
            eng.wait_ge(*at(f"norm{n}_ss", 1))
            SC.activation(inv[:, 0, :], bank[4][:, 0:T], ACT.Sqrt, bias=eps_t[:], scale=1.0 / D)\
              .then_inc(sig(f"norm{n}_root"), 1)

        def norm_pe(pe, n):
            pe.wait_ge(*at(f"norm{n}_sq", 1))
            for j in range(KD):
                last = PE.matmul(bank[4][:, 0:T], ones[:], inv[:, j, :], start=j == 0, stop=j == KD - 1)
            last.then_inc(sig(f"norm{n}_ss"), 1)

        def norm_dve(dve, n, gain, link):
            dve.wait_ge(*at(f"norm{n}_root", 1))
            link(V.reciprocal(inv[:, 1, :], inv[:, 0, :]))
            for j in range(KD):
                last = V.scalar_tensor_tensor(hT[:, j, :], xT[:, j, :], col(gain, j), inv[:, 1, :], ALU.mult, ALU.mult)
            last.then_inc(sig(f"norm{n}_done"), 1)

        def dense_pe(pe, name, tiles, act_in, out_sig, free_sig, k_tiles=KD, first_free=None):
            for m in range(tiles):
                n, c = divmod(m, CHUNK_COLS // P)
                i = place[name, n]
                w = chunk(name, n)
                if c == 0:
                    wait_chunk(pe, i)
                if m >= 4:
                    pe.wait_ge(*at(free_sig, m - 3))
                for j in range(k_tiles):
                    last = PE.matmul(bank[m % 4][:, 0:T], w[:, j, c * P:(c + 1) * P], act_in[:, j, :],
                                     start=j == 0, stop=j == k_tiles - 1)
                last.then_inc(sig(out_sig), 1)
                if c == CHUNK_COLS // P - 1 or m == tiles - 1:
                    used(pe)

        def used(pe):
            PE.drain().then_inc(sig("chunk_used"), 1)

        @block.scalar
        def _(act_e):
            q = act_e
            q.dma_start(x_tok[:, 0:TT, :], A["x_prompt"][0].rearrange("(t p) d -> p t d", p=P)).then_inc(sig("x_loaded"), 16)
            q.dma_start(x_tok[0:TS, TT, :], A["x_sample"].rearrange("b t d -> (b t) d")).then_inc(sig("x_loaded"), 16)
            q.dma_start(w_ba[:], A["w_in_o"][0][:, QKV + D:QKV + D + 2 * HC].rearrange("(j p) n -> p j n", p=P)).then_inc(sig("small_w"), 16)
            q.dma_start(w_router[:], A["router_w"][0].rearrange("(j p) n -> p j n", p=P)).then_inc(sig("small_w"), 16)
            q.dma_start(alog_b[:], A["a_log"].broadcast_to([P, HC])).then_inc(sig("small_w"), 16)
            q.dma_start(dt_b[:], A["dt_bias"].broadcast_to([P, HC])).then_inc(sig("small_w"), 16)
            n_par = 0
            for r0, n, ap in rows.values():
                flat = ap
                while len(flat.shape) > 1:
                    d = len(flat.shape)
                    flat = flat.rearrange({2: "a b -> (a b)", 3: "a b c -> (a b c)"}[d])
                q.dma_start(par_rows[r0:r0 + n, :], flat.rearrange("(r p) -> r p", p=P)).then_inc(sig("par_loaded"), 16)
                n_par += 1
            for r, a, b in ((r_gq, "qk_gain_q", "qk_gain_q"), (r_gk, "qk_gain_k", "qk_gain_k"),
                            (r_lq, "lam_q1", "lam_q2"), (r_lk, "lam_k1", "lam_k2")):
                q.dma_start(par_rows[r:r + 1, 0:DH], A[a]).then_inc(sig("par_loaded"), 16)
                q.dma_start(par_rows[r:r + 1, DH:P], A[b]).then_inc(sig("par_loaded"), 16)
                n_par += 2
            q.dma_start(cd_rows[0:N_CD, :], A["conv_delta_w"][0].rearrange("j (t p) -> (j t) p", p=P)).then_inc(sig("par_loaded"), 16)
            q.dma_start(hist_rows, A["state_lru_conv"][0].rearrange("b j c -> (b j) c")).then_inc(sig("par_loaded"), 16)
            q.dma_start(h0_rows, A["state_lru_h"][0]).then_inc(sig("par_loaded"), 16)
            assert n_par == N_PAR - 3

            for j in range(KD):
                act_e.wait_ge(*at("xT_psum", j + 1))
                SC.activation(xT[:, j, :], bank[j % 4][:, 0:T], ACT.Copy).then_inc(sig("xT_done"), 1)
            norm_act_squares(act_e, 0, ("xT_done", KD))
            act_e.wait_ge(*at("lam_abs", 1))
            SC.activation(v_s[0], v_s[0], ACT.Exp).then_inc(sig("lam_absexp"), 1)
            norm_act_root(act_e, 0)
            for m in range(IN_E // P):
                act_e.wait_ge(*at("proj_psum", m + 1))
                SC.activation(proj[:, m, :], bank[m % 4][:, 0:T], ACT.Copy).then_inc(sig("proj_done"), 1)
            for g, (dst, bias) in enumerate(((gate_x, "lru_bx"), (gate_a, "lru_ba"))):
                for t in range(NL):
                    act_e.wait_ge(*at("lru_gate_psum", g * NL + t + 1))
                    SC.activation(dst[:, t, :], bank[g * NL + t][:, 0:T], ACT.Sigmoid, bias=col(bias, t))\
                      .then_inc(sig("lru_gates"), 1)
            act_e.wait_ge(*at("lru_y", 1))
            SC.activation(decay_a, gate_a, ACT.Exp, scale=-1.0).then_inc(sig("lru_a"), 1)
            SC.activation(tanh_y, gate_a, ACT.Tanh).then_inc(sig("lru_a"), 1)
            SC.activation(proj[:, GATE:GATE + NL, :], proj[:, GATE:GATE + NL, :], ACT.Gelu_apprx_tanh).then_inc(sig("gelu"), 1)
            act_e.wait_ge(*at("lru_m", 1))
            SC.activation(tanh_y, tanh_y, ACT.Sqrt).then_inc(sig("lru_root"), 1)
            act_e.wait_ge(*at("lru_done", 1))
            SC.activation(inv[:], proj[:, Q_:Q_ + 2 * HB, :], ACT.Square).then_inc(sig("qk_sq"), 1)
            for i in range(2 * HB):
                act_e.wait_ge(*at("qk_ss", i + 1))
                SC.activation(inv[:, i, :], bank[i % 4][:, 0:T], ACT.Sqrt, bias=eps_t[:], scale=1.0 / DH)\
                  .then_inc(sig("qk_root"), 1)
            act_e.wait_ge(*at("lam_psum", 1))
            SC.activation(lam_e, bank[4][:, 0:2], ACT.Exp).then_inc(sig("lam_exp"), 1)
            for i, (s0, n) in enumerate(TOK):
                act_e.wait_ge(*at("ktok_psum", i + 1))
                SC.activation(ktok[0:n, i, :], bank[i][0:n, :], ACT.Copy).then_inc(sig("ktok"), 1)
            for i, (s0, n) in enumerate(TOK):
                act_e.wait_ge(*at("vtok_psum", i + 1))
                SC.activation(vtok[0:n, i, :], bank[3 + i][0:n, :], ACT.Copy).then_inc(sig("vtok"), 1)
            act_e.wait_ge(*at("qs_psum", 1))
            SC.activation(qs_tok, bank[6][0:TS, :], ACT.Copy).then_inc(sig("qs_tok"), 1)
            act_e.wait_ge(*at("tail_psum", 1))
            SC.activation(tail_tok, bank[7][0:TAIL, 0:LW], ACT.Copy).then_inc(sig("tail_tok"), 1)
            outs = (("ktok", 3, ktok, "k_prompt", "k_sample"), ("vtok", 3, vtok, "v_prompt", "v_sample"))
            for s, k, src, a, b in outs:
                act_e.wait_ge(*at(s, k))
                q.dma_start(O[a][0, 0].rearrange("(t p) h e -> p t (h e)", p=P), src[:, 0:TT, :]).then_inc(sig("out_written"), 16)
                q.dma_start(O[b][0, :, 0].rearrange("b h e -> b (h e)"), src[0:TS, TT, :]).then_inc(sig("out_written"), 16)
            act_e.wait_ge(*at("tail_tok", 1))
            q.dma_start(O["lru_conv_prompt"][0, 0], tail_tok[0:HIST, :]).then_inc(sig("out_written"), 16)
            q.dma_start(O["lru_conv_sample"][0, :, HIST - 1, :], tail_tok[HIST:TAIL, :]).then_inc(sig("out_written"), 16)
            q.dma_start(O["lru_conv_sample"][0, :, 0:HIST - 1, :], A["state_lru_conv"][0, :, 1:HIST, :]).then_inc(sig("out_written"), 16)
            act_e.wait_ge(*at("hlast", 1))
            q.dma_start(O["lru_h_prompt"], hl_tok[0:1, :]).then_inc(sig("h_written"), 16)
            q.dma_start(O["lru_h_sample"][0], hl_tok[1:1 + TS, :]).then_inc(sig("h_written"), 16)
            act_e.wait_ge(*at("ss_psum", 1))
            for i in range(2):
                SC.activation(ss[:, i, 0:NP_ * P], bank[4][0:NB, i * NP_ * P:(i + 1) * NP_ * P], ACT.Copy, scale=DH ** -0.5)
            act_e.wait_ge(*at("self_psum", 1))
            SC.activation(ss[:, :, NP_ * P], bank[5][0:NB, 0:2], ACT.Copy, scale=DH ** -0.5).then_inc(sig("ss"), 1)
            act_e.wait_ge(*at("neg_max_s", 1))
            for i in range(2):
                SC.activation(ss[:, i, :], ss[:, i, :], ACT.Exp, bias=mx_s[0:NB, i:i + 1],
                              accum_out=ssum_s[0:NB, i:i + 1]).then_inc(sig("exps_s"), 1)
            for i in range(HH):
                for s, (c0, c1) in enumerate(((0, P), (P, 3 * P))):
                    act_e.wait_ge(*at("neg_max", 1))
                    SC.activation(sc_p[:, i, c0:c1], sc_p[:, i, c0:c1], ACT.Exp, bias=mx[:, s * HH + i:s * HH + i + 1],
                                  accum_out=ssum[:, s * HH + i:s * HH + i + 1]).then_inc(sig("exps"), 1)
            for h in range(HB):
                act_e.wait_ge(*at("pT_psum", h + 1))
                if h >= 2:
                    act_e.wait_ge(*at("pv_psum", h - 1))
                SC.activation(pT[h % 2], bank[h % 2][:, 0:3 * P], ACT.Copy).then_inc(sig("pT"), 1)
                act_e.wait_ge(*at("pv_psum", h + 1))
                SC.activation(mixT[:, NL + h, 0:TP], bank[2 + h % 2][:, 0:TP], ACT.Copy).then_inc(sig("o_prompt"), 1)
            act_e.wait_ge(*at("o_sample", 1))
            act_e.wait_ge(*at("o_prompt", HB))
            SC.activation(osq, mixT[:, NL:NL + HB, :], ACT.Square).then_inc(sig("o_sq"), 1)
            for h in range(HB):
                act_e.wait_ge(*at("o_ss", h + 1))
                SC.activation(osq[:, h, :], bank[4 + h][:, 0:T], ACT.Sqrt, bias=eps_t[:], scale=1.0 / E2)\
                  .then_inc(sig("o_root"), 1)
            norm_act_squares(act_e, 1, ("out_e_added", KD))
            norm_act_root(act_e, 1)
            for m in range(NF):
                act_e.wait_ge(*at("ffn_g", m + 1))
                if m >= 2:
                    act_e.wait_ge(*at("ffn_act", m - 1))
                SC.activation(sil[:, m % 2, :], bank[(2 * m) % 8][:, 0:T], ACT.Silu).then_inc(sig("ffn_sil"), 1)

            act_e.wait_ge(*at("ffn_act", NF))
            act_e.wait_ge(*at("out_written", 16 * 7))
            q.dma_start(dhist_rows, A["state_delta_conv"][0].rearrange("b j c -> (b j) c")).then_inc(sig("dhist_loaded"), 16)
            norm_act_squares(act_e, 2, ("ffn_added", KD))
            norm_act_root(act_e, 2)
            act_e.wait_ge(*at("ba_read", 1))
            SC.activation(beta, ba[:, :, 0:HC], ACT.Sigmoid).then_inc(sig("beta"), 1)
            act_e.wait_ge(*at("g_abs", 1))
            SC.activation(sp_t[0], sp_t[0], ACT.Exp).then_inc(sig("g_absexp"), 1)
            SC.activation(alog_b[:], alog_b[:], ACT.Exp).then_inc(sig("ealog"), 1)
            def silu_qkv(m):
                act_e.wait_ge(*at("dconv", m + 1))
                SC.activation(qkvT[:, m, :], qkvT[:, m, :], ACT.Silu).then_inc(sig("qkv"), 1)

            for m in range(NQ):
                act_e.wait_ge(*at("qkvz_psum", m + 1))
                if m >= 4:
                    act_e.wait_ge(*at("dconv", m - 3))
                SC.activation(pre[:, m % 4, :], bank[m % 4][:, 0:T], ACT.Copy).then_inc(sig("pre"), 1)
                SC.activation(tailT[:, m, :], bank[m % 4][:, T - TAIL:T], ACT.Copy).then_inc(sig("qkvz_read"), 1)
                if m >= 2:
                    silu_qkv(m - 2)
            silu_qkv(NQ - 2)
            silu_qkv(NQ - 1)
            for m in range(NQ, NQ + HC):
                act_e.wait_ge(*at("qkvz_psum", m + 1))
                SC.activation(zT[:, m - NQ, :], bank[m % 4][:, 0:T], ACT.Silu).then_inc(sig("qkvz_read"), 1)
            for n in range(QKV // CHUNK_COLS):
                act_e.wait_ge(*at("dtail_psum", n + 1))
                SC.activation(tail_rows[:, n * CHUNK_COLS:(n + 1) * CHUNK_COLS], bank[5 + n % 3][0:TAIL, :], ACT.Copy)\
                  .then_inc(sig("dtail"), 1)
            act_e.wait_ge(*at("dtail", QKV // CHUNK_COLS))
            q.dma_start(O["delta_conv_prompt"][0, 0], tail_rows[0:HIST, :]).then_inc(sig("tail_written"), 16)
            q.dma_start(O["delta_conv_sample"][0, :, HIST - 1, :], tail_rows[HIST:TAIL, :]).then_inc(sig("tail_written"), 16)
            q.dma_start(O["delta_conv_sample"][0, :, 0:HIST - 1, :], A["state_delta_conv"][0, :, 1:HIST, :]).then_inc(sig("out_written"), 16)
            for r in range(2):
                if r:
                    act_e.wait_ge(*at("l2_used", 1))
                act_e.wait_ge(*at("qkv", NQ))
                SC.activation(inv, qkvT[:, r * HC:(r + 1) * HC, :], ACT.Square).then_inc(sig("l2_sq"), 1)
            act_e.wait_ge(*at("l2_ss", 1))
            SC.activation(inv[0:2 * HC, 0, :], bank[4][0:2 * HC, 0:T], ACT.Sqrt, bias=eps_t[0:2 * HC, :]).then_inc(sig("l2_root"), 1)
            act_e.wait_ge(*at("Gt", 1))
            SC.activation(eG, Gt, ACT.Exp).then_inc(sig("eG"), 1)
            for n in range(NGROUPS):
                c, h0_ = divmod(n * NG, HC)
                act_e.wait_ge(*at("d_in", n + 1))
                SC.activation(Gb, bank[0][:, :].rearrange("p (h t) -> p h t", h=NG), ACT.Copy).then_inc(sig("d_gb"), 1)
                act_e.wait_ge(*at("d_diff", n + 1))
                SC.activation(EA, EA, ACT.Exp, scale=-1.0)
                SC.activation(QK, QK, ACT.Exp)
                if c:
                    act_e.wait_ge(*at("d_gb", n + 1))
                    SC.activation(ge[:, 0:NG], Gb[:, :, P - 1], ACT.Exp)
                    SC.activation(QD, Gb, ACT.Exp)
                SC.activation(kd_s[:, 0:NG], kd_s[:, 0:NG], ACT.Exp).then_inc(sig("d_exp"), 1)
                for l in range(1, LEVELS):
                    k = n * (LEVELS - 1) + l
                    act_e.wait_ge(*at("d_Y", k))
                    SC.activation(Yb, bank[6][:, :].rearrange("p (h t) -> p h t", h=NG), ACT.Copy).then_inc(sig("d_Yc"), 1)
                if c:
                    act_e.wait_ge(*at("d_w", n - NGROUPS // TT + 1))
                    SC.activation(NW, bank[1][:, :].rearrange("p (h t) -> p h t", h=NG), ACT.Copy, scale=-1.0).then_inc(sig("d_nw"), 1)
                act_e.wait_ge(*at("d_v", n + 1))
                SC.activation(VN, bank[2][:, :].rearrange("p (h t) -> p h t", h=NG), ACT.Copy).then_inc(sig("d_vn"), 1)
                act_e.wait_ge(*at("d_o", n + 1))
                SC.activation(oT[:, h0_:h0_ + NG, c * P:(c + 1) * P], bank[3][:, :].rearrange("p (h t) -> p h t", h=NG), ACT.Copy)\
                  .then_inc(sig("d_done"), 1)
            act_e.wait_ge(*at("d_done", 2 * NGROUPS))
            q.dma_start(O["delta_s_prompt"][0, 0].rearrange("h d e -> d h e"), S_pr).then_inc(sig("sp_written"), 16)
            act_e.wait_ge(*at("s_gb", 1))
            SC.activation(egb[:, 0], bank[0][:, 0:HC * TS].rearrange("p (h b) -> p h b", h=HC), ACT.Exp)
            SC.activation(egb[:, 1], bank[0][:, HC * TS:2 * HC * TS].rearrange("p (h b) -> p h b", h=HC), ACT.Copy).then_inc(sig("s_egb"), 1)
            act_e.wait_ge(*at("s_qk", 1))
            SC.activation(qks, bank[1][:, 0:HC * TS].rearrange("p (h b) -> p h b", h=HC), ACT.Copy).then_inc(sig("s_qks"), 1)
            for h in range(HC):
                act_e.wait_ge(*at("s_state", h + 1))
                q.dma_start(O["delta_s_sample"][0, :, h].rearrange("b d e -> d b e"), s_ring[h % 4]).then_inc(sig(f"state{h % 4}_written"), 16)
            act_e.wait_ge(*at("s_o", HC))
            SC.activation(inv, oT[:], ACT.Square).then_inc(sig("on_sq"), 1)
            act_e.wait_ge(*at("on_ss", 1))
            SC.activation(inv[0:HC, 0, :], bank[4][0:HC, 0:T], ACT.Sqrt, bias=eps_t[0:HC, :], scale=1.0 / DV).then_inc(sig("on_root"), 1)
            for k in range(4):
                act_e.wait_ge(*at(f"state{k}_written", 32))
            act_e.wait_ge(*at("sp_written", 16))
            act_e.wait_ge(*at("tail_written", 32))
            norm_act_squares(act_e, 3, ("out_o_added", KD))
            norm_act_root(act_e, 3)
            act_e.wait_ge(*at("top_diff", 1))
            SC.activation(gates[:, 0:TT, 1:2], gates[:, 0:TT, 1:2], ACT.Exp)
            SC.activation(gates[0:TS, TT, 1:2], gates[0:TS, TT, 1:2], ACT.Exp).then_inc(sig("gate_exp"), 1)
            for s, dst in (("xtok", acc), ("htok", h_tok)):
                for i, (t0, n) in enumerate(TOK):
                    for k in range(YC):
                        act_e.wait_ge(*at(s + "_psum", i * YC + k + 1))
                        SC.activation(dst[0:n, i, k * CHUNK_COLS:(k + 1) * CHUNK_COLS],
                                      bank[(i * YC + k) % 4][0:n, :], ACT.Copy).then_inc(sig(s), 1)
            SC.activation(spare[:, 0:1], eps_t[:], ACT.Copy).then_inc(sig("tr_out"), 1)
            SC.activation(spare[:, 1:2], eps_t[:], ACT.Copy).then_inc(sig("y0_out"), 1)

            def dispatch_out(it):
                for r in range(2):
                    act_e.wait_ge(*at("moe_disp", it * 2 + r + 1))
                    n = KD // 2
                    SC.activation(hTe[:, r * n:(r + 1) * n, :], bank[(7, 3)[r]][:, :].rearrange("p (j t) -> p j t", j=n), ACT.Copy)\
                      .then_inc(sig("hte"), 1)

            def tr_out(it, c):
                act_e.wait_ge(*at("moe_tr", it * NSTEP + c + 1))
                SC.activation(m_actT[:, c % 2], bank[4][:, :].rearrange("p (k t) -> p k t", k=KF), ACT.Copy).then_inc(sig("tr_out"), 1)

            def act_expert(it, more):
                for c in range(NSTEP):
                    act_e.wait_ge(*at("moe_g", it * NSTEP + c + 1))
                    SC.activation(m_sil[:, c % 2, :], bank[c % 2 * 2][:, :], ACT.Silu).then_inc(sig("sil"), 1)
                    if c == 0:
                        act_e.wait_ge(*at("moe_w", it + 1))
                        SC.activation(WT, bank[4][:, 0:T], ACT.Copy).then_inc(sig("wt_out"), 1)
                    else:
                        tr_out(it, c - 1)
                if more:
                    dispatch_out(it + 1)
                tr_out(it, NSTEP - 1)
                act_e.wait_ge(*at("moe_d", (it + 1) * NSTEP))
                SC.activation(y_e[:, 0:CHUNK_COLS], bank[5][:, :], ACT.Copy).then_inc(sig("y0_out"), 1)

            dispatch_out(0)
            with act_e.Fori(0, NE - 1) as e:
                act_expert(e, True)
            act_expert(NE - 1, False)
            with act_e.If(act_e.value_load(count_i[0:1, 0:1], min_val=0, max_val=T) > CAP):
                with act_e.Fori(1, PASSES) as p:
                    with act_e.Fori(0, NE) as e:
                        dispatch_out(p * NE + e)
                        act_expert(p * NE + e, False)
            act_e.wait_ge(*at("out_written", OUTS * 16))
            act_e.wait_ge(*at("h_written", 32))

        @block.vector
        def _(dve):
            chain = [0]

            def link(ins):
                chain[0] += 1
                ins.then_inc(sig("dve_chain"), 1)
                dve.wait_ge(*at("dve_chain", chain[0]))

            dve.wait_ge(*at("constants", 2))
            V.memset(pick[:, 2 * HC - 1:2 * HC], 1.0)
            dve.wait_ge(*at("par_psum", 1))
            V.tensor_copy(par[:, 0:N_ROWS], bank[4][:, 0:N_ROWS])
            V.tensor_copy(cd[:, 0:N_CD], bank[4][:, P:P + N_CD])
            V.tensor_copy(hist, bank[4][:, 2 * P:2 * P + NL * TS * HIST].rearrange("p (a b c) -> p a b c", a=NL, b=TS))
            link(V.tensor_copy(h0, bank[4][:, 3 * P:3 * P + NL * TS].rearrange("p (a b) -> p a b", a=NL)))
            V.tensor_tensor(lamv, par[:, r_lq:r_lq + 1], par[:, r_lk:r_lk + 1], ALU.mult).then_inc(sig("par_done"), 1)
            softplus(dve, link, sp8, par[:, rows["lru_lambda"][0]:rows["lru_lambda"][0] + NL], v_s, "lam_abs", "lam_absexp", -1.0)
            link(V.tensor_scalar(sp8, sp8, RG_C, None, ALU.mult))
            V.tensor_scalar(subg, col("subln_g"), 1.0 - LAM_INIT, None, ALU.mult)
            norm_dve(dve, 0, "ln_mix_e", link)

            dve.wait_ge(*at("proj_done", XR + NL))
            conv(dve, link, xc, lambda t: proj[:, XR + t, :], lambda t, j: col("conv_lru_w", j * NL + t),
                 lambda t: col("conv_lru_b", t), lambda t, j: hist[:, t, :, j], range(NL), V, "xc_done")
            dve.wait_ge(*at("lru_gates", 2 * NL))
            for t in range(NL):
                last = V.tensor_scalar(gate_a[:, t, :], gate_a[:, t, :], sp8[:, t:t + 1], None, ALU.mult)
            last.then_inc(sig("lru_y"), 1)
            link(V.tensor_tensor(gate_x, gate_x, xc, ALU.mult))
            dve.wait_ge(*at("lru_a", 2))
            link(V.tensor_scalar(tmp_l, tanh_y, 1.0, None, ALU.add))
            link(V.reciprocal(tmp_l, tmp_l))
            link(V.tensor_scalar(tmp_l, tmp_l, 2.0, None, ALU.mult))
            V.tensor_tensor(tanh_y, tanh_y, tmp_l, ALU.mult).then_inc(sig("lru_m"), 1)
            dve.wait_ge(*at("lru_root", 1))
            link(V.tensor_tensor(gate_x, gate_x, tanh_y, ALU.mult))
            link(V.tensor_tensor(tmp_l[:, :, 0:TS], decay_a[:, :, TP:T], h0, ALU.mult))
            for t in range(NL):
                V.tensor_tensor_scan(xc[:, t, 0:TP], decay_a[:, t, 0:TP], gate_x[:, t, 0:TP], 0.0, ALU.mult, ALU.add)
            link(V.tensor_tensor(xc[:, :, TP:T], gate_x[:, :, TP:T], tmp_l[:, :, 0:TS], ALU.add))
            dve.wait_ge(*at("gelu", 1))
            V.tensor_copy(hl, xc[:, :, TP - 1:T])
            V.tensor_tensor(mixT[:, 0:NL, :], proj[:, GATE:GATE + NL, :], xc, ALU.mult).then_inc(sig("lru_done"), 1)
            dve.wait_ge(*at("qk_root", 2 * HB))
            link(V.reciprocal(inv, inv))
            for i in range(2 * HB):
                g = r_gq if i < HB else r_gk
                last = V.scalar_tensor_tensor(proj[:, Q_ + i, :], proj[:, Q_ + i, :], par[:, g:g + 1], inv[:, i, :],
                                              ALU.mult, ALU.mult)
            last.then_inc(sig("qk_done"), 1)
            dve.wait_ge(*at("lam_exp", 1))
            link(V.tensor_tensor(nlam, lam_e[:, 1:2], lam_e[:, 0:1], ALU.subtract))
            link(V.tensor_scalar(nlam, nlam, -LAM_INIT, None, ALU.add))
            dve.wait_ge(*at("hlast_psum", 1))
            V.tensor_copy(hl_tok, bank[7][0:TS + 1, 0:LW]).then_inc(sig("hlast"), 1)

            for b in range(TS):
                dve.wait_ge(*at("qb_psum", b + 1))
                dve.wait_ge(*at(f"kv{b % 4}_loaded", 32 * (b // 4 + 1)))
                if b:
                    dve.wait_ge(*at("k_pages_used", b))
                for g in range(NP_):
                    last = V.tensor_tensor(kv_mul[:, g, :], pages_kv[:, b % 4, g, :], bank[4 + b % 2][:, :], ALU.mult)
                chain[0] += 1
                last.then_inc(sig("dve_chain"), 1)
                dve.wait_ge(*at("dve_chain", chain[0]))
                for g in range(NP_):
                    last = V.reduce_sum(sc_s[:, g, :, :, b].rearrange("p i h -> p h i"),
                                        kv_mul[:, g, :].rearrange("p (h i d) -> p h i d", i=2, d=DH), X)
                last.then_inc(sig("k_pages_used"), 1)
            dve.wait_ge(*at("qk_done", 1))
            V.tensor_tensor(qk_s, proj[:, Q_:Q_ + HB, TP:T], proj[:, K_:K_ + HB, TP:T], ALU.mult).then_inc(sig("qk_self"), 1)
            dve.wait_ge(*at("ss", 1))
            link(V.reduce_max(mx_s[0:NB, :], ss, X))
            V.tensor_scalar(mx_s[0:NB, :], mx_s[0:NB, :], -1.0, None, ALU.mult).then_inc(sig("neg_max_s"), 1)
            dve.wait_ge(*at("exps_s", 2))
            link(V.reciprocal(rsum_s[0:NB, :], ssum_s[0:NB, :]))
            link(V.tensor_tensor(rsum_s[0:NB, 1:2], rsum_s[0:NB, 1:2], nlam[0:NB, :], ALU.mult))
            link(V.tensor_scalar(ss[:, 0, :], ss[:, 0, :], rsum_s[0:NB, 0:1], None, ALU.mult))
            V.scalar_tensor_tensor(ss[:, 0, :], ss[:, 1, :], rsum_s[0:NB, 1:2], ss[:, 0, :], ALU.mult, ALU.add).then_inc(sig("p_s"), 1)
            dve.wait_ge(*at("pT_s_psum", 1))
            V.tensor_copy(pT_s, bank[6][:, 0:NP_ * NB].rearrange("p (g n) -> p g n", g=NP_))
            V.tensor_copy(pself, bank[6][:, NP_ * NB:(NP_ + 1) * NB]).then_inc(sig("pT_s"), 1)
            dve.wait_ge(*at("pT_s", 1))
            link(V.tensor_tensor(pself.rearrange("p (h b) -> p h b", h=HB), pself.rearrange("p (h b) -> p h b", h=HB),
                                 proj[:, V_:V_ + HB, TP:T], ALU.mult))
            dve.wait_ge(*at("v_pages_used", TS))
            V.tensor_tensor(mixT[:, NL:NL + HB, TP:T], pself.rearrange("p (h b) -> p h b", h=HB),
                            bank[7][:, 0:NB].rearrange("p (h b) -> p h b", h=HB), ALU.add).then_inc(sig("o_sample"), 1)

            for i in range(HH):
                dve.wait_ge(*at("scores_psum", i + 1))
                if i == 0:
                    dve.wait_ge(*at("o_sample", 1))
                    dve.wait_ge(*at("h_written", 32))
                last = V.scalar_tensor_tensor(sc_p[:, i, :], bank[i % 4][:, 0:3 * P], DH ** -0.5, causal[:], ALU.mult, ALU.add)
                last.then_inc(sig("scores"), 1)
            dve.wait_ge(*at("scores", HH))
            V.reduce_max(mx[:, 0:HH], sc_p[:, :, 0:P], X)
            link(V.reduce_max(mx[:, HH:2 * HH], sc_p[:, :, P:3 * P], X))
            V.tensor_scalar(mx, mx, -1.0, None, ALU.mult).then_inc(sig("neg_max"), 1)
            dve.wait_ge(*at("exps", 2 * HH))
            link(V.reciprocal(rsum, ssum))
            r4 = rsum.rearrange("p (s h i) -> p s h i", s=2, i=2)
            link(V.tensor_scalar(r4[:, :, :, 1], r4[:, :, :, 1], nlam, None, ALU.mult))
            seg = ((0, P), (P, 3 * P))
            for h in range(HB):
                for s, (c0, c1) in enumerate(seg):
                    r = s * HH + 2 * h
                    last = V.tensor_scalar(sc_p[:, 2 * h, c0:c1], sc_p[:, 2 * h, c0:c1], rsum[:, r:r + 1], None, ALU.mult)
            link(last)
            for h in range(HB):
                for s, (c0, c1) in enumerate(seg):
                    r = s * HH + 2 * h + 1
                    last = V.scalar_tensor_tensor(sc_p[:, 2 * h, c0:c1], sc_p[:, 2 * h + 1, c0:c1], rsum[:, r:r + 1],
                                                  sc_p[:, 2 * h, c0:c1], ALU.mult, ALU.add)
                last.then_inc(sig("probs"), 1)
            dve.wait_ge(*at("o_root", HB))
            link(V.reciprocal(osq, osq))
            for h in range(HB):
                last = V.scalar_tensor_tensor(mixT[:, NL + h, :], mixT[:, NL + h, :], subg, osq[:, h, :], ALU.mult, ALU.mult)
            last.then_inc(sig("mix_done"), 1)
            for m in range(KD):
                dve.wait_ge(*at("out_e_psum", m + 1))
                V.tensor_tensor(xT[:, m, :], xT[:, m, :], bank[m % 4][:, 0:T], ALU.add).then_inc(sig("out_e_added"), 1)
            norm_dve(dve, 1, "ln_ffn_e", link)
            for m in range(NF):
                dve.wait_ge(*at("ffn_u", m + 1))
                dve.wait_ge(*at("ffn_sil", m + 1))
                V.tensor_tensor(act[:, m, :], sil[:, m % 2, :], bank[(2 * m + 1) % 8][:, 0:T], ALU.mult).then_inc(sig("ffn_act"), 1)
            for m in range(KD):
                dve.wait_ge(*at("ffn_d_psum", m + 1))
                V.tensor_tensor(xT[:, m, :], xT[:, m, :], bank[m % 4][:, 0:T], ALU.add).then_inc(sig("ffn_added"), 1)

            def heads(b, n=NG):
                return bank[b][:, 0:n * P].rearrange("p (h t) -> p h t", h=n)

            dve.wait_ge(*at("dhist_psum", 1))
            half = NQ // 2
            for k in range(2):
                last = V.tensor_copy(dhist[:, k * half:(k + 1) * half],
                                     bank[5 + k][:, 0:half * TS * HIST].rearrange("p (a b c) -> p a b c", a=half, b=TS))
            link(last)
            norm_dve(dve, 2, "ln_mix_o", link)
            dve.wait_ge(*at("ba_psum", 1))
            V.tensor_copy(ba[:, 0:TT, :], bank[7][:, 0:TT * 2 * HC].rearrange("p (t c) -> p t c", t=TT))
            V.tensor_copy(ba[0:TS, TT, :], bank[7][0:TS, TT * 2 * HC:NTT * 2 * HC]).then_inc(sig("ba_read"), 1)
            dve.wait_ge(*at("ba_read", 1))
            dve.wait_ge(*at("small_w", 64))
            dve.wait_ge(*at("beta", 1))
            az = ba[:, :, HC:2 * HC]
            link(V.tensor_tensor(az, az, dt_b[:].unsqueeze(1).broadcast_to([P, NTT, HC]), ALU.add))
            softplus(dve, link, g_t, az, sp_t, "g_abs", "g_absexp", 1.0)
            dve.wait_ge(*at("ealog", 1))
            link(V.scalar_tensor_tensor(g_t, g_t, -1.0, alog_b[:].unsqueeze(1).broadcast_to([P, NTT, HC]), ALU.mult, ALU.mult))
            V.tensor_tensor(gd[0:TS, 0], ident[0:TS, 0:TS].unsqueeze(1).broadcast_to([TS, HC, TS]),
                            g_t[0:TS, TT, :].unsqueeze(2).broadcast_to([TS, HC, TS]), ALU.mult)
            V.tensor_tensor(gd[0:TS, 1], ident[0:TS, 0:TS].unsqueeze(1).broadcast_to([TS, HC, TS]),
                            beta[0:TS, TT, :].unsqueeze(2).broadcast_to([TS, HC, TS]), ALU.mult).then_inc(sig("g"), 1)
            for m in range(NQ):
                dve.wait_ge(*at("pre", m + 1))
                x, o = pre[:, m % 4, :], qkvT[:, m, :]
                tap = [cd[:, j * NQ + m:j * NQ + m + 1] for j in range(CW)]
                link(V.tensor_scalar(o, x, tap[HIST], None, ALU.mult))
                for j in range(HIST - 1, -1, -1):
                    back = HIST - j
                    V.scalar_tensor_tensor(o[:, back:TP], x[:, 0:TP - back], tap[j], o[:, back:TP], ALU.mult, ALU.add)
                    last = V.scalar_tensor_tensor(o[:, TP:T], dhist[:, m, :, j], tap[j], o[:, TP:T], ALU.mult, ALU.add)
                    if j:
                        link(last)
                last.then_inc(sig("dconv"), 1)
            dve.wait_ge(*at("Gt_psum", 1))
            V.tensor_copy(Gt, bank[7][:, 0:TT * HC].rearrange("p (c h) -> p c h", c=TT)).then_inc(sig("Gt"), 1)
            dve.wait_ge(*at("eG", 1))
            link(V.tensor_tensor(bkb, beta[:, 0:TT, :], eG, ALU.mult))
            dve.wait_ge(*at("l2_root", 1))
            V.reciprocal(inv[0:2 * HC, 0, :], inv[0:2 * HC, 0, :]).then_inc(sig("l2_inv"), 1)
            for i in range(2 * HC):
                dve.wait_ge(*at("l2_b", i + 1))
                V.scalar_tensor_tensor(qkvT[:, i, :], qkvT[:, i, :], DK ** -0.5 if i < HC else 1.0, bank[i % 4][:, 0:T],
                                       ALU.mult, ALU.mult).then_inc(sig("l2_applied"), 1)
            for n in range(NGROUPS):
                c, h0_ = divmod(n * NG, HC)
                hs = range(NG)

                def per_head(v, h):
                    return v[:, c, h0_ + h:h0_ + h + 1]
                dve.wait_ge(*at("d_gb", n + 1))
                if n == 0:
                    dve.wait_ge(*at("levels", 1))
                for h in hs:
                    V.tensor_scalar(EA[:, h, :], Gb[:, h, :], per_head(Gt, h), 0.0, ALU.subtract, ALU.max)
                    V.tensor_scalar(QK[:, h, :], Gb[:, h, :], per_head(Gt, h), 0.0, ALU.subtract, ALU.min)
                V.tensor_tensor(kd_s[:, 0:NG], Gb[:, :, P - 1], Gt[:, c, h0_:h0_ + NG], ALU.subtract).then_inc(sig("d_diff"), 1)
                dve.wait_ge(*at("d_exp", n + 1))
                V.tensor_tensor(EA, EA, heads(1), ALU.mult)
                V.tensor_tensor(QK, QK, heads(2), ALU.mult)
                if c:
                    V.tensor_tensor(QD, QD, qT[:, h0_:h0_ + NG, c * P:(c + 1) * P], ALU.mult)
                for h in hs:
                    V.tensor_scalar(KDc[:, h, :], bank[3][:, h * P:(h + 1) * P], kd_s[:, h:h + 1], None, ALU.mult)
                    V.tensor_scalar(KB[:, h, :], bank[3][:, h * P:(h + 1) * P], per_head(bkb, h), None, ALU.mult)
                    last = V.tensor_scalar(VB[:, h, :], bank[4][:, h * P:(h + 1) * P], per_head(beta, h), None, ALU.mult)
                link(last)
                V.tensor_tensor(QK, QK, le_mask[:].unsqueeze(1).broadcast_to([P, NG, P]), ALU.mult)
                for h in hs:
                    last = V.scalar_tensor_tensor(EA[:, h, :], EA[:, h, :], per_head(beta, h), gt_mask[:], ALU.mult, ALU.mult)
                link(last)
                link(V.tensor_tensor(Am, EA, lvl[:, 0, :].unsqueeze(1).broadcast_to([P, NG, P]), ALU.mult))
                V.tensor_tensor(Tm, ident[:].unsqueeze(1).broadcast_to([P, NG, P]), Am, ALU.subtract).then_inc(sig("d_T0"), 1)
                dve.wait_ge(*at("d_T0t", n + 1))
                V.tensor_copy(Tt, heads(5)).then_inc(sig("d_T"), 1)
                for l in range(1, LEVELS):
                    k = n * (LEVELS - 1) + l
                    if l > 1:
                        dve.wait_ge(*at("d_Y", k - 1))
                    else:
                        dve.wait_ge(*at("d_T0", n + 1))
                    V.tensor_tensor(Am, EA, lvl[:, l, :].unsqueeze(1).broadcast_to([P, NG, P]), ALU.mult).then_inc(sig("d_Am"), 1)
                    if l > 1:
                        dve.wait_ge(*at("d_D", k - 1))
                        V.tensor_tensor(Tm, Tm, heads(0), ALU.subtract)
                        V.tensor_tensor(Tt, Tt, heads(7), ALU.subtract).then_inc(sig("d_T"), 1)
                dve.wait_ge(*at("d_D", (n + 1) * (LEVELS - 1)))
                V.tensor_tensor(Tt, Tt, heads(7), ALU.subtract).then_inc(sig("d_T"), 1)
                dve.wait_ge(*at("d_S", n + 1))
                for h in hs:
                    if c:
                        last = V.scalar_tensor_tensor(S_pr[:, h0_ + h, :], S_pr[:, h0_ + h, :], ge[:, h:h + 1],
                                                      bank[4][:, h * P:(h + 1) * P], ALU.mult, ALU.add)
                    else:
                        last = V.tensor_copy(S_pr[:, h0_ + h, :], bank[4][:, h * P:(h + 1) * P])
                last.then_inc(sig("d_done"), 1)
            dve.wait_ge(*at("d_done", 2 * NGROUPS))
            prod = inv[:, 0, 0:HC * TS].rearrange("p (h b) -> p h b", h=HC)
            V.tensor_tensor(prod, qT[:, :, TP:T], kT[:, :, TP:T], ALU.mult).then_inc(sig("s_prod"), 1)
            dve.wait_ge(*at("s_egb", 1))
            dve.wait_ge(*at("s_qks", 1))
            for h in range(HC):
                eg, be = egb[:, 0, h, :], egb[:, 1, h, :]
                dve.wait_ge(*at("s_ks", h + 1))
                qS = bank[2 + h % 2][:, 0:2 * TS].rearrange("p (b k) -> p b k", k=2)[:, :, 0]
                kS = bank[2 + h % 2][:, 0:2 * TS].rearrange("p (b k) -> p b k", k=2)[:, :, 1]
                link(V.tensor_tensor(vn_s, kS, eg, ALU.mult))
                link(V.tensor_tensor(vn_s, vT[:, h, TP:T], vn_s, ALU.subtract))
                link(V.tensor_tensor(vn_s, vn_s, be, ALU.mult))
                V.tensor_tensor(vn_t, qS, eg, ALU.mult).then_inc(sig("s_v"), 1)
                link(V.tensor_tensor(prod[:, 0, :], vn_s, qks[:, h, :], ALU.mult))
                V.tensor_tensor(oT[:, h, TP:T], prod[:, 0, :], vn_t, ALU.add).then_inc(sig("s_o"), 1)
                dve.wait_ge(*at("s_vt", h + 1))
                if h:
                    dve.wait_ge(*at("s_outer", h))
                link(V.tensor_copy(k_row, bank[4][0:TS, P:2 * P]))
                V.tensor_tensor(v_diag[0:TS], ident[0:TS, 0:TS].unsqueeze(2).broadcast_to([TS, TS, P]),
                                bank[4][0:TS, 0:P].unsqueeze(1).broadcast_to([TS, TS, P]), ALU.mult).then_inc(sig("s_vd"), 1)
                for b in range(TS):
                    last = V.tensor_scalar(s_ring[h % 4][:, b, :], s_ring[h % 4][:, b, :], eg[:, b:b + 1], None, ALU.mult)
                link(last)
                dve.wait_ge(*at("s_outer", h + 1))
                for k in range(2):
                    n = TS // 2
                    last = V.tensor_tensor(s_ring[h % 4][:, k * n:(k + 1) * n, :], s_ring[h % 4][:, k * n:(k + 1) * n, :], heads(5 + k), ALU.add)
                last.then_inc(sig("s_state"), 1)
            dve.wait_ge(*at("on_root", 1))
            V.reciprocal(inv[0:HC, 0, :], inv[0:HC, 0, :]).then_inc(sig("on_inv"), 1)
            for h in range(HC):
                dve.wait_ge(*at("on_b", h + 1))
                V.scalar_tensor_tensor(oT[:, h, :], oT[:, h, :], col("onorm_g"), bank[h % 4][:, 0:T], ALU.mult, ALU.mult)\
                 .then_inc(sig("on_applied"), 1)
            dve.wait_ge(*at("on_applied", HC))
            V.tensor_tensor(oT[:], oT[:], zT, ALU.mult).then_inc(sig("on_done"), 1)
            for m in range(KD):
                dve.wait_ge(*at("out_o_psum", m + 1))
                V.tensor_tensor(xT[:, m, :], xT[:, m, :], bank[m % 4][:, 0:T], ALU.add).then_inc(sig("out_o_added"), 1)
            norm_dve(dve, 3, "ln_ffn_o", link)
            dve.wait_ge(*at("iota_psum", 1))
            V.tensor_copy(iota, bank[7][:, 0:P]).then_inc(sig("iota"), 1)
            dve.wait_ge(*at("iota", 1))
            dve.wait_ge(*at("logits_psum", 1))
            for i, (t0, n) in enumerate(TOK):
                last = V.tensor_copy(logit[0:n, i, :], bank[5][0:n, i * NE:(i + 1) * NE])
            link(last)
            for i, (t0, n) in enumerate(TOK):
                last = V.max(top[0:n, i, :], logit[0:n, i, :])
            link(last)
            for i, (t0, n) in enumerate(TOK):
                V.max_index(top_i[0:n, i, :], top[0:n, i, :], logit[0:n, i, :])
                last = V.tensor_tensor(gates[0:n, i, 1:2], top[0:n, i, 1:2], top[0:n, i, 0:1], ALU.subtract)
            last.then_inc(sig("top_diff"), 1)
            dve.wait_ge(*at("gate_exp", 1))
            for i, (t0, n) in enumerate(TOK):
                V.tensor_copy(idx_f[0:n, i, :], top_i[0:n, i, 0:2])
                last = V.tensor_scalar(gates[0:n, i, 0:1], gates[0:n, i, 1:2], 1.0, None, ALU.add)
            link(last)
            for i, (t0, n) in enumerate(TOK):
                last = V.reciprocal(gates[0:n, i, 0:1], gates[0:n, i, 0:1])
            link(last)
            for i, (t0, n) in enumerate(TOK):
                last = V.tensor_tensor(gates[0:n, i, 1:2], gates[0:n, i, 1:2], gates[0:n, i, 0:1], ALU.mult)
            link(last)
            for i, (t0, n) in enumerate(TOK):
                io = iota[0:n, 0:NE]
                V.tensor_scalar(mask[0:n, i, :], io, idx_f[0:n, i, 0:1], None, ALU.is_equal)
                V.tensor_scalar(comb[0:n, i, :], io, idx_f[0:n, i, 0:1], gates[0:n, i, 0:1], ALU.is_equal, ALU.mult)
                last = V.tensor_scalar(comb2[0:n, i, :], io, idx_f[0:n, i, 1:2], gates[0:n, i, 1:2], ALU.is_equal, ALU.mult)
            link(last)
            for i, (t0, n) in enumerate(TOK):
                V.tensor_tensor(comb[0:n, i, :], comb[0:n, i, :], comb2[0:n, i, :], ALU.add)
                last = V.scalar_tensor_tensor(mask[0:n, i, :], iota[0:n, 0:NE], idx_f[0:n, i, 1:2], mask[0:n, i, :], ALU.is_equal, ALU.add)
            last.then_inc(sig("masks"), 1)
            dve.wait_ge(*at("ranks_psum", 1))
            V.reduce_max(count, bank[6][:, NTT * NE:(NTT + 1) * NE], X)
            for i, (t0, n) in enumerate(TOK):
                last = V.scalar_tensor_tensor(rank[0:n, i, :], mask[0:n, i, :], -FAR, bank[6][0:n, i * NE:(i + 1) * NE], ALU.mult, ALU.add)
            link(last)
            for i, (t0, n) in enumerate(TOK):
                last = V.tensor_scalar(rank[0:n, i, :], rank[0:n, i, :], FAR, None, ALU.add)
            last.then_inc(sig("ranks"), 1)
            V.tensor_copy(count_i, count).then_inc(sig("flag"), 1)
            dve.wait_ge(*at("flag", 1))
            for i, (name, k) in enumerate((("act_done", 2), ("y1_out", 1), ("added", NTT * YC))):
                V.memset(spare[:, 2 + i:3 + i], 0.0).then_inc(sig(name), k)

            def column(v, i, n, e):
                return v[0:n, i, e:e + 1] if isinstance(e, int) else v[0:n, i, bass.ds(e, 1)]

            def select(e):
                for i, (t0, n) in enumerate(TOK):
                    V.tensor_scalar(sel[0:n, i, :], iota[0:n, 0:CAP], column(rank, i, n, e), None, ALU.is_equal)
                    last = V.tensor_scalar(selw[0:n, i, :], iota[0:n, 0:CAP], column(rank, i, n, e), column(comb, i, n, e),
                                           ALU.is_equal, ALU.mult)
                last.then_inc(sig("sel"), 1)

            def dve_expert(it, more, e_next):
                for c in range(NSTEP):
                    dve.wait_ge(*at("sil", it * NSTEP + c + 1))
                    dve.wait_ge(*at("moe_u", it * NSTEP + c + 1))
                    V.tensor_tensor(m_act[:, c % 2, :], m_sil[:, c % 2, :], bank[c % 2 * 2 + 1][:, :], ALU.mult).then_inc(sig("act_done"), 1)
                    if c == 2 and more:
                        dve.wait_ge(*at("moe_w", it + 1))
                        select(e_next)
                dve.wait_ge(*at("moe_d", (it + 1) * NSTEP))
                V.tensor_copy(y_e[:, CHUNK_COLS:D], bank[6][:, :]).then_inc(sig("y1_out"), 1)
                for k in range(NTT * YC):
                    i, hf = divmod(k, YC)
                    n = TOK[i][1]
                    a = acc[0:n, i, hf * CHUNK_COLS:(hf + 1) * CHUNK_COLS]
                    dve.wait_ge(*at("moe_c", it * (NTT * YC) + k + 1))
                    V.tensor_tensor(a, a, bank[(7, 3, 2)[k % 3]][0:n, :], ALU.add).then_inc(sig("added"), 1)

            select(0)
            dve.wait_ge(*at("xtok", NTT * YC))
            with dve.Fori(0, NE - 1) as e:
                dve_expert(e, True, e + 1)
            dve_expert(NE - 1, False, 0)
            with dve.If(dve.value_load(count_i[0:1, 0:1], min_val=0, max_val=T) > CAP):
                with dve.Fori(1, PASSES) as p:
                    dve.wait_ge(*at("moe_w", p * NE))
                    for i, (t0, n) in enumerate(TOK):
                        last = V.tensor_scalar(rank[0:n, i, :], rank[0:n, i, :], float(-CAP), None, ALU.add)
                    last.then_inc(sig("rank_pass"), 1)
                    with dve.Fori(0, NE) as e:
                        dve.wait_ge(*at("rank_pass", p))
                        dve.wait_ge(*at("moe_w", p * NE + e))
                        select(e)
                        dve_expert(p * NE + e, False, 0)
            V.memset(spare[:, 5:6], 0.0).then_inc(sig("y_ready"), 1)

        @block.tensor
        def _(pe):
            pe.wait_ge(*at("constants", 2))
            pe.wait_ge(*at("par_loaded", 16 * N_PAR))
            PE.transpose(bank[4][:, 0:N_ROWS], par_rows[0:N_ROWS, :], ident[0:N_ROWS, 0:N_ROWS])
            PE.transpose(bank[4][:, P:P + N_CD], cd_rows[0:N_CD, :], ident[0:N_CD, 0:N_CD])
            n = TS * HIST
            for t in range(NL):
                PE.transpose(bank[4][:, 2 * P + t * n:2 * P + (t + 1) * n], hist_rows[:, t * P:(t + 1) * P], ident[0:n, 0:n])
                last = PE.transpose(bank[4][:, 3 * P + t * TS:3 * P + (t + 1) * TS], h0_rows[:, t * P:(t + 1) * P],
                                    ident[0:TS, 0:TS])
            last.then_inc(sig("par_psum"), 1)
            pe.wait_ge(*at("x_loaded", 32))
            for j in range(KD):
                if j >= 4:
                    pe.wait_ge(*at("xT_done", j - 3))
                for i, (t0, n) in enumerate(TOK):
                    last = PE.transpose(bank[j % 4][:, t0:t0 + n], x_tok[0:n, i, j * P:(j + 1) * P], ident[0:n, 0:n])
                last.then_inc(sig("xT_psum"), 1)
            pe.wait_ge(*at("par_done", 1))
            norm_pe(pe, 0)
            pe.wait_ge(*at("norm0_done", 1))
            dense_pe(pe, "w_in_e", IN_E // P, hT, "proj_psum", "proj_done")
            pe.wait_ge(*at("proj_done", IN_E // P))
            pe.wait_ge(*at("xc_done", 1))
            pe.wait_ge(*at("lru_w_loaded", 64))
            for g in range(2):
                for t in range(NL):
                    PE.matmul(bank[g * NL + t][:, 0:T], lru_w[:, g, t, :], xc[:, t, :], start=True, stop=True)\
                      .then_inc(sig("lru_gate_psum"), 1)
            pe.wait_ge(*at("qk_sq", 1))
            for i in range(2 * HB):
                if i >= 4:
                    pe.wait_ge(*at("qk_root", i - 3))
                PE.matmul(bank[i % 4][:, 0:T], halves[:], inv[:, i, :], start=True, stop=True).then_inc(sig("qk_ss"), 1)
            PE.matmul(bank[4][:, 0:2], lamv.broadcast_to([P, P]), half2[:], start=True, stop=True).then_inc(sig("lam_psum"), 1)
            pe.wait_ge(*at("qk_done", 1))
            pe.wait_ge(*at("lam_exp", 1))
            for i, (t0, n) in enumerate(TOK):
                for h in range(HB):
                    last = PE.transpose(bank[i][0:n, h * P:(h + 1) * P], proj[:, K_ + h, t0:t0 + n], ident[:])
                last.then_inc(sig("ktok_psum"), 1)
            for i, (t0, n) in enumerate(TOK):
                for h in range(HB):
                    last = PE.transpose(bank[3 + i][0:n, h * P:(h + 1) * P], proj[:, V_ + h, t0:t0 + n], ident[:])
                last.then_inc(sig("vtok_psum"), 1)
            for h in range(HB):
                last = PE.transpose(bank[6][0:TS, h * P:(h + 1) * P], proj[:, Q_ + h, TP:T], ident[:])
            last.then_inc(sig("qs_psum"), 1)
            for t in range(NL):
                last = PE.transpose(bank[7][0:TAIL, t * P:(t + 1) * P], proj[:, XR + t, T - TAIL:T], ident[:])
            last.then_inc(sig("tail_psum"), 1)
            pe.wait_ge(*at("tail_tok", 1))
            for t in range(NL):
                last = PE.transpose(bank[7][0:TS + 1, t * P:(t + 1) * P], hl[:, t, :], ident[:])
            last.then_inc(sig("hlast_psum"), 1)
            pe.wait_ge(*at("vtok", 3))
            pe.wait_ge(*at("qs_tok", 1))
            for b in range(TS):
                if b >= 2:
                    pe.wait_ge(*at("k_pages_used", b - 1))
                PE.matmul(bank[4 + b % 2][:, 0:AW], ident[0:TS, b:b + 1].broadcast_to([TS, P]), qs_tok, start=True, stop=True)\
                  .then_inc(sig("qb_psum"), 1)
            pe.wait_ge(*at("k_pages_used", TS))
            for i in range(2):
                for g in range(NP_):
                    c = (i * NP_ + g) * P
                    last = PE.transpose(bank[4][0:NB, c:c + P], sc_s[:, g, i].rearrange("p h b -> p (h b)"), ident[:])
            last.then_inc(sig("ss_psum"), 1)
            pe.wait_ge(*at("qk_self", 1))
            PE.matmul(bank[5][0:NB, 0:2], qk_s.rearrange("p h b -> p (h b)"), half2[:], start=True, stop=True).then_inc(sig("self_psum"), 1)
            pe.wait_ge(*at("p_s", 1))
            for g in range(NP_):
                PE.transpose(bank[6][:, g * NB:(g + 1) * NB], ss[:, 0, g * P:(g + 1) * P], ident[0:NB, 0:NB])
            PE.matmul(bank[6][:, NP_ * NB:(NP_ + 1) * NB], ss[:, 0, NP_ * P:NP_ * P + 1].broadcast_to([NB, P]), ident[0:NB, 0:NB],
                      start=True, stop=True).then_inc(sig("pT_s_psum"), 1)
            pe.wait_ge(*at("pT_s", 1))
            pe.wait_ge(*at("hlast", 1))
            for b in range(TS):
                n = TS + b
                pe.wait_ge(*at(f"kv{n % 4}_loaded", 32 * (n // 4 + 1)))
                for h in range(HB):
                    o = bank[7][:, h * TS + b:h * TS + b + 1]
                    for g in range(NP_):
                        last = PE.matmul(o, pages_kv[:, n % 4, g, h * P:(h + 1) * P], pT_s[:, g, h * TS + b:h * TS + b + 1],
                                         start=g == 0, stop=g == NP_ - 1)
                last.then_inc(sig("v_pages_used"), 1)
            pe.wait_ge(*at("v_pages_used", TS))
            for i in range(HH):
                h, k = divmod(i, 2)
                rows_ = slice(k * DH, (k + 1) * DH)
                if i >= 4:
                    pe.wait_ge(*at("scores", i - 3))
                PE.matmul(bank[i % 4][:, 0:P], proj[rows_, Q_ + h, 0:P], proj[rows_, K_ + h, 0:P], start=True, stop=True)
                PE.matmul(bank[i % 4][:, P:3 * P], proj[rows_, Q_ + h, P:2 * P], proj[rows_, K_ + h, 0:2 * P],
                          start=True, stop=True).then_inc(sig("scores_psum"), 1)
            pe.wait_ge(*at("scores", HH))
            for h in range(HB):
                pe.wait_ge(*at("probs", h + 1))
                if h >= 2:
                    pe.wait_ge(*at("pT", h - 1))
                    pe.wait_ge(*at("o_prompt", h - 1))
                for c in range(3):
                    last = PE.transpose(bank[h % 2][:, c * P:(c + 1) * P], sc_p[:, 2 * h, c * P:(c + 1) * P], ident[:])
                last.then_inc(sig("pT_psum"), 1)
                pe.wait_ge(*at("pT", h + 1))
                o = bank[2 + h % 2]
                v = [vtok[:, i, h * P:(h + 1) * P] for i in range(TT)]
                PE.matmul(o[:, 0:P], v[0], pT[h % 2][:, 0:P], start=True, stop=True)
                PE.matmul(o[:, P:2 * P], v[0], pT[h % 2][:, P:2 * P], start=True, stop=False)
                PE.matmul(o[:, P:2 * P], v[1], pT[h % 2][:, 2 * P:3 * P], start=False, stop=True).then_inc(sig("pv_psum"), 1)
            pe.wait_ge(*at("o_sq", 1))
            for h in range(HB):
                PE.matmul(bank[4 + h][:, 0:T], ones[:], osq[:, h, :], start=True, stop=True).then_inc(sig("o_ss"), 1)
            pe.wait_ge(*at("mix_done", 1))
            dense_pe(pe, "w_out_e", KD, mixT, "out_e_psum", "out_e_added")
            norm_pe(pe, 1)
            pe.wait_ge(*at("norm1_done", 1))
            for m in range(NF):
                n, c = divmod(m, CHUNK_COLS // P)
                if c == 0:
                    wait_chunk(pe, place["ffn_wg", n])
                    wait_chunk(pe, place["ffn_wu", n])
                for k, (name, s) in enumerate((("ffn_wg", "ffn_g"), ("ffn_wu", "ffn_u"))):
                    if m >= 4:
                        pe.wait_ge(*at("ffn_act", m - 3))
                    w = chunk(name, n)
                    for j in range(KD):
                        last = PE.matmul(bank[(2 * m + k) % 8][:, 0:T], w[:, j, c * P:(c + 1) * P], hT[:, j, :],
                                         start=j == 0, stop=j == KD - 1)
                    last.then_inc(sig(s), 1)
                if c == CHUNK_COLS // P - 1 or m == NF - 1:
                    used(pe)
                    used(pe)
            pe.wait_ge(*at("ffn_act", NF))
            for n in range(-(-NF // JD)):
                wait_chunk(pe, place["ffn_wd", n])
            for m in range(KD):
                if m >= 4:
                    pe.wait_ge(*at("ffn_added", m - 3))
                for j in range(NF):
                    n, c = divmod(j, JD)
                    last = PE.matmul(bank[m % 4][:, 0:T], chunk("ffn_wd", n)[:, c, m * P:(m + 1) * P], act[:, j, :],
                                     start=j == 0, stop=j == NF - 1)
                last.then_inc(sig("ffn_d_psum"), 1)
            for n in range(-(-NF // JD)):
                used(pe)

            pe.wait_ge(*at("dhist_loaded", 16))
            n = TS * HIST
            for m in range(NQ):
                k, t = divmod(m, NQ // 2)
                last = PE.transpose(bank[5 + k][:, t * n:(t + 1) * n], dhist_rows[:, m * P:(m + 1) * P], ident[0:n, 0:n])
            last.then_inc(sig("dhist_psum"), 1)
            norm_pe(pe, 2)
            pe.wait_ge(*at("norm2_done", 1))
            pe.wait_ge(*at("small_w", 64))
            for i, (t0, n) in enumerate(TOK):
                for j in range(KD):
                    last = PE.matmul(bank[7][0:n, i * 2 * HC:(i + 1) * 2 * HC], hT[:, j, t0:t0 + n], w_ba[:, j, :],
                                     start=j == 0, stop=j == KD - 1)
            last.then_inc(sig("ba_psum"), 1)
            dense_pe(pe, "w_in_o", NQ + HC, hT, "qkvz_psum", "qkvz_read")
            for n in range(QKV // CHUNK_COLS):
                if n >= 3:
                    pe.wait_ge(*at("dtail", n - 2))
                if n == 2:
                    pe.wait_ge(*at("g", 1))
                for k in range(CHUNK_COLS // P):
                    m = n * (CHUNK_COLS // P) + k
                    last = PE.transpose(bank[5 + n % 3][0:TAIL, k * P:(k + 1) * P], tailT[:, m, :], ident[:])
                last.then_inc(sig("dtail_psum"), 1)
            for r in range(2):
                pe.wait_ge(*at("l2_sq", r + 1))
                for i in range(HC):
                    k = r * HC + i
                    last = PE.matmul(bank[4][0:2 * HC, 0:T], pick[:, 2 * HC - 1 - k:4 * HC - 1 - k], inv[:, i, :],
                                     start=k == 0, stop=k == 2 * HC - 1)
                last.then_inc(sig("l2_used" if r == 0 else "l2_ss"), 1)
            pe.wait_ge(*at("dtail", QKV // CHUNK_COLS))
            PE.matmul(bank[7][:, 0:TT * HC], le_mask[:], g_t[:, 0:TT, :].rearrange("p c h -> p (c h)"), start=True, stop=True)\
              .then_inc(sig("Gt_psum"), 1)
            pe.wait_ge(*at("l2_inv", 1))
            pe.wait_ge(*at("qkvz_read", NQ + HC))
            for i in range(2 * HC):
                if i >= 4:
                    pe.wait_ge(*at("l2_applied", i - 3))
                PE.matmul(bank[i % 4][:, 0:T], ident[0:2 * HC, i:i + 1].broadcast_to([2 * HC, P]), inv[0:2 * HC, 0, :],
                          start=True, stop=True).then_inc(sig("l2_b"), 1)
            pe.wait_ge(*at("l2_applied", 2 * HC))
            for n in range(NGROUPS):
                c, h0_ = divmod(n * NG, HC)
                tc = slice(c * P, (c + 1) * P)
                hs = range(NG)

                def hb(b, h):
                    return bank[b][:, h * P:(h + 1) * P]
                if n:
                    pe.wait_ge(*at("d_done", 2 * n))
                for h in hs:
                    PE.matmul(hb(0, h), g_t[:, c, h0_ + h:h0_ + h + 1].broadcast_to([P, P]), le_mask[:], start=True, stop=True)
                for h in hs:
                    PE.matmul(hb(1, h), kT[:, h0_ + h, tc], kT[:, h0_ + h, tc], start=True, stop=True)
                for h in hs:
                    PE.matmul(hb(2, h), kT[:, h0_ + h, tc], qT[:, h0_ + h, tc], start=True, stop=True)
                for h in hs:
                    PE.transpose(hb(3, h), kT[:, h0_ + h, tc], ident[:])
                for h in hs:
                    last = PE.transpose(hb(4, h), vT[:, h0_ + h, tc], ident[:])
                last.then_inc(sig("d_in"), 1)
                pe.wait_ge(*at("d_T0", n + 1))
                for h in hs:
                    last = PE.transpose(hb(5, h), Tm[:, h, :], ident[:])
                last.then_inc(sig("d_T0t"), 1)
                for l in range(1, LEVELS):
                    k = n * (LEVELS - 1) + l
                    pe.wait_ge(*at("d_Am", k))
                    pe.wait_ge(*at("d_T", n * LEVELS + l))
                    for h in hs:
                        last = PE.matmul(hb(6, h), Am[:, h, :], Tt[:, h, :], start=True, stop=True)
                    last.then_inc(sig("d_Y"), 1)
                    pe.wait_ge(*at("d_Yc", k))
                    for h in hs:
                        last = PE.matmul(hb(7, h), Tm[:, h, :], Yb[:, h, :], start=True, stop=True)
                    if l < LEVELS - 1:
                        for h in hs:
                            last = PE.matmul(hb(0, h), Yb[:, h, :], Tm[:, h, :], start=True, stop=True)
                    last.then_inc(sig("d_D"), 1)
                pe.wait_ge(*at("d_T", (n + 1) * LEVELS))
                if c:
                    for h in hs:
                        last = PE.matmul(hb(1, h), KB[:, h, :], Tt[:, h, :], start=True, stop=True)
                    last.then_inc(sig("d_w"), 1)
                    pe.wait_ge(*at("d_nw", n - NGROUPS // TT + 1))
                for h in hs:
                    last = PE.matmul(hb(2, h), Tt[:, h, :], VB[:, h, :], start=True, stop=not c)
                    if c:
                        last = PE.matmul(hb(2, h), NW[:, h, :], S_pr[:, h0_ + h, :], start=False, stop=True)
                last.then_inc(sig("d_v"), 1)
                pe.wait_ge(*at("d_vn", n + 1))
                for h in hs:
                    last = PE.matmul(hb(3, h), VN[:, h, :], QK[:, h, :], start=True, stop=not c)
                    if c:
                        last = PE.matmul(hb(3, h), S_pr[:, h0_ + h, :], QD[:, h, :], start=False, stop=True)
                last.then_inc(sig("d_o"), 1)
                for h in hs:
                    last = PE.matmul(hb(4, h), KDc[:, h, :], VN[:, h, :], start=True, stop=True)
                last.then_inc(sig("d_S"), 1)
            pe.wait_ge(*at("d_done", 2 * NGROUPS))
            PE.matmul(bank[0][:, 0:2 * HC * TS], ones[0:TS, :], gd[0:TS].rearrange("p a b c -> p (a b c)"), start=True, stop=True)\
              .then_inc(sig("s_gb"), 1)
            pe.wait_ge(*at("s_prod", 1))
            PE.matmul(bank[1][:, 0:HC * TS], ones[:], inv[:, 0, 0:HC * TS], start=True, stop=True).then_inc(sig("s_qk"), 1)
            for h in range(HC):
                pe.wait_ge(*at(f"state{h % 4}_loaded", 16 * (h // 4 + 1)))
                if h >= 2:
                    pe.wait_ge(*at("s_o", h - 1))
                for b in range(TS):
                    last = PE.matmul(bank[2 + h % 2][:, 2 * b:2 * b + 2], s_ring[h % 4][:, b, :],
                                     qkvT[:, h:h + HC + 1:HC, TP + b], start=True, stop=True)
                last.then_inc(sig("s_ks"), 1)
                pe.wait_ge(*at("s_v", h + 1))
                if h:
                    pe.wait_ge(*at("s_vd", h))
                PE.transpose(bank[4][0:TS, 0:P], vn_s, ident[:])
                PE.transpose(bank[4][0:TS, P:2 * P], kT[:, h, TP:T], ident[:]).then_inc(sig("s_vt"), 1)
                pe.wait_ge(*at("s_vd", h + 1))
                if h:
                    pe.wait_ge(*at("s_state", h))
                for k in range(2):
                    n = TS // 2
                    last = PE.matmul(bank[5 + k][:, :], k_row, v_diag[0:TS, k * n:(k + 1) * n, :].rearrange("p b e -> p (b e)"),
                                     start=True, stop=True)
                last.then_inc(sig("s_outer"), 1)
            pe.wait_ge(*at("on_sq", 1))
            for i in range(HC):
                last = PE.matmul(bank[4][0:HC, 0:T], pick[:, 2 * HC - 1 - i:3 * HC - 1 - i], inv[:, i, :],
                                 start=i == 0, stop=i == HC - 1)
            last.then_inc(sig("on_ss"), 1)
            pe.wait_ge(*at("on_inv", 1))
            for h in range(HC):
                if h >= 4:
                    pe.wait_ge(*at("on_applied", h - 3))
                PE.matmul(bank[h % 4][:, 0:T], ident[0:HC, h:h + 1].broadcast_to([HC, P]), inv[0:HC, 0, :],
                          start=True, stop=True).then_inc(sig("on_b"), 1)
            pe.wait_ge(*at("on_done", 1))
            dense_pe(pe, "w_out_o", KD, oT, "out_o_psum", "out_o_added")
            norm_pe(pe, 3)
            pe.wait_ge(*at("norm3_done", 1))
            PE.matmul(bank[7][:, 0:P], ones[:], lt_mask[:], start=True, stop=True).then_inc(sig("iota_psum"), 1)
            for i, (t0, n) in enumerate(TOK):
                for j in range(KD):
                    last = PE.matmul(bank[5][0:n, i * NE:(i + 1) * NE], hT[:, j, t0:t0 + n], w_router[:, j, :],
                                     start=j == 0, stop=j == KD - 1)
            last.then_inc(sig("logits_psum"), 1)
            for s, src in (("xtok", xT), ("htok", hT)):
                for i, (t0, n) in enumerate(TOK):
                    for k in range(YC):
                        r = i * YC + k
                        if r >= 4:
                            pe.wait_ge(*at(s, r - 3))
                        elif s == "htok":
                            pe.wait_ge(*at("xtok", NTT * YC))
                        for m in range(KF):
                            last = PE.transpose(bank[r % 4][0:n, m * P:(m + 1) * P], src[:, k * KF + m, t0:t0 + n], ident[:])
                        last.then_inc(sig(s + "_psum"), 1)
            pe.wait_ge(*at("masks", 1))
            for i, (t0, n) in enumerate(TOK):
                for u in range(i + 1):
                    m = TOK[u][1]
                    PE.matmul(bank[6][0:n, i * NE:(i + 1) * NE], (lt_mask if u == i else ones)[0:m, 0:n], mask[0:m, u, :],
                              start=u == 0, stop=u == i)
            for u in range(NTT):
                m = TOK[u][1]
                last = PE.matmul(bank[6][:, NTT * NE:(NTT + 1) * NE], ones[0:m, :], mask[0:m, u, :], start=u == 0, stop=u == NTT - 1)
            last.then_inc(sig("ranks_psum"), 1)
            pe.wait_ge(*at("htok", NTT * YC))
            pe.wait_ge(*at("flag", 1))

            def dispatch(it):
                pe.wait_ge(*at("sel", it + 1))
                for r in range(2):
                    for jj in range(KD // 2):
                        j = r * (KD // 2) + jj
                        for i, (t0, n) in enumerate(TOK):
                            last = PE.matmul(bank[(7, 3)[r]][:, jj * CAP:(jj + 1) * CAP], h_tok[0:n, i, j * P:(j + 1) * P],
                                             sel[0:n, i, :], start=i == 0, stop=i == NTT - 1)
                    last.then_inc(sig("moe_disp"), 1)

            def transposes(it, c):
                pe.wait_ge(*at("act_done", it * NSTEP + c + 3))
                pe.wait_ge(*at("tr_out", it * NSTEP + c + 1))
                if c == 0:
                    pe.wait_ge(*at("wt_out", it + 1))
                for k in range(KF):
                    last = PE.transpose(bank[4][:, k * P:(k + 1) * P], m_act[:, c % 2, k * P:(k + 1) * P], ident[:])
                last.then_inc(sig("moe_tr"), 1)

            def down(it, c):
                wait_e_chunk(pe, it, "d", c)
                pe.wait_ge(*at("tr_out", it * NSTEP + c + 2))
                if c == 0:
                    pe.wait_ge(*at("y0_out", it + 1))
                    pe.wait_ge(*at("y1_out", it + 1))
                w = e_slot("d", c)
                for k in range(KF):
                    for hf in range(YC):
                        last = PE.matmul(bank[5 + hf][:, :], m_actT[:, c % 2, k, :], w[:, k, hf * CHUNK_COLS:(hf + 1) * CHUNK_COLS],
                                         start=c == 0 and k == 0, stop=c == NSTEP - 1 and k == KF - 1)
                last.then_inc(sig("moe_d"), 1)

            def pe_expert(it, more):
                pe.wait_ge(*at("hte", it * 2 + 2))
                for c in range(NSTEP):
                    pe.wait_ge(*at("act_done", it * NSTEP + c + 1))
                    if c == 1:
                        pe.wait_ge(*at("added", (it + 1) * (NTT * YC)))
                    wait_e_chunk(pe, it, "g", c)
                    w = e_slot("g", c)
                    for j in range(KD):
                        last = PE.matmul(bank[c % 2 * 2][:, :], hTe[:, j, :], w[:, j, :], start=j == 0, stop=j == KD - 1)
                    last.then_inc(sig("moe_g"), 1)
                    if c == 0:
                        pe.wait_ge(*at("tr_out", it * NSTEP + 1))
                        for i, (t0, n) in enumerate(TOK):
                            last = PE.transpose(bank[4][:, t0:t0 + n], selw[0:n, i, :], ident[0:n, 0:n])
                        last.then_inc(sig("moe_w"), 1)
                    else:
                        transposes(it, c - 1)
                    wait_e_chunk(pe, it, "u", c)
                    w = e_slot("u", c)
                    for j in range(KD):
                        last = PE.matmul(bank[c % 2 * 2 + 1][:, :], hTe[:, j, :], w[:, j, :], start=j == 0, stop=j == KD - 1)
                    last.then_inc(sig("moe_u"), 1)
                    if c:
                        down(it, c - 1)
                if more:
                    dispatch(it + 1)
                transposes(it, NSTEP - 1)
                down(it, NSTEP - 1)
                pe.wait_ge(*at("y0_out", it + 2))
                pe.wait_ge(*at("y1_out", it + 2))
                if more:
                    pe.wait_ge(*at("hte", it * 2 + 4))
                for k in range(NTT * YC):
                    i, hf = divmod(k, YC)
                    t0, n = TOK[i]
                    if k >= 3:
                        pe.wait_ge(*at("added", (it + 1) * (NTT * YC) + (k - 2)))
                    PE.matmul(bank[(7, 3, 2)[k % 3]][0:n, :], WT[:, t0:t0 + n], y_e[:, hf * CHUNK_COLS:(hf + 1) * CHUNK_COLS],
                              start=True, stop=True).then_inc(sig("moe_c"), 1)

            dispatch(0)
            with pe.Fori(0, NE - 1) as e:
                pe_expert(e, True)
            pe_expert(NE - 1, False)
            with pe.If(pe.value_load(count_i[0:1, 0:1], min_val=0, max_val=T) > CAP):
                with pe.Fori(1, PASSES) as p:
                    with pe.Fori(0, NE) as e:
                        pe.wait_ge(*at("added", (p * NE + e + 1) * (NTT * YC)))
                        dispatch(p * NE + e)
                        pe_expert(p * NE + e, False)


INPUTS = ["x_prompt", "x_sample", "cache_k", "cache_v", "state_lru_conv", "state_lru_h", "state_delta_conv",
          "state_delta_s", "page_table", "ln_mix_e", "w_in_e", "conv_lru_w", "conv_lru_b", "lru_wx", "lru_bx",
          "lru_wa", "lru_ba", "lru_lambda", "qk_gain_q", "qk_gain_k", "lam_q1", "lam_k1", "lam_q2", "lam_k2",
          "subln_g", "w_out_e", "ln_ffn_e", "ffn_wg", "ffn_wu", "ffn_wd", "ln_mix_o", "w_in_o", "conv_delta_w",
          "a_log", "dt_bias", "onorm_g", "w_out_o", "ln_ffn_o", "router_w", "moe_wg", "moe_wu", "moe_wd"]
OUTPUTS = ["y_prompt", "y_sample", "k_prompt", "v_prompt", "lru_conv_prompt", "lru_h_prompt", "delta_conv_prompt",
           "delta_s_prompt", "k_sample", "v_sample", "lru_conv_sample", "lru_h_sample", "delta_conv_sample",
           "delta_s_sample"]


def output_shapes(s):
    _, bp, tp, d = (1,) + s["x_prompt"]
    bs, ts, _ = s["x_sample"]
    hb, e = s["cache_k"][3:]
    hist, lw = s["state_lru_conv"][2:]
    qkv = s["state_delta_conv"][3]
    hc, dk, dv = s["state_delta_s"][2:]
    return {"y_prompt": (bp, tp, d), "y_sample": (bs, ts, d),
            "k_prompt": (1, bp, tp, hb, e), "v_prompt": (1, bp, tp, hb, e),
            "lru_conv_prompt": (1, bp, hist, lw), "lru_h_prompt": (1, bp, lw),
            "delta_conv_prompt": (1, bp, hist, qkv), "delta_s_prompt": (1, bp, hc, dk, dv),
            "k_sample": (1, bs, ts, hb, e), "v_sample": (1, bs, ts, hb, e),
            "lru_conv_sample": (1, bs, hist, lw), "lru_h_sample": (1, bs, lw),
            "delta_conv_sample": (1, bs, hist, qkv), "delta_s_sample": (1, bs, hc, dk, dv)}


def kernel(**inputs):
    import numpy as np
    import concourse.bacc as bacc
    from concourse.bass_utils import run_bass_kernel_spmd

    nc = bacc.Bacc("TRN2", target_bir_lowering=False, num_devices=1)
    arrays = {f"in_{n}": np.ascontiguousarray(inputs[n]) for n in INPUTS}
    A = {n: nc.dram_tensor(f"in_{n}", arrays[f"in_{n}"].shape, mybir.dt.from_np(arrays[f"in_{n}"].dtype),
                           kind="ExternalInput").ap() for n in INPUTS}
    shapes = output_shapes({n: arrays[f"in_{n}"].shape for n in INPUTS})
    O = {n: nc.dram_tensor(f"out_{n}", shapes[n], F32, kind="ExternalOutput").ap() for n in OUTPUTS}
    program(nc, A, O)
    r = run_bass_kernel_spmd(nc, [arrays], core_ids=[0])
    return tuple(r.results[0][f"out_{n}"] for n in OUTPUTS)
```

```python
import math
from contextlib import ExitStack

import concourse.bass as bass
from concourse import mybir

F32 = mybir.dt.float32
F32R = mybir.dt.float32r
I32 = mybir.dt.int32
U32 = mybir.dt.uint32
ACT = mybir.ActivationFunctionType
ALU = mybir.AluOpType
X = mybir.AxisListType.X

P = 128
CHUNK_COLS = 512
SLOTS = 3
EPS = 1e-6
MASKED = -1e30
RG_C = 8.0
LAM_INIT = 0.8 - 0.6 * math.exp(-0.3 * 0)


def program(nc, A, O):
    TP, D = A["x_prompt"].shape[1:]
    TS = A["x_sample"].shape[0]
    T = TP + TS
    KD = D // P
    TT = TP // P
    TOK = [(i * P, P) for i in range(TT)] + [(TP, TS)]
    LW = A["lru_bx"].shape[1]
    NL = LW // P
    HB, E2 = A["cache_k"].shape[3:]
    DH = E2 // 2
    AW = HB * E2
    NP_ = A["page_table"].shape[1]
    NPOOL = A["cache_k"].shape[1]
    CW = A["conv_lru_w"].shape[1]
    HIST = CW - 1
    IN_E = A["w_in_e"].shape[2]
    FF = A["ffn_wg"].shape[2]
    NF = FF // P
    _, _, HC, DK, DV = A["state_delta_s"].shape
    QKV = A["conv_delta_w"].shape[2]
    NQ = QKV // P
    NE = A["router_w"].shape[2]
    FE = A["moe_wg"].shape[3]
    NCH = FE // CHUNK_COLS
    HH = 2 * HB
    NB = TS * HB
    assert D == KD * P and TP == TT * P and TT == 2 and E2 == P and NP_ == 2 and FE % CHUNK_COLS == 0
    TAIL = HIST + TS

    with ExitStack() as ctx:
        def sb(name, shape, dt=F32):
            return ctx.enter_context(nc.sbuf_tensor(name, shape, dt))

        sems, step_at, given = {}, {}, {}

        def sem(name):
            if name not in sems:
                sems[name] = ctx.enter_context(nc.semaphore(name))
            return sems[name]

        def sig(name):
            if name not in step_at:
                return sem(name)
            engine, first, count = step_at[name]
            assert given.get(engine, 0) == first + given.get(name, 0) and given.get(name, 0) < count, (name, given.get(engine, 0), first)
            given[engine] = given.get(engine, 0) + 1
            given[name] = given.get(name, 0) + 1
            return sem(engine)

        def at(name, count=1):
            if name not in step_at:
                return sem(name), count
            engine, first, most = step_at[name]
            assert 0 < count <= most, (name, count)
            return sem(engine), first + count

        def order(engine, *events):
            first = 0
            for name, count in events:
                step_at[name] = (engine, first, count)
                first += count

        order("scalar_steps",
              ("xT_done", KD), ("norm0_sq", 1), ("lam_absexp", 1), ("norm0_root", 1), ("norm0_hi", 2), ("proj_done", IN_E // P),
              ("lru_gates", 2 * NL), ("lru_a", 2), ("gelu", 1), ("lru_root", 1), ("ya_hi", 1), ("qk_sq", 1), ("qk_root", HH),
              ("lam_exp", 1), ("ktok", 3), ("vtok", 3), ("qs_tok", 1), ("tail_tok", 1), ("ss", 1), ("exps_s", 2),
              ("exps", 2 * HH), ("o_sq", 1), ("o_root", HB), ("mix_hi", 1), ("norm1_sq", 1), ("norm1_root", 1), ("norm1_hi", 2), ("ffn_sil", NF),
              ("norm2_sq", 1), ("norm2_root", 1), ("norm2_hi", 2), ("beta", 1), ("g_absexp", 1), ("ealog", 1),
              ("dtail", QKV // CHUNK_COLS), ("l2_sq", 2), ("l2_root", 1), ("eG", 1), ("s_egb", 1), ("s_qks", 1),
              ("on_sq", 1), ("on_root", 1), ("on_hi", 2), ("norm3_sq", 1), ("norm3_root", 1), ("gate_exp", 1),
              ("xtok", 6), ("htok", 6))
        order("tensor_steps",
              ("par_psum", 1), ("xT_psum", KD), ("norm0_ss", 1), ("proj_psum", IN_E // P), ("lru_gate_psum", 2 * NL),
              ("qk_ss", HH), ("lam_psum", 1), ("ktok_psum", 3), ("vtok_psum", 3), ("qs_psum", 1), ("tail_psum", 1),
              ("hlast_psum", 1), ("qb_psum", TS), ("ss_psum", 1), ("self_psum", 1), ("pT_s_psum", 1),
              ("scores_psum", HH), ("o_ss", HB), ("out_e_psum", KD), ("norm1_ss", 1), ("ffn_d_psum", KD),
              ("dhist_psum", 1), ("norm2_ss", 1), ("ba_psum", 1), ("qkvz_psum", NQ + HC),
              ("dtail_psum", QKV // CHUNK_COLS), ("l2_used", 1), ("l2_ss", 1), ("Gt_psum", 1), ("l2_b", 2 * HC),
              ("s_gb", 1), ("s_qk", 1), ("on_ss", 1), ("on_b", HC), ("out_o_psum", KD), ("norm3_ss", 1),
              ("iota_psum", 1), ("logits_psum", 1), ("xtok_psum", 6), ("htok_psum", 6), ("ranks_psum", 1))
        order("vector_steps",
              ("par_done", 1), ("lam_abs", 1), ("norm0_h", 2), ("norm0_done", 2), ("xc_done", 1), ("lru_y", 1), ("lru_m", 1),
              ("lru_done", 1), ("qk_done", 1), ("ya_lo", 1), ("hlast", 1), ("k_pages_used", TS), ("qk_self", 1), ("neg_max_s", 1),
              ("p_s", 1), ("pT_s", 1), ("o_sample", 1), ("scores", HH), ("neg_max", 1), ("probs", HB),
              ("mix_done", 1), ("mix_lo", 1), ("out_e_added", KD), ("norm1_h", 2), ("norm1_done", 2), ("ffn_act", NF), ("ffn_added", KD),
              ("norm2_h", 2), ("norm2_done", 2), ("ba_read", 1), ("g_abs", 1), ("g", 1), ("dconv", NQ), ("Gt", 1), ("l2_inv", 1),
              ("l2_applied", 2 * HC), ("s_prod", 1), ("on_inv", 1), ("on_applied", HC), ("on_done", 2), ("on_lo", 2),
              ("out_o_added", KD), ("norm3_done", 1), ("iota", 1), ("top_diff", 1), ("masks", 1), ("ranks", 1))

        ring = sb("weight_ring", [P, SLOTS, KD * CHUNK_COLS])
        PIECE = KD * CHUNK_COLS // 2
        SPLIT = 3
        whi = sb("weight_hi", [P, SPLIT, PIECE], F32R)
        wlo = sb("weight_lo", [P, SPLIT, PIECE], F32R)
        h_hi = sb("h_hi", [P, KD, T], F32R)
        h_lo = sb("h_lo", [P, KD, T], F32R)

        def expert_part(t):
            flat = t[:].rearrange("p a b -> p (a b)")
            KC = CHUNK_COLS // P
            return (flat[:, 0:KD * P].rearrange("p (j t) -> p j t", j=KD),
                    flat[:, KD * P:KD * P + 2 * KC * P].rearrange("p (s k t) -> p s k t", s=2, k=KC))

        hte_h, act_h = expert_part(h_hi)
        hte_l, act_l = expert_part(h_lo)
        ident = sb("ident", [P, P])
        ones = sb("ones", [P, P])
        halves = sb("halves", [P, P])
        half2 = sb("half2", [P, 2])
        le_mask = sb("le_mask", [P, P])
        lt_mask = sb("lt_mask", [P, P])
        causal = sb("causal", [P, 3 * P])
        eps_t = sb("eps_t", [P, 1])
        par = sb("par", [P, 80])
        cd = sb("cd", [P, 96])
        small = sb("small", [P, 304])
        xT = sb("xT", [P, KD, T])
        hT = sb("hT", [P, KD, T])
        W = 17700
        work = sb("work", [P, W])
        bank = [ctx.enter_context(nc.psum_tensor(f"bank{i}", [P, CHUNK_COLS], F32)) for i in range(8)]

        class Arena:

            def __init__(self):
                self.at = 0

            def take(self, *dims):
                n = math.prod(dims)
                v = work[:, self.at:self.at + n]
                self.at += n
                assert self.at <= W, self.at
                names = "abcd"[:len(dims)]
                if len(dims) > 1:
                    v = v.rearrange(f"p ({' '.join(names)}) -> p {' '.join(names)}", **dict(zip(names, dims)))
                return v

        rows, row = {}, 0
        for name, ap in (("ln_mix_e", A["ln_mix_e"]), ("conv_lru_w", A["conv_lru_w"]), ("conv_lru_b", A["conv_lru_b"]),
                         ("lru_bx", A["lru_bx"]), ("lru_ba", A["lru_ba"]), ("lru_lambda", A["lru_lambda"]),
                         ("ln_ffn_e", A["ln_ffn_e"]), ("ln_mix_o", A["ln_mix_o"]), ("ln_ffn_o", A["ln_ffn_o"]),
                         ("subln_g", A["subln_g"]), ("onorm_g", A["onorm_g"])):
            n = math.prod(ap.shape)
            rows[name] = (row, n // P, ap)
            row += n // P
        r_gq, r_gk, r_lq, r_lk = row, row + 1, row + 2, row + 3
        N_ROWS = row + 4
        N_CD = CW * NQ

        def col(name, i=0):
            return par[:, rows[name][0] + i:rows[name][0] + i + 1]

        sm_at = [0]

        def vec(n):
            v = small[:, sm_at[0]:sm_at[0] + n]
            sm_at[0] += n
            assert sm_at[0] <= 304
            return v

        def cols(ap, c0, n):
            return ap[:, c0:c0 + n].rearrange("(j p) n -> p j n", p=P)

        dense = []
        place = {}

        def stream_cols(name, ap, total, n):
            c0 = n * CHUNK_COLS
            w = min(CHUNK_COLS, total - c0)
            place[name, n] = len(dense)
            dense.append((cols(ap, c0, w), KD, w))

        for n in range(IN_E // CHUNK_COLS):
            stream_cols("w_in_e", A["w_in_e"][0], IN_E, n)
        for n in range(D // CHUNK_COLS):
            stream_cols("w_out_e", A["w_out_e"][0], D, n)
        NFC = -(-FF // CHUNK_COLS)
        for n in range(NFC):
            stream_cols("ffn_wg", A["ffn_wg"][0], FF, n)
            stream_cols("ffn_wu", A["ffn_wu"][0], FF, n)
        for m in range(KD):
            place["ffn_wd", m] = len(dense)
            dense.append((cols(A["ffn_wd"][0], m * P, P), NF, P))
        NQC = (QKV + D) // CHUNK_COLS
        for n in range(NQC):
            stream_cols("w_in_o", A["w_in_o"][0], QKV + D, n)
        for n in range(D // CHUNK_COLS):
            stream_cols("w_out_o", A["w_out_o"][0], D, n)
        ND = len(dense)

        def slot_view(i, k, w):
            return ring[:, i % SLOTS, 0:k * w].rearrange("p (j n) -> p j n", j=k)

        def chunk(name, n):
            i = place[name, n]
            return slot_view(i, dense[i][1], dense[i][2])

        def wait_chunk(eng, i):
            eng.wait_ge(sig(f"slot{i % SLOTS}_loaded"), 16 * (i // SLOTS + 1))

        split_at = {}
        for i in range(ND):
            if i not in [place["ffn_wd", m] for m in range(KD)]:
                split_at[i] = 2 * len(split_at)
        chunk_of = {n: i for i, n in split_at.items()}
        NDP = 2 * len(split_at)

        def dense_piece(p):
            i = chunk_of[p - p % 2]
            half = dense[i][1] * dense[i][2] // 2
            return i, ring[:, i % SLOTS, p % 2 * half:(p % 2 + 1) * half], half

        a0 = Arena()
        proj = a0.take(IN_E // P, T)
        mixT = proj[:, 0:KD, :]
        inv = a0.take(KD, T)
        pages_kv = a0.take(4, NP_, AW)
        scr = a0.take(3 * D)
        ktok = a0.take(3, AW)
        vtok = a0.take(3, AW)
        lru_w = vtok.rearrange("p a b -> p (a b)")[:, 0:2 * NL * P].rearrange(
            "p (a b c) -> p a b c", a=2, b=NL)
        GATE, XR, Q_, K_, V_ = 0, NL, 2 * NL, 2 * NL + HB, 2 * NL + 2 * HB
        x_tok = scr.rearrange("p (t d) -> p t d", t=3)
        kt_flat = ktok.rearrange("p a b -> p (a b)")
        par_rows, cd_rows = kt_flat[:, 0:P], kt_flat[:, P:2 * P]
        hist_rows = kt_flat[0:TS * HIST, 2 * P:2 * P + LW]
        h0_rows = kt_flat[0:TS, 2 * P + LW:2 * P + 2 * LW]
        kv_flat = pages_kv.rearrange("p a b c -> p (a b c)")
        xc = kv_flat[:, 0:NL * T].rearrange("p (a b) -> p a b", a=NL)
        decay_a = kv_flat[:, NL * T:2 * NL * T].rearrange("p (a b) -> p a b", a=NL)
        gate_x = inv[:, 0:NL, :]
        gate_a = inv[:, NL:2 * NL, :]
        tanh_y = scr[:, 0:NL * T].rearrange("p (a b) -> p a b", a=NL)
        tmp_l = scr[:, NL * T:2 * NL * T].rearrange("p (a b) -> p a b", a=NL)
        hist = vec(NL * TS * HIST).rearrange("p (a b c) -> p a b c", a=NL, b=TS)
        h0 = vec(NL * TS).rearrange("p (a b) -> p a b", a=NL)
        sp8 = vec(NL)
        v_s = [vec(NL) for _ in range(3)]
        lamv = vec(1)
        lam_e = vec(2)
        nlam = vec(1)
        mx = vec(2 * HH)
        ssum = vec(2 * HH)
        rsum = vec(2 * HH)
        subg = vec(1)
        mx_s, ssum_s, rsum_s = vec(2), vec(2), vec(2)
        sc_p = scr[:, 0:HH * 3 * P].rearrange("p (i c) -> p i c", i=HH)
        inv_flat = inv.rearrange("p a b -> p (a b)")
        pT = [inv_flat[:, k * 384:k * 384 + 3 * P] for k in range(2)]
        kv_mul = inv_flat[:, 0:NP_ * AW].rearrange("p (a b) -> p a b", a=NP_)
        qs_tok = inv_flat[0:TS, 1024:1024 + AW]
        tail_tok = inv_flat[0:TAIL, 1536:1536 + LW]
        sc_s = scr[:, 0:NP_ * HH * TS].rearrange("p (g i h b) -> p g i h b", g=NP_, i=2, h=HB)
        qk_s = scr[:, 256:256 + NB].rearrange("p (h b) -> p h b", h=HB)
        NK_S = NP_ * P + 1
        ss = scr[0:NB, 512:512 + 2 * NK_S].rearrange("p (i c) -> p i c", i=2)
        pT_s = scr[:, 1100:1100 + NP_ * NB].rearrange("p (g n) -> p g n", g=NP_)
        pself = scr[:, 1200:1200 + NB]
        osq = scr[:, 1300:1300 + HB * T].rearrange("p (h t) -> p h t", h=HB)
        hl = vec(NL * (TS + 1)).rearrange("p (a b) -> p a b", a=NL)
        hl_tok = scr[0:TS + 1, 2560:2560 + LW]
        act = work[:, 0:NF * T].rearrange("p (a b) -> p a b", a=NF)
        sil = scr[:, 0:4 * T].rearrange("p (a b) -> p a b", a=4)
        pg_sb = sb("page_numbers", [1, TS * NP_], I32)


        def shaped(v, dims):
            names = "abcd"[:len(dims)]
            return v if len(dims) == 1 else v.rearrange(f"p ({' '.join(names)}) -> p {' '.join(names)}", **dict(zip(names, dims)))

        def cut(o, *dims):
            return shaped(work[:, o:o + math.prod(dims)], dims)

        NGROUPS = TT * HC // 4
        NG = 4
        LEVELS = 7
        GRP = NG * P
        INV0 = (IN_E // P) * T
        QKV0 = INV0 + KD * T
        TMP0 = QKV0 + NQ * T
        A_0 = HC * T + HC * P
        B_0 = TMP0 + LEVELS * P
        zT = cut(0, HC, T)
        pre = cut(HC * T, 4, T)
        S_pr = cut(HC * T, HC, P)
        qkvT = cut(QKV0, NQ, T)
        qT, kT, vT = qkvT[:, 0:HC, :], qkvT[:, HC:2 * HC, :], qkvT[:, 2 * HC:3 * HC, :]
        oT = hT
        dhist_rows = work[0:TS * HIST, TMP0:TMP0 + QKV]
        tail_rows = work[0:TAIL, TMP0:TMP0 + QKV]
        tailT = cut(TMP0 + QKV, NQ, TAIL)
        dhist = cut(TMP0 + QKV + NQ * TAIL, NQ, TS, HIST)
        lvl = cut(TMP0, LEVELS, P)
        Gb, EA, QK, Tm = (cut(A_0 + k * GRP, NG, P) for k in range(4))
        Tt, Am, KB, KDc, VB, QD = (cut(B_0 + k * GRP, NG, P) for k in range(6))
        Yb, NW, VN = Gb, Tm, Am
        s_ring = [cut(A_0, TS, P), cut(A_0 + 2 * GRP, TS, P), cut(B_0, TS, P), cut(B_0 + 2 * GRP, TS, P)]
        v_diag = cut(B_0 + 4 * GRP, TS, P)
        assert A_0 + 4 * GRP <= INV0 and B_0 + 6 * GRP <= W and TMP0 + QKV + NQ * (TAIL + TS * HIST) <= W
        gt_mask = sb("gt_mask", [P, P])
        w_ba = sb("w_ba", [P, KD, 2 * HC])
        w_router = sb("w_router", [P, KD, NE])
        alog_b = sb("alog_b", [P, HC])
        dt_b = sb("dt_b", [P, HC])
        NS1 = 599
        sm1 = sb("sm1", [P, NS1])
        sm1_at = [0]

        def vec1(*dims):
            n = math.prod(dims)
            v = sm1[:, sm1_at[0]:sm1_at[0] + n]
            sm1_at[0] += n
            assert sm1_at[0] <= NS1
            return shaped(v, dims)

        NTT = TT + 1
        pick = vec1(4 * HC - 1)
        ba = vec1(NTT, 2 * HC)
        beta = vec1(NTT, HC)
        g_t = vec1(NTT, HC)
        sp_t = [vec1(NTT, HC) for _ in range(3)]
        Gt = vec1(TT, HC)
        eG = vec1(TT, HC)
        bkb = vec1(TT, HC)
        kd_s = vec1(HC)
        ge = vec1(HC)
        gd = vec1(2, HC, TS)
        egb = vec1(2, HC, TS)
        qks = vec1(HC, TS)
        k_row = inv[0:TS, 1, 0:P]
        vn_s = vec1(TS)
        vn_t = vec1(TS)


        NSTEP = FE // CHUNK_COLS
        KF = CHUNK_COLS // P
        CAP = P
        PASSES = -(-T // CAP)
        YC = D // CHUNK_COLS
        acc = cut(0, NTT, D)
        m_act = cut(NTT * D, 2, CHUNK_COLS)
        m_sil = cut(NTT * D + 2 * CHUNK_COLS, 2, CHUNK_COLS)
        assert NTT * D + 4 * CHUNK_COLS <= INV0
        h_tok = cut(QKV0, NTT, D)
        raw_last = cut(QKV0 + NTT * D, PIECE)
        mo = [QKV0 + NTT * D + PIECE]

        def more_of(*dims):
            v = cut(mo[0], *dims)
            mo[0] += math.prod(dims)
            assert mo[0] <= W
            return v

        sel = more_of(NTT, CAP)
        selw = more_of(NTT, CAP)
        WT = more_of(T)
        y_e = more_of(D)
        iota = more_of(P)
        logit = more_of(NTT, NE)
        top = more_of(NTT, NE)
        top_i = more_of(NTT, NE).bitcast(U32)
        idx_f = more_of(NTT, 2)
        gates = more_of(NTT, 2)
        comb = more_of(NTT, NE)
        comb2 = more_of(NTT, NE)
        mask = more_of(NTT, NE)
        rank = more_of(NTT, NE)
        count = more_of(1)
        count_i = more_of(1).bitcast(I32)
        spare = more_of(8)
        FAR = 16384.0
        order_e = [("g", 0), ("u", 0)]
        for c in range(1, NSTEP):
            order_e += [("g", c), ("u", c), ("d", c - 1)]
        order_e.append(("d", NSTEP - 1))
        order_e = [(kind, c, part) for kind, c in order_e for part in range(2)]
        PER = len(order_e)
        RAW = 2 * SLOTS + 1
        assert PER % RAW == 0 and PER % SPLIT == 0
        e_at = {k: i for i, k in enumerate(order_e)}
        FREED = [ND - SLOTS + i for i in range(SLOTS)]
        FFN_END = split_at[place["w_in_o", 0]]

        def raw_piece(n):
            r = n % RAW
            if r == RAW - 1:
                return raw_last
            return ring[:, FREED[r // 2] % SLOTS, r % 2 * PIECE:(r % 2 + 1) * PIECE]

        def piece_view(flat, kind):
            return flat.rearrange("p (j n) -> p j n", n=D if kind == "d" else CHUNK_COLS)

        def hi_part(p, src, size):
            return SC.activation(whi[:, p % SPLIT, 0:size], src, ACT.Copy).then_inc(sig("hi_done"), 1)

        def lo_part(p, src, size):
            V.tensor_tensor(wlo[:, p % SPLIT, 0:size], src, whi[:, p % SPLIT, 0:size].bitcast(F32), ALU.subtract)\
             .then_inc(sig("lo_done"), 1)

        def take_hi(act_e, it, n):
            act_e.wait_ge(*at(f"raw{n % RAW}_loaded", it * (16 * (PER // RAW)) + 16 * (n // RAW + 1)))
            act_e.wait_ge(*at("piece_used", it * PER + (NDP + n - SPLIT + 1)))
            hi_part(NDP + n, raw_piece(n), PIECE)

        def take_lo(dve, it, n):
            dve.wait_ge(*at("hi_done", it * PER + (NDP + n + 1)))
            lo_part(NDP + n, raw_piece(n), PIECE)

        def dense_hi(act_e, p):
            if p >= NDP:
                return take_hi(act_e, 0, p - NDP)
            i, src, size = dense_piece(p)
            wait_chunk(act_e, i)
            if p >= SPLIT:
                act_e.wait_ge(*at("piece_used", p - SPLIT + 1))
            hi_part(p, src, size)

        def dense_lo(dve, p):
            if p >= NDP:
                return take_lo(dve, 0, p - NDP)
            dve.wait_ge(*at("hi_done", p + 1))
            _, src, size = dense_piece(p)
            lo_part(p, src, size)

        def behind(split, eng, name, n, part, last=None):
            p = split_at[place[name, n]] + part + SPLIT
            if last is None or p < last:
                split(eng, p)

        def wait_used(eng, it, kind, c, part=1):
            eng.wait_ge(*at("piece_used", it * PER + (NDP + e_at[kind, c, part] + 1)))

        N_PAR = len(rows) + 11
        OUTS = 8
        block = ctx.enter_context(nc.Block())
        V, SC, PE, GP = nc.vector, nc.scalar, nc.tensor, nc.gpsimd

        @block.sync
        def _(sp):
            for i, (src, k, w) in enumerate(dense):
                before = i - SLOTS
                if before in split_at:
                    sp.wait_ge(*at("lo_done", split_at[before] + 2))
                elif before >= 0:
                    sp.wait_ge(*at("chunk_used", before - place["ffn_wd", 0] + 1))
                sp.dma_start(slot_view(i, k, w), src).then_inc(sig(f"slot{i % SLOTS}_loaded"), 16)

            def load_expert(e, it, first):
                for n, (kind, c, part) in enumerate(order_e):
                    if not first or n >= RAW:
                        sp.wait_ge(*at("lo_done", it * PER + (NDP + n - RAW + 1)))
                    elif n < RAW - 1:
                        sp.wait_ge(*at("lo_done", split_at[FREED[n // 2]] + n % 2 + 1))
                    else:
                        sp.wait_ge(*at("out_o_psum", KD))
                    if kind == "d":
                        r0 = c * CHUNK_COLS + part * (CHUNK_COLS // 2)
                        src = A["moe_wd"][0, e, r0:r0 + CHUNK_COLS // 2, :]
                    else:
                        src = A["moe_w" + kind][0, e, part * (D // 2):(part + 1) * (D // 2), c * CHUNK_COLS:(c + 1) * CHUNK_COLS]
                    sp.dma_start(piece_view(raw_piece(n), kind), src.rearrange("(j p) n -> p j n", p=P))\
                      .then_inc(sig(f"raw{n % RAW}_loaded"), 16)

            load_expert(0, 0, True)
            with sp.Fori(1, NE) as e:
                load_expert(e, e, False)
            sp.wait_ge(*at("flag", 1))
            with sp.If(sp.value_load(count_i[0:1, 0:1], min_val=0, max_val=T) > CAP):
                with sp.Fori(1, PASSES) as p:
                    with sp.Fori(0, NE) as e:
                        load_expert(e, p * NE + e, False)
            sp.wait_ge(*at("y_ready", 1))
            sp.dma_start(O["y_prompt"][0].rearrange("(t p) d -> p t d", p=P), acc[:, 0:TT, :]).then_inc(sig("y_written"), 16)
            sp.dma_start(O["y_sample"].rearrange("b t d -> (b t) d"), acc[0:TS, TT, :]).then_inc(sig("y_written"), 16)
            sp.wait_ge(*at("y_written", 32))

        @block.gpsimd
        def _(gp):
            GP.memset(ident[:], 0.0)
            GP.memset(ones[:], 1.0)
            GP.memset(halves[:], 0.0)
            GP.memset(half2[:], 0.0)
            GP.memset(le_mask[:], 1.0)
            GP.memset(lt_mask[:], 1.0)
            GP.memset(gt_mask[:], 1.0)
            GP.memset(sm1[:], 0.0)
            GP.memset(causal[:], 0.0)
            GP.memset(eps_t[:], EPS)
            GP.memset(lru_w, 0.0).then_inc(sig("gp_filled"), 1)
            gp.wait_ge(*at("gp_filled", 1))
            GP.affine_select(out=ident[:], in_=ident[:], compare_op=ALU.not_equal, fill=1.0, base=0,
                             pattern=[[-1, P]], channel_multiplier=1)
            for m, base in ((le_mask, 0), (lt_mask, -1)):
                GP.affine_select(out=m[:], in_=m[:], compare_op=ALU.is_ge, fill=0.0, base=base,
                                 pattern=[[1, P]], channel_multiplier=-1)
            GP.affine_select(out=gt_mask[:], in_=gt_mask[:], compare_op=ALU.is_ge, fill=0.0, base=-1,
                             pattern=[[-1, P]], channel_multiplier=1)
            for c in (0, 2):
                last = GP.affine_select(out=causal[:, c * P:(c + 1) * P], in_=causal[:, c * P:(c + 1) * P],
                                        compare_op=ALU.is_ge, fill=MASKED, base=0, pattern=[[-1, P]], channel_multiplier=1)
            last.then_inc(sig("gp_filled"), 1)
            gp.wait_ge(*at("gp_filled", 2))
            for k in range(2):
                GP.memset(halves[k * DH:(k + 1) * DH, k * DH:(k + 1) * DH], 1.0)
                GP.memset(half2[k * DH:(k + 1) * DH, k:k + 1], 1.0).then_inc(sig("constants"), 1)
            for g, name in enumerate(("lru_wx", "lru_wa")):
                w = A[name][0].rearrange("(t k) c d -> k c t d", k=2)
                for k in range(2):
                    gp.dma_start(lru_w[k * DH:(k + 1) * DH, g, :, k * DH:(k + 1) * DH], w[k])\
                      .then_inc(sig("lru_w_loaded"), 16)
            gp.dma_start(pg_sb[:], A["page_table"].rearrange("(o b) g -> o (b g)", o=1)).then_inc(sig("pages_loaded"), 16)
            gp.wait_ge(*at("pages_loaded", 16))
            gp.wait_ge(*at("lru_done", 1))
            for n in range(2 * TS):
                b, src = n % TS, A["cache_k" if n < TS else "cache_v"]
                if n >= 4:
                    if n - 4 < TS:
                        gp.wait_ge(*at("k_pages_used", n - 3))
                    else:
                        gp.wait_ge(*at("v_pages_used", n - 3 - TS))
                for g in range(NP_):
                    r = gp.value_load(pg_sb[0:1, b * NP_ + g:b * NP_ + g + 1], min_val=0, max_val=NPOOL - 1)
                    gp.dma_start(pages_kv[:, n % 4, g, :], src[0, r].rearrange("t h e -> t (h e)"))\
                      .then_inc(sig(f"kv{n % 4}_loaded"), 16)

            gp.wait_ge(*at("tail_written", 32))
            GP.memset(lvl, 0.0).then_inc(sig("gp_filled"), 1)
            gp.wait_ge(*at("gp_filled", 3))
            for n in range(LEVELS):
                s = 1 << n
                last = GP.memset(lvl[:, n, :].rearrange("p (k c) -> p k c", c=2 * s)[:, :, 0:s], 1.0)
            last.then_inc(sig("gp_filled"), 1)
            for k in range(2):
                gp.wait_ge(*at("gp_filled", 4 + k))
                for n in range(LEVELS):
                    s = 1 << n
                    m = lvl[:, n, :].rearrange("p (k c) -> p k c", c=2 * s)[:, :, 0:s]
                    base, cm = ((-s, 1), (2 * s - 1, -1))[k]
                    last = GP.affine_select(out=m, in_=m, compare_op=ALU.is_ge, fill=0.0, base=base,
                                            pattern=[[-cm * 2 * s, P // (2 * s)], [0, s]], channel_multiplier=cm)
                last.then_inc(sig("gp_filled" if k == 0 else "levels"), 1)
            gp.wait_ge(*at("d_done", 2 * NGROUPS))
            for h in range(HC):
                if h >= 4:
                    gp.wait_ge(*at(f"state{h % 4}_written", 16))
                gp.dma_start(s_ring[h % 4], A["state_delta_s"][0, :, h].rearrange("b d e -> d b e"))\
                  .then_inc(sig(f"state{h % 4}_loaded"), 16)

        def softplus(dve, link, out, z, tmp, abs_sig, exp_sig, sign):
            t, s, s2 = tmp
            V.tensor_scalar(out, z, sign, 0.0, ALU.mult, ALU.max)
            link(V.tensor_scalar(s, z, -1.0, None, ALU.mult))
            V.tensor_tensor(t, s, z, ALU.min).then_inc(sig(abs_sig), 1)
            dve.wait_ge(*at(exp_sig, 1))
            link(V.tensor_scalar(s, t, 2.0, None, ALU.add))
            link(V.reciprocal(s, s))
            link(V.tensor_tensor(s, s, t, ALU.mult))
            link(V.tensor_tensor(s2, s, s, ALU.mult))
            link(V.tensor_scalar(t, s2, 1.0 / 17, 1.0 / 15, ALU.mult, ALU.add))
            for k in (13, 11, 9, 7, 5, 3, 1):
                link(V.tensor_tensor(t, t, s2, ALU.mult))
                link(V.tensor_scalar(t, t, 1.0 / k, None, ALU.add))
            link(V.tensor_tensor(t, t, s, ALU.mult))
            link(V.scalar_tensor_tensor(out, t, 2.0, out, ALU.mult, ALU.add))

        def conv(dve, link, out, x, tap, bias, past, tiles, E, done):
            for t in tiles:
                last = E.tensor_scalar(out[:, t, :], x(t), tap(t, HIST), bias(t), ALU.mult, ALU.add)
            link(last)
            for j in range(HIST - 1, -1, -1):
                back = HIST - j
                for t in tiles:
                    E.scalar_tensor_tensor(out[:, t, back:TP], x(t)[:, 0:TP - back], tap(t, j), out[:, t, back:TP],
                                           ALU.mult, ALU.add)
                    last = E.scalar_tensor_tensor(out[:, t, TP:T], past(t, j), tap(t, j), out[:, t, TP:T], ALU.mult, ALU.add)
                if j:
                    link(last)
            last.then_inc(sig(done), 1)

        def norm_act_squares(eng, n, dep):
            eng.wait_ge(*at(*dep))
            SC.activation(inv[:], xT[:], ACT.Square).then_inc(sig(f"norm{n}_sq"), 1)

        def norm_act_root(eng, n):
            eng.wait_ge(*at(f"norm{n}_ss", 1))
            SC.activation(inv[:, 0, :], bank[4][:, 0:T], ACT.Sqrt, bias=eps_t[:], scale=1.0 / D)\
              .then_inc(sig(f"norm{n}_root"), 1)

        def norm_pe(pe, n):
            pe.wait_ge(*at(f"norm{n}_sq", 1))
            for j in range(KD):
                last = PE.matmul(bank[4][:, 0:T], ones[:], inv[:, j, :], start=j == 0, stop=j == KD - 1)
            last.then_inc(sig(f"norm{n}_ss"), 1)

        def norm_dve(dve, n, gain, link):
            dve.wait_ge(*at(f"norm{n}_root", 1))
            link(V.reciprocal(inv[:, 1, :], inv[:, 0, :]))
            for j in range(KD):
                last = V.scalar_tensor_tensor(hT[:, j, :], xT[:, j, :], col(gain, j), inv[:, 1, :], ALU.mult, ALU.mult)
                if n < 3 and j % HALF == HALF - 1:
                    last.then_inc(sig(f"norm{n}_h"), 1)
            if n < 3:
                low_parts(dve, hT, f"norm{n}_hi", f"norm{n}_done")
            else:
                last.then_inc(sig(f"norm{n}_done"), 1)

        HALF = KD // 2

        def high_parts(act_e, src, ready, done, halves=(0, 1)):
            for k, r in enumerate(halves):
                act_e.wait_ge(*at(ready, k + 1))
                SC.activation(h_hi[:, r * HALF:(r + 1) * HALF, :], src[:, r * HALF:(r + 1) * HALF, :], ACT.Copy).then_inc(sig(done), 1)

        def low_parts(dve, src, ready, done, halves=(0, 1)):
            for k, r in enumerate(halves):
                part = slice(r * HALF, (r + 1) * HALF)
                dve.wait_ge(*at(ready, k + 1))
                V.tensor_tensor(h_lo[:, part, :], src[:, part, :], h_hi[:, part, :].bitcast(F32), ALU.subtract).then_inc(sig(done), 1)

        def dense_chunk(pe, name, n, tiles, bank_of, out_sig, before):
            i = place[name, n]
            k, w = dense[i][1:]
            half = k // 2
            for part in range(2):
                p = split_at[i] + part
                pe.wait_ge(*at("lo_done", p + 1))
                hi, lo = (t[:, p % SPLIT, 0:half * w].rearrange("p (j n) -> p j n", j=half) for t in (whi, wlo))
                for c, m in enumerate(tiles):
                    out = bank[bank_of(m)][:, 0:T]
                    if part == 0:
                        before(m)
                    cols_ = slice(c * P, (c + 1) * P)
                    for jj in range(half):
                        j = part * half + jj
                        PE.matmul(out, lo[:, jj, cols_], h_hi[:, j, :], start=j == 0, stop=False)
                        PE.matmul(out, hi[:, jj, cols_], h_lo[:, j, :], start=False, stop=False)
                        last = PE.matmul(out, hi[:, jj, cols_], h_hi[:, j, :], start=False, stop=j == k - 1)
                    if part == 1:
                        last.then_inc(sig(out_sig), 1)
                if part == 0:
                    last.then_inc(sig("piece_used"), 1)
                else:
                    PE.drain().then_inc(sig("piece_used"), 1)

        def dense_pe(pe, name, tiles, out_sig, free_sig, before=()):
            def wait_bank(m):
                for first, event, count in before:
                    if m == first:
                        pe.wait_ge(*at(event, count))
                if m >= 8:
                    pe.wait_ge(*at(free_sig, m - 7))
            per = CHUNK_COLS // P
            for n in range(-(-tiles // per)):
                dense_chunk(pe, name, n, range(n * per, min(tiles, (n + 1) * per)), lambda m: m % 8, out_sig, wait_bank)

        def used(pe):
            PE.drain().then_inc(sig("chunk_used"), 1)

        @block.scalar
        def _(act_e):
            q = act_e
            q.dma_start(x_tok[:, 0:TT, :], A["x_prompt"][0].rearrange("(t p) d -> p t d", p=P)).then_inc(sig("x_loaded"), 16)
            q.dma_start(x_tok[0:TS, TT, :], A["x_sample"].rearrange("b t d -> (b t) d")).then_inc(sig("x_loaded"), 16)
            q.dma_start(w_ba[:], A["w_in_o"][0][:, QKV + D:QKV + D + 2 * HC].rearrange("(j p) n -> p j n", p=P)).then_inc(sig("small_w"), 16)
            q.dma_start(w_router[:], A["router_w"][0].rearrange("(j p) n -> p j n", p=P)).then_inc(sig("small_w"), 16)
            q.dma_start(alog_b[:], A["a_log"].broadcast_to([P, HC])).then_inc(sig("small_w"), 16)
            q.dma_start(dt_b[:], A["dt_bias"].broadcast_to([P, HC])).then_inc(sig("small_w"), 16)
            n_par = 0
            for r0, n, ap in rows.values():
                flat = ap
                while len(flat.shape) > 1:
                    d = len(flat.shape)
                    flat = flat.rearrange({2: "a b -> (a b)", 3: "a b c -> (a b c)"}[d])
                q.dma_start(par_rows[r0:r0 + n, :], flat.rearrange("(r p) -> r p", p=P)).then_inc(sig("par_loaded"), 16)
                n_par += 1
            for r, a, b in ((r_gq, "qk_gain_q", "qk_gain_q"), (r_gk, "qk_gain_k", "qk_gain_k"),
                            (r_lq, "lam_q1", "lam_q2"), (r_lk, "lam_k1", "lam_k2")):
                q.dma_start(par_rows[r:r + 1, 0:DH], A[a]).then_inc(sig("par_loaded"), 16)
                q.dma_start(par_rows[r:r + 1, DH:P], A[b]).then_inc(sig("par_loaded"), 16)
                n_par += 2
            q.dma_start(cd_rows[0:N_CD, :], A["conv_delta_w"][0].rearrange("j (t p) -> (j t) p", p=P)).then_inc(sig("par_loaded"), 16)
            q.dma_start(hist_rows, A["state_lru_conv"][0].rearrange("b j c -> (b j) c")).then_inc(sig("par_loaded"), 16)
            q.dma_start(h0_rows, A["state_lru_h"][0]).then_inc(sig("par_loaded"), 16)
            assert n_par == N_PAR - 3

            for j in range(KD):
                act_e.wait_ge(*at("xT_psum", j + 1))
                SC.activation(xT[:, j, :], bank[j % 4][:, 0:T], ACT.Copy).then_inc(sig("xT_done"), 1)
            norm_act_squares(act_e, 0, ("xT_done", KD))
            dense_hi(act_e, 0)
            dense_hi(act_e, 1)
            act_e.wait_ge(*at("lam_abs", 1))
            SC.activation(v_s[0], v_s[0], ACT.Exp).then_inc(sig("lam_absexp"), 1)
            norm_act_root(act_e, 0)
            high_parts(act_e, hT, "norm0_h", "norm0_hi")
            dense_hi(act_e, 2)
            for m in range(IN_E // P):
                if m % 4 == 0:
                    behind(dense_hi, act_e, "w_in_e", m // 4, 0)
                act_e.wait_ge(*at("proj_psum", m + 1))
                SC.activation(proj[:, m, :], bank[m % 8][:, 0:T], ACT.Copy).then_inc(sig("proj_done"), 1)
                if m % 4 == 3:
                    behind(dense_hi, act_e, "w_in_e", m // 4, 1)
            for g, (dst, bias) in enumerate(((gate_x, "lru_bx"), (gate_a, "lru_ba"))):
                for t in range(NL):
                    act_e.wait_ge(*at("lru_gate_psum", g * NL + t + 1))
                    SC.activation(dst[:, t, :], bank[g * NL + t][:, 0:T], ACT.Sigmoid, bias=col(bias, t))\
                      .then_inc(sig("lru_gates"), 1)
            act_e.wait_ge(*at("lru_y", 1))
            SC.activation(decay_a, gate_a, ACT.Exp, scale=-1.0).then_inc(sig("lru_a"), 1)
            SC.activation(tanh_y, gate_a, ACT.Tanh).then_inc(sig("lru_a"), 1)
            SC.activation(proj[:, GATE:GATE + NL, :], proj[:, GATE:GATE + NL, :], ACT.Gelu_apprx_tanh).then_inc(sig("gelu"), 1)
            act_e.wait_ge(*at("lru_m", 1))
            SC.activation(tanh_y, tanh_y, ACT.Sqrt).then_inc(sig("lru_root"), 1)
            high_parts(act_e, mixT, "lru_done", "ya_hi", halves=(0,))
            SC.activation(inv[:], proj[:, Q_:Q_ + 2 * HB, :], ACT.Square).then_inc(sig("qk_sq"), 1)
            for i in range(2 * HB):
                act_e.wait_ge(*at("qk_ss", i + 1))
                SC.activation(inv[:, i, :], bank[i % 4][:, 0:T], ACT.Sqrt, bias=eps_t[:], scale=1.0 / DH)\
                  .then_inc(sig("qk_root"), 1)
            act_e.wait_ge(*at("lam_psum", 1))
            SC.activation(lam_e, bank[4][:, 0:2], ACT.Exp).then_inc(sig("lam_exp"), 1)
            for i, (s0, n) in enumerate(TOK):
                act_e.wait_ge(*at("ktok_psum", i + 1))
                SC.activation(ktok[0:n, i, :], bank[i][0:n, :], ACT.Copy).then_inc(sig("ktok"), 1)
            for i, (s0, n) in enumerate(TOK):
                act_e.wait_ge(*at("vtok_psum", i + 1))
                SC.activation(vtok[0:n, i, :], bank[3 + i][0:n, :], ACT.Copy).then_inc(sig("vtok"), 1)
            act_e.wait_ge(*at("qs_psum", 1))
            SC.activation(qs_tok, bank[6][0:TS, :], ACT.Copy).then_inc(sig("qs_tok"), 1)
            act_e.wait_ge(*at("tail_psum", 1))
            SC.activation(tail_tok, bank[7][0:TAIL, 0:LW], ACT.Copy).then_inc(sig("tail_tok"), 1)
            outs = (("ktok", 3, ktok, "k_prompt", "k_sample"), ("vtok", 3, vtok, "v_prompt", "v_sample"))
            for s, k, src, a, b in outs:
                act_e.wait_ge(*at(s, k))
                q.dma_start(O[a][0, 0].rearrange("(t p) h e -> p t (h e)", p=P), src[:, 0:TT, :]).then_inc(sig("out_written"), 16)
                q.dma_start(O[b][0, :, 0].rearrange("b h e -> b (h e)"), src[0:TS, TT, :]).then_inc(sig("out_written"), 16)
            act_e.wait_ge(*at("tail_tok", 1))
            q.dma_start(O["lru_conv_prompt"][0, 0], tail_tok[0:HIST, :]).then_inc(sig("out_written"), 16)
            q.dma_start(O["lru_conv_sample"][0, :, HIST - 1, :], tail_tok[HIST:TAIL, :]).then_inc(sig("out_written"), 16)
            q.dma_start(O["lru_conv_sample"][0, :, 0:HIST - 1, :], A["state_lru_conv"][0, :, 1:HIST, :]).then_inc(sig("out_written"), 16)
            act_e.wait_ge(*at("hlast", 1))
            q.dma_start(O["lru_h_prompt"], hl_tok[0:1, :]).then_inc(sig("h_written"), 16)
            q.dma_start(O["lru_h_sample"][0], hl_tok[1:1 + TS, :]).then_inc(sig("h_written"), 16)
            act_e.wait_ge(*at("ss_psum", 1))
            for i in range(2):
                SC.activation(ss[:, i, 0:NP_ * P], bank[4][0:NB, i * NP_ * P:(i + 1) * NP_ * P], ACT.Copy, scale=DH ** -0.5)
            act_e.wait_ge(*at("self_psum", 1))
            SC.activation(ss[:, :, NP_ * P], bank[5][0:NB, 0:2], ACT.Copy, scale=DH ** -0.5).then_inc(sig("ss"), 1)
            act_e.wait_ge(*at("neg_max_s", 1))
            for i in range(2):
                SC.activation(ss[:, i, :], ss[:, i, :], ACT.Exp, bias=mx_s[0:NB, i:i + 1],
                              accum_out=ssum_s[0:NB, i:i + 1]).then_inc(sig("exps_s"), 1)
            for i in range(HH):
                for s, (c0, c1) in enumerate(((0, P), (P, 3 * P))):
                    act_e.wait_ge(*at("neg_max", 1))
                    SC.activation(sc_p[:, i, c0:c1], sc_p[:, i, c0:c1], ACT.Exp, bias=mx[:, s * HH + i:s * HH + i + 1],
                                  accum_out=ssum[:, s * HH + i:s * HH + i + 1]).then_inc(sig("exps"), 1)
            for h in range(HB):
                act_e.wait_ge(*at("pT_psum", h + 1))
                if h >= 2:
                    act_e.wait_ge(*at("pv_psum", h - 1))
                SC.activation(pT[h % 2], bank[h % 2][:, 0:3 * P], ACT.Copy).then_inc(sig("pT"), 1)
                act_e.wait_ge(*at("pv_psum", h + 1))
                SC.activation(mixT[:, NL + h, 0:TP], bank[2 + h % 2][:, 0:TP], ACT.Copy).then_inc(sig("o_prompt"), 1)
            act_e.wait_ge(*at("o_sample", 1))
            act_e.wait_ge(*at("o_prompt", HB))
            SC.activation(osq, mixT[:, NL:NL + HB, :], ACT.Square).then_inc(sig("o_sq"), 1)
            for h in range(HB):
                act_e.wait_ge(*at("o_ss", h + 1))
                SC.activation(osq[:, h, :], bank[4 + h][:, 0:T], ACT.Sqrt, bias=eps_t[:], scale=1.0 / E2)\
                  .then_inc(sig("o_root"), 1)
            high_parts(act_e, mixT, "mix_done", "mix_hi", halves=(1,))
            for n in range(D // CHUNK_COLS):
                for part in range(2):
                    behind(dense_hi, act_e, "w_out_e", n, part)
            norm_act_squares(act_e, 1, ("out_e_added", KD))
            norm_act_root(act_e, 1)
            high_parts(act_e, hT, "norm1_h", "norm1_hi")
            for m in range(NF):
                if m % 4 == 0:
                    behind(dense_hi, act_e, "ffn_wg", m // 4, 0, FFN_END)
                act_e.wait_ge(*at("ffn_g", m + 1))
                if m >= 4:
                    act_e.wait_ge(*at("ffn_act", m - 3))
                SC.activation(sil[:, m % 4, :], bank[m % 4][:, 0:T], ACT.Silu).then_inc(sig("ffn_sil"), 1)
                if m % 4 == 3 or m == NF - 1:
                    behind(dense_hi, act_e, "ffn_wg", m // 4, 1, FFN_END)
                    behind(dense_hi, act_e, "ffn_wu", m // 4, 0, FFN_END)
                    behind(dense_hi, act_e, "ffn_wu", m // 4, 1, FFN_END)

            act_e.wait_ge(*at("ffn_act", NF))
            act_e.wait_ge(*at("out_written", 16 * 7))
            q.dma_start(dhist_rows, A["state_delta_conv"][0].rearrange("b j c -> (b j) c")).then_inc(sig("dhist_loaded"), 16)
            norm_act_squares(act_e, 2, ("ffn_added", KD))
            dense_hi(act_e, FFN_END)
            dense_hi(act_e, FFN_END + 1)
            norm_act_root(act_e, 2)
            high_parts(act_e, hT, "norm2_h", "norm2_hi")
            dense_hi(act_e, FFN_END + 2)
            act_e.wait_ge(*at("ba_read", 1))
            SC.activation(beta, ba[:, :, 0:HC], ACT.Sigmoid).then_inc(sig("beta"), 1)
            act_e.wait_ge(*at("g_abs", 1))
            SC.activation(sp_t[0], sp_t[0], ACT.Exp).then_inc(sig("g_absexp"), 1)
            SC.activation(alog_b[:], alog_b[:], ACT.Exp).then_inc(sig("ealog"), 1)
            def silu_qkv(m):
                act_e.wait_ge(*at("dconv", m + 1))
                SC.activation(qkvT[:, m, :], qkvT[:, m, :], ACT.Silu).then_inc(sig("qkv"), 1)

            for m in range(NQ):
                if m % 4 == 0:
                    behind(dense_hi, act_e, "w_in_o", m // 4, 0)
                act_e.wait_ge(*at("qkvz_psum", m + 1))
                if m >= 4:
                    act_e.wait_ge(*at("dconv", m - 3))
                SC.activation(pre[:, m % 4, :], bank[m % 8][:, 0:T], ACT.Copy).then_inc(sig("pre"), 1)
                SC.activation(tailT[:, m, :], bank[m % 8][:, T - TAIL:T], ACT.Copy).then_inc(sig("qkvz_read"), 1)
                if m % 4 == 3:
                    behind(dense_hi, act_e, "w_in_o", m // 4, 1)
                if m >= 2:
                    silu_qkv(m - 2)
            silu_qkv(NQ - 2)
            silu_qkv(NQ - 1)
            for m in range(NQ, NQ + HC):
                if m % 4 == 0:
                    behind(dense_hi, act_e, "w_in_o", m // 4, 0)
                act_e.wait_ge(*at("qkvz_psum", m + 1))
                SC.activation(zT[:, m - NQ, :], bank[m % 8][:, 0:T], ACT.Silu).then_inc(sig("qkvz_read"), 1)
                if m % 4 == 3:
                    behind(dense_hi, act_e, "w_in_o", m // 4, 1)
            for n in range(QKV // CHUNK_COLS):
                act_e.wait_ge(*at("dtail_psum", n + 1))
                SC.activation(tail_rows[:, n * CHUNK_COLS:(n + 1) * CHUNK_COLS], bank[5 + n % 3][0:TAIL, :], ACT.Copy)\
                  .then_inc(sig("dtail"), 1)
            act_e.wait_ge(*at("dtail", QKV // CHUNK_COLS))
            q.dma_start(O["delta_conv_prompt"][0, 0], tail_rows[0:HIST, :]).then_inc(sig("tail_written"), 16)
            q.dma_start(O["delta_conv_sample"][0, :, HIST - 1, :], tail_rows[HIST:TAIL, :]).then_inc(sig("tail_written"), 16)
            q.dma_start(O["delta_conv_sample"][0, :, 0:HIST - 1, :], A["state_delta_conv"][0, :, 1:HIST, :]).then_inc(sig("out_written"), 16)
            for r in range(2):
                if r:
                    act_e.wait_ge(*at("l2_used", 1))
                act_e.wait_ge(*at("qkv", NQ))
                SC.activation(inv, qkvT[:, r * HC:(r + 1) * HC, :], ACT.Square).then_inc(sig("l2_sq"), 1)
            act_e.wait_ge(*at("l2_ss", 1))
            SC.activation(inv[0:2 * HC, 0, :], bank[4][0:2 * HC, 0:T], ACT.Sqrt, bias=eps_t[0:2 * HC, :]).then_inc(sig("l2_root"), 1)
            act_e.wait_ge(*at("Gt", 1))
            SC.activation(eG, Gt, ACT.Exp).then_inc(sig("eG"), 1)
            for n in range(NGROUPS):
                c, h0_ = divmod(n * NG, HC)
                act_e.wait_ge(*at("d_in", n + 1))
                SC.activation(Gb, bank[0][:, :].rearrange("p (h t) -> p h t", h=NG), ACT.Copy).then_inc(sig("d_gb"), 1)
                act_e.wait_ge(*at("d_diff", n + 1))
                SC.activation(EA, EA, ACT.Exp, scale=-1.0)
                SC.activation(QK, QK, ACT.Exp)
                if c:
                    act_e.wait_ge(*at("d_gb", n + 1))
                    SC.activation(ge[:, 0:NG], Gb[:, :, P - 1], ACT.Exp)
                    SC.activation(QD, Gb, ACT.Exp)
                SC.activation(kd_s[:, 0:NG], kd_s[:, 0:NG], ACT.Exp).then_inc(sig("d_exp"), 1)
                for l in range(1, LEVELS):
                    k = n * (LEVELS - 1) + l
                    act_e.wait_ge(*at("d_Y", k))
                    SC.activation(Yb, bank[6][:, :].rearrange("p (h t) -> p h t", h=NG), ACT.Copy).then_inc(sig("d_Yc"), 1)
                if c:
                    act_e.wait_ge(*at("d_w", n - NGROUPS // TT + 1))
                    SC.activation(NW, bank[1][:, :].rearrange("p (h t) -> p h t", h=NG), ACT.Copy, scale=-1.0).then_inc(sig("d_nw"), 1)
                act_e.wait_ge(*at("d_v", n + 1))
                SC.activation(VN, bank[2][:, :].rearrange("p (h t) -> p h t", h=NG), ACT.Copy).then_inc(sig("d_vn"), 1)
                act_e.wait_ge(*at("d_o", n + 1))
                SC.activation(oT[:, h0_:h0_ + NG, c * P:(c + 1) * P], bank[3][:, :].rearrange("p (h t) -> p h t", h=NG), ACT.Copy)\
                  .then_inc(sig("d_done"), 1)
            act_e.wait_ge(*at("d_done", 2 * NGROUPS))
            q.dma_start(O["delta_s_prompt"][0, 0].rearrange("h d e -> d h e"), S_pr).then_inc(sig("sp_written"), 16)
            act_e.wait_ge(*at("s_gb", 1))
            SC.activation(egb[:, 0], bank[0][:, 0:HC * TS].rearrange("p (h b) -> p h b", h=HC), ACT.Exp)
            SC.activation(egb[:, 1], bank[0][:, HC * TS:2 * HC * TS].rearrange("p (h b) -> p h b", h=HC), ACT.Copy).then_inc(sig("s_egb"), 1)
            act_e.wait_ge(*at("s_qk", 1))
            SC.activation(qks, bank[1][:, 0:HC * TS].rearrange("p (h b) -> p h b", h=HC), ACT.Copy).then_inc(sig("s_qks"), 1)
            for h in range(HC):
                act_e.wait_ge(*at("s_state", h + 1))
                q.dma_start(O["delta_s_sample"][0, :, h].rearrange("b d e -> d b e"), s_ring[h % 4]).then_inc(sig(f"state{h % 4}_written"), 16)
            act_e.wait_ge(*at("s_o", HC))
            SC.activation(inv, oT[:], ACT.Square).then_inc(sig("on_sq"), 1)
            act_e.wait_ge(*at("on_ss", 1))
            SC.activation(inv[0:HC, 0, :], bank[4][0:HC, 0:T], ACT.Sqrt, bias=eps_t[0:HC, :], scale=1.0 / DV).then_inc(sig("on_root"), 1)
            high_parts(act_e, oT, "on_done", "on_hi")
            for k in range(4):
                act_e.wait_ge(*at(f"state{k}_written", 32))
            act_e.wait_ge(*at("sp_written", 16))
            act_e.wait_ge(*at("tail_written", 32))
            for n in range(D // CHUNK_COLS):
                for part in range(2):
                    behind(dense_hi, act_e, "w_out_o", n, part)
            norm_act_squares(act_e, 3, ("out_o_added", KD))
            norm_act_root(act_e, 3)
            act_e.wait_ge(*at("top_diff", 1))
            SC.activation(gates[:, 0:TT, 1:2], gates[:, 0:TT, 1:2], ACT.Exp)
            SC.activation(gates[0:TS, TT, 1:2], gates[0:TS, TT, 1:2], ACT.Exp).then_inc(sig("gate_exp"), 1)
            for s, dst in (("xtok", acc), ("htok", h_tok)):
                for i, (t0, n) in enumerate(TOK):
                    for k in range(YC):
                        act_e.wait_ge(*at(s + "_psum", i * YC + k + 1))
                        SC.activation(dst[0:n, i, k * CHUNK_COLS:(k + 1) * CHUNK_COLS],
                                      bank[(i * YC + k) % 4][0:n, :], ACT.Copy).then_inc(sig(s), 1)
            SC.activation(spare[:, 1:2], eps_t[:], ACT.Copy).then_inc(sig("y0_out"), 1)

            def dispatch_out(it):
                for r in range(2):
                    act_e.wait_ge(*at("moe_disp", it * 2 + r + 1))
                    n = KD // 2
                    SC.activation(hte_h[:, r * n:(r + 1) * n, :], bank[(7, 3)[r]][:, :].rearrange("p (j t) -> p j t", j=n), ACT.Copy)\
                      .then_inc(sig("hte_hi"), 1)

            def tr_out(it, c):
                act_e.wait_ge(*at("moe_tr", it * NSTEP + c + 1))
                SC.activation(act_h[:, c % 2], bank[4][:, :].rearrange("p (k t) -> p k t", k=KF), ACT.Copy).then_inc(sig("tr_hi"), 1)

            def act_expert(it, more):
                for n, (kind, c, part) in enumerate(order_e):
                    if kind == "g" and part:
                        wait_used(act_e, it, "g", c)
                        SC.activation(m_sil[:, c % 2, :], bank[c % 2 * 2][:, :], ACT.Silu).then_inc(sig("sil"), 1)
                        if c == 0:
                            act_e.wait_ge(*at("moe_w", it + 1))
                            SC.activation(WT, bank[4][:, 0:T], ACT.Copy).then_inc(sig("wt_out"), 1)
                        else:
                            tr_out(it, c - 1)
                    if n == PER - 3:
                        if more:
                            dispatch_out(it + 1)
                        tr_out(it, NSTEP - 1)
                    if n == PER - 1:
                        wait_used(act_e, it, "d", NSTEP - 1)
                        SC.activation(y_e[:, 0:CHUNK_COLS], bank[5][:, :], ACT.Copy).then_inc(sig("y0_out"), 1)
                    if more or n + SPLIT < PER:
                        take_hi(act_e, it, n + SPLIT)

            dispatch_out(0)
            with act_e.Fori(0, NE - 1) as e:
                act_expert(e, True)
            act_expert(NE - 1, False)
            with act_e.If(act_e.value_load(count_i[0:1, 0:1], min_val=0, max_val=T) > CAP):
                with act_e.Fori(1, PASSES) as p:
                    with act_e.Fori(0, NE) as e:
                        for n in range(SPLIT):
                            take_hi(act_e, p * NE + e, n)
                        dispatch_out(p * NE + e)
                        act_expert(p * NE + e, False)
            act_e.wait_ge(*at("out_written", OUTS * 16))
            act_e.wait_ge(*at("h_written", 32))

        @block.vector
        def _(dve):
            chain = [0]

            def link(ins):
                chain[0] += 1
                ins.then_inc(sig("dve_chain"), 1)
                dve.wait_ge(*at("dve_chain", chain[0]))

            dve.wait_ge(*at("constants", 2))
            V.memset(pick[:, 2 * HC - 1:2 * HC], 1.0)
            dve.wait_ge(*at("par_psum", 1))
            V.tensor_copy(par[:, 0:N_ROWS], bank[4][:, 0:N_ROWS])
            V.tensor_copy(cd[:, 0:N_CD], bank[4][:, P:P + N_CD])
            V.tensor_copy(hist, bank[4][:, 2 * P:2 * P + NL * TS * HIST].rearrange("p (a b c) -> p a b c", a=NL, b=TS))
            link(V.tensor_copy(h0, bank[4][:, 3 * P:3 * P + NL * TS].rearrange("p (a b) -> p a b", a=NL)))
            V.tensor_tensor(lamv, par[:, r_lq:r_lq + 1], par[:, r_lk:r_lk + 1], ALU.mult).then_inc(sig("par_done"), 1)
            softplus(dve, link, sp8, par[:, rows["lru_lambda"][0]:rows["lru_lambda"][0] + NL], v_s, "lam_abs", "lam_absexp", -1.0)
            link(V.tensor_scalar(sp8, sp8, RG_C, None, ALU.mult))
            V.tensor_scalar(subg, col("subln_g"), 1.0 - LAM_INIT, None, ALU.mult)
            dense_lo(dve, 0)
            dense_lo(dve, 1)
            norm_dve(dve, 0, "ln_mix_e", link)
            dense_lo(dve, 2)
            for n in range(3):
                for part in range(2):
                    behind(dense_lo, dve, "w_in_e", n, part)

            dve.wait_ge(*at("proj_done", XR + NL))
            conv(dve, link, xc, lambda t: proj[:, XR + t, :], lambda t, j: col("conv_lru_w", j * NL + t),
                 lambda t: col("conv_lru_b", t), lambda t, j: hist[:, t, :, j], range(NL), V, "xc_done")
            for n in range(3, 5):
                for part in range(2):
                    behind(dense_lo, dve, "w_in_e", n, part)
            dve.wait_ge(*at("lru_gates", 2 * NL))
            for t in range(NL):
                last = V.tensor_scalar(gate_a[:, t, :], gate_a[:, t, :], sp8[:, t:t + 1], None, ALU.mult)
            last.then_inc(sig("lru_y"), 1)
            link(V.tensor_tensor(gate_x, gate_x, xc, ALU.mult))
            dve.wait_ge(*at("lru_a", 2))
            link(V.tensor_scalar(tmp_l, tanh_y, 1.0, None, ALU.add))
            link(V.reciprocal(tmp_l, tmp_l))
            link(V.tensor_scalar(tmp_l, tmp_l, 2.0, None, ALU.mult))
            V.tensor_tensor(tanh_y, tanh_y, tmp_l, ALU.mult).then_inc(sig("lru_m"), 1)
            dve.wait_ge(*at("lru_root", 1))
            link(V.tensor_tensor(gate_x, gate_x, tanh_y, ALU.mult))
            link(V.tensor_tensor(tmp_l[:, :, 0:TS], decay_a[:, :, TP:T], h0, ALU.mult))
            for t in range(NL):
                V.tensor_tensor_scan(xc[:, t, 0:TP], decay_a[:, t, 0:TP], gate_x[:, t, 0:TP], 0.0, ALU.mult, ALU.add)
            link(V.tensor_tensor(xc[:, :, TP:T], gate_x[:, :, TP:T], tmp_l[:, :, 0:TS], ALU.add))
            dve.wait_ge(*at("gelu", 1))
            V.tensor_copy(hl, xc[:, :, TP - 1:T])
            V.tensor_tensor(mixT[:, 0:NL, :], proj[:, GATE:GATE + NL, :], xc, ALU.mult).then_inc(sig("lru_done"), 1)
            dve.wait_ge(*at("qk_root", 2 * HB))
            link(V.reciprocal(inv, inv))
            for i in range(2 * HB):
                g = r_gq if i < HB else r_gk
                last = V.scalar_tensor_tensor(proj[:, Q_ + i, :], proj[:, Q_ + i, :], par[:, g:g + 1], inv[:, i, :],
                                              ALU.mult, ALU.mult)
            last.then_inc(sig("qk_done"), 1)
            low_parts(dve, mixT, "ya_hi", "ya_lo", halves=(0,))
            dve.wait_ge(*at("lam_exp", 1))
            link(V.tensor_tensor(nlam, lam_e[:, 1:2], lam_e[:, 0:1], ALU.subtract))
            link(V.tensor_scalar(nlam, nlam, -LAM_INIT, None, ALU.add))
            dve.wait_ge(*at("hlast_psum", 1))
            V.tensor_copy(hl_tok, bank[7][0:TS + 1, 0:LW]).then_inc(sig("hlast"), 1)

            for b in range(TS):
                dve.wait_ge(*at("qb_psum", b + 1))
                dve.wait_ge(*at(f"kv{b % 4}_loaded", 32 * (b // 4 + 1)))
                if b:
                    dve.wait_ge(*at("k_pages_used", b))
                for g in range(NP_):
                    last = V.tensor_tensor(kv_mul[:, g, :], pages_kv[:, b % 4, g, :], bank[4 + b % 2][:, :], ALU.mult)
                chain[0] += 1
                last.then_inc(sig("dve_chain"), 1)
                dve.wait_ge(*at("dve_chain", chain[0]))
                for g in range(NP_):
                    last = V.reduce_sum(sc_s[:, g, :, :, b].rearrange("p i h -> p h i"),
                                        kv_mul[:, g, :].rearrange("p (h i d) -> p h i d", i=2, d=DH), X)
                last.then_inc(sig("k_pages_used"), 1)
            dve.wait_ge(*at("qk_done", 1))
            V.tensor_tensor(qk_s, proj[:, Q_:Q_ + HB, TP:T], proj[:, K_:K_ + HB, TP:T], ALU.mult).then_inc(sig("qk_self"), 1)
            dve.wait_ge(*at("ss", 1))
            link(V.reduce_max(mx_s[0:NB, :], ss, X))
            V.tensor_scalar(mx_s[0:NB, :], mx_s[0:NB, :], -1.0, None, ALU.mult).then_inc(sig("neg_max_s"), 1)
            dve.wait_ge(*at("exps_s", 2))
            link(V.reciprocal(rsum_s[0:NB, :], ssum_s[0:NB, :]))
            link(V.tensor_tensor(rsum_s[0:NB, 1:2], rsum_s[0:NB, 1:2], nlam[0:NB, :], ALU.mult))
            link(V.tensor_scalar(ss[:, 0, :], ss[:, 0, :], rsum_s[0:NB, 0:1], None, ALU.mult))
            V.scalar_tensor_tensor(ss[:, 0, :], ss[:, 1, :], rsum_s[0:NB, 1:2], ss[:, 0, :], ALU.mult, ALU.add).then_inc(sig("p_s"), 1)
            dve.wait_ge(*at("pT_s_psum", 1))
            V.tensor_copy(pT_s, bank[6][:, 0:NP_ * NB].rearrange("p (g n) -> p g n", g=NP_))
            V.tensor_copy(pself, bank[6][:, NP_ * NB:(NP_ + 1) * NB]).then_inc(sig("pT_s"), 1)
            dve.wait_ge(*at("pT_s", 1))
            link(V.tensor_tensor(pself.rearrange("p (h b) -> p h b", h=HB), pself.rearrange("p (h b) -> p h b", h=HB),
                                 proj[:, V_:V_ + HB, TP:T], ALU.mult))
            dve.wait_ge(*at("v_pages_used", TS))
            V.tensor_tensor(mixT[:, NL:NL + HB, TP:T], pself.rearrange("p (h b) -> p h b", h=HB),
                            bank[7][:, 0:NB].rearrange("p (h b) -> p h b", h=HB), ALU.add).then_inc(sig("o_sample"), 1)

            for i in range(HH):
                dve.wait_ge(*at("scores_psum", i + 1))
                if i == 0:
                    dve.wait_ge(*at("o_sample", 1))
                    dve.wait_ge(*at("h_written", 32))
                last = V.scalar_tensor_tensor(sc_p[:, i, :], bank[i % 4][:, 0:3 * P], DH ** -0.5, causal[:], ALU.mult, ALU.add)
                last.then_inc(sig("scores"), 1)
            dve.wait_ge(*at("scores", HH))
            V.reduce_max(mx[:, 0:HH], sc_p[:, :, 0:P], X)
            link(V.reduce_max(mx[:, HH:2 * HH], sc_p[:, :, P:3 * P], X))
            V.tensor_scalar(mx, mx, -1.0, None, ALU.mult).then_inc(sig("neg_max"), 1)
            dve.wait_ge(*at("exps", 2 * HH))
            link(V.reciprocal(rsum, ssum))
            r4 = rsum.rearrange("p (s h i) -> p s h i", s=2, i=2)
            link(V.tensor_scalar(r4[:, :, :, 1], r4[:, :, :, 1], nlam, None, ALU.mult))
            seg = ((0, P), (P, 3 * P))
            for h in range(HB):
                for s, (c0, c1) in enumerate(seg):
                    r = s * HH + 2 * h
                    last = V.tensor_scalar(sc_p[:, 2 * h, c0:c1], sc_p[:, 2 * h, c0:c1], rsum[:, r:r + 1], None, ALU.mult)
            link(last)
            for h in range(HB):
                for s, (c0, c1) in enumerate(seg):
                    r = s * HH + 2 * h + 1
                    last = V.scalar_tensor_tensor(sc_p[:, 2 * h, c0:c1], sc_p[:, 2 * h + 1, c0:c1], rsum[:, r:r + 1],
                                                  sc_p[:, 2 * h, c0:c1], ALU.mult, ALU.add)
                last.then_inc(sig("probs"), 1)
            dve.wait_ge(*at("o_root", HB))
            link(V.reciprocal(osq, osq))
            for h in range(HB):
                last = V.scalar_tensor_tensor(mixT[:, NL + h, :], mixT[:, NL + h, :], subg, osq[:, h, :], ALU.mult, ALU.mult)
            last.then_inc(sig("mix_done"), 1)
            low_parts(dve, mixT, "mix_hi", "mix_lo", halves=(1,))
            for m in range(KD):
                if m % 4 == 0:
                    behind(dense_lo, dve, "w_out_e", m // 4, 0)
                dve.wait_ge(*at("out_e_psum", m + 1))
                V.tensor_tensor(xT[:, m, :], xT[:, m, :], bank[m % 8][:, 0:T], ALU.add).then_inc(sig("out_e_added"), 1)
                if m % 4 == 3:
                    behind(dense_lo, dve, "w_out_e", m // 4, 1)
            norm_dve(dve, 1, "ln_ffn_e", link)
            for m in range(NF):
                if m % 4 == 0:
                    behind(dense_lo, dve, "ffn_wg", m // 4, 0, FFN_END)
                    behind(dense_lo, dve, "ffn_wg", m // 4, 1, FFN_END)
                    behind(dense_lo, dve, "ffn_wu", m // 4, 0, FFN_END)
                dve.wait_ge(*at("ffn_u", m + 1))
                dve.wait_ge(*at("ffn_sil", m + 1))
                V.tensor_tensor(act[:, m, :], sil[:, m % 4, :], bank[4 + m % 4][:, 0:T], ALU.mult).then_inc(sig("ffn_act"), 1)
                if m % 4 == 3 or m == NF - 1:
                    behind(dense_lo, dve, "ffn_wu", m // 4, 1, FFN_END)
            for m in range(KD):
                dve.wait_ge(*at("ffn_d_psum", m + 1))
                V.tensor_tensor(xT[:, m, :], xT[:, m, :], bank[m % 4][:, 0:T], ALU.add).then_inc(sig("ffn_added"), 1)

            def heads(b, n=NG):
                return bank[b][:, 0:n * P].rearrange("p (h t) -> p h t", h=n)

            dve.wait_ge(*at("dhist_psum", 1))
            half = NQ // 2
            for k in range(2):
                last = V.tensor_copy(dhist[:, k * half:(k + 1) * half],
                                     bank[5 + k][:, 0:half * TS * HIST].rearrange("p (a b c) -> p a b c", a=half, b=TS))
            link(last)
            dense_lo(dve, FFN_END)
            dense_lo(dve, FFN_END + 1)
            norm_dve(dve, 2, "ln_mix_o", link)
            dense_lo(dve, FFN_END + 2)
            dve.wait_ge(*at("ba_psum", 1))
            V.tensor_copy(ba[:, 0:TT, :], bank[7][:, 0:TT * 2 * HC].rearrange("p (t c) -> p t c", t=TT))
            V.tensor_copy(ba[0:TS, TT, :], bank[7][0:TS, TT * 2 * HC:NTT * 2 * HC]).then_inc(sig("ba_read"), 1)
            dve.wait_ge(*at("ba_read", 1))
            dve.wait_ge(*at("small_w", 64))
            dve.wait_ge(*at("beta", 1))
            az = ba[:, :, HC:2 * HC]
            link(V.tensor_tensor(az, az, dt_b[:].unsqueeze(1).broadcast_to([P, NTT, HC]), ALU.add))
            softplus(dve, link, g_t, az, sp_t, "g_abs", "g_absexp", 1.0)
            dve.wait_ge(*at("ealog", 1))
            link(V.scalar_tensor_tensor(g_t, g_t, -1.0, alog_b[:].unsqueeze(1).broadcast_to([P, NTT, HC]), ALU.mult, ALU.mult))
            V.tensor_tensor(gd[0:TS, 0], ident[0:TS, 0:TS].unsqueeze(1).broadcast_to([TS, HC, TS]),
                            g_t[0:TS, TT, :].unsqueeze(2).broadcast_to([TS, HC, TS]), ALU.mult)
            V.tensor_tensor(gd[0:TS, 1], ident[0:TS, 0:TS].unsqueeze(1).broadcast_to([TS, HC, TS]),
                            beta[0:TS, TT, :].unsqueeze(2).broadcast_to([TS, HC, TS]), ALU.mult).then_inc(sig("g"), 1)
            for m in range(NQ):
                if m % 2 == 0:
                    behind(dense_lo, dve, "w_in_o", m // 4, m % 4 // 2)
                dve.wait_ge(*at("pre", m + 1))
                x, o = pre[:, m % 4, :], qkvT[:, m, :]
                tap = [cd[:, j * NQ + m:j * NQ + m + 1] for j in range(CW)]
                link(V.tensor_scalar(o, x, tap[HIST], None, ALU.mult))
                for j in range(HIST - 1, -1, -1):
                    back = HIST - j
                    V.scalar_tensor_tensor(o[:, back:TP], x[:, 0:TP - back], tap[j], o[:, back:TP], ALU.mult, ALU.add)
                    last = V.scalar_tensor_tensor(o[:, TP:T], dhist[:, m, :, j], tap[j], o[:, TP:T], ALU.mult, ALU.add)
                    if j:
                        link(last)
                last.then_inc(sig("dconv"), 1)
            for n in range(NQ * P // CHUNK_COLS, (QKV + D) // CHUNK_COLS):
                for part in range(2):
                    behind(dense_lo, dve, "w_in_o", n, part)
            dve.wait_ge(*at("Gt_psum", 1))
            V.tensor_copy(Gt, bank[7][:, 0:TT * HC].rearrange("p (c h) -> p c h", c=TT)).then_inc(sig("Gt"), 1)
            dve.wait_ge(*at("eG", 1))
            link(V.tensor_tensor(bkb, beta[:, 0:TT, :], eG, ALU.mult))
            dve.wait_ge(*at("l2_root", 1))
            V.reciprocal(inv[0:2 * HC, 0, :], inv[0:2 * HC, 0, :]).then_inc(sig("l2_inv"), 1)
            for i in range(2 * HC):
                dve.wait_ge(*at("l2_b", i + 1))
                V.scalar_tensor_tensor(qkvT[:, i, :], qkvT[:, i, :], DK ** -0.5 if i < HC else 1.0, bank[i % 4][:, 0:T],
                                       ALU.mult, ALU.mult).then_inc(sig("l2_applied"), 1)
            for n in range(NGROUPS):
                c, h0_ = divmod(n * NG, HC)
                hs = range(NG)

                def per_head(v, h):
                    return v[:, c, h0_ + h:h0_ + h + 1]
                dve.wait_ge(*at("d_gb", n + 1))
                if n == 0:
                    dve.wait_ge(*at("levels", 1))
                for h in hs:
                    V.tensor_scalar(EA[:, h, :], Gb[:, h, :], per_head(Gt, h), 0.0, ALU.subtract, ALU.max)
                    V.tensor_scalar(QK[:, h, :], Gb[:, h, :], per_head(Gt, h), 0.0, ALU.subtract, ALU.min)
                V.tensor_tensor(kd_s[:, 0:NG], Gb[:, :, P - 1], Gt[:, c, h0_:h0_ + NG], ALU.subtract).then_inc(sig("d_diff"), 1)
                dve.wait_ge(*at("d_exp", n + 1))
                V.tensor_tensor(EA, EA, heads(1), ALU.mult)
                V.tensor_tensor(QK, QK, heads(2), ALU.mult)
                if c:
                    V.tensor_tensor(QD, QD, qT[:, h0_:h0_ + NG, c * P:(c + 1) * P], ALU.mult)
                for h in hs:
                    V.tensor_scalar(KDc[:, h, :], bank[3][:, h * P:(h + 1) * P], kd_s[:, h:h + 1], None, ALU.mult)
                    V.tensor_scalar(KB[:, h, :], bank[3][:, h * P:(h + 1) * P], per_head(bkb, h), None, ALU.mult)
                    last = V.tensor_scalar(VB[:, h, :], bank[4][:, h * P:(h + 1) * P], per_head(beta, h), None, ALU.mult)
                link(last)
                V.tensor_tensor(QK, QK, le_mask[:].unsqueeze(1).broadcast_to([P, NG, P]), ALU.mult)
                for h in hs:
                    last = V.scalar_tensor_tensor(EA[:, h, :], EA[:, h, :], per_head(beta, h), gt_mask[:], ALU.mult, ALU.mult)
                link(last)
                link(V.tensor_tensor(Am, EA, lvl[:, 0, :].unsqueeze(1).broadcast_to([P, NG, P]), ALU.mult))
                V.tensor_tensor(Tm, ident[:].unsqueeze(1).broadcast_to([P, NG, P]), Am, ALU.subtract).then_inc(sig("d_T0"), 1)
                dve.wait_ge(*at("d_T0t", n + 1))
                V.tensor_copy(Tt, heads(5)).then_inc(sig("d_T"), 1)
                for l in range(1, LEVELS):
                    k = n * (LEVELS - 1) + l
                    if l > 1:
                        dve.wait_ge(*at("d_Y", k - 1))
                    else:
                        dve.wait_ge(*at("d_T0", n + 1))
                    V.tensor_tensor(Am, EA, lvl[:, l, :].unsqueeze(1).broadcast_to([P, NG, P]), ALU.mult).then_inc(sig("d_Am"), 1)
                    if l > 1:
                        dve.wait_ge(*at("d_D", k - 1))
                        V.tensor_tensor(Tm, Tm, heads(0), ALU.subtract)
                        V.tensor_tensor(Tt, Tt, heads(7), ALU.subtract).then_inc(sig("d_T"), 1)
                dve.wait_ge(*at("d_D", (n + 1) * (LEVELS - 1)))
                V.tensor_tensor(Tt, Tt, heads(7), ALU.subtract).then_inc(sig("d_T"), 1)
                dve.wait_ge(*at("d_S", n + 1))
                for h in hs:
                    if c:
                        last = V.scalar_tensor_tensor(S_pr[:, h0_ + h, :], S_pr[:, h0_ + h, :], ge[:, h:h + 1],
                                                      bank[4][:, h * P:(h + 1) * P], ALU.mult, ALU.add)
                    else:
                        last = V.tensor_copy(S_pr[:, h0_ + h, :], bank[4][:, h * P:(h + 1) * P])
                last.then_inc(sig("d_done"), 1)
            dve.wait_ge(*at("d_done", 2 * NGROUPS))
            prod = inv[:, 0, 0:HC * TS].rearrange("p (h b) -> p h b", h=HC)
            V.tensor_tensor(prod, qT[:, :, TP:T], kT[:, :, TP:T], ALU.mult).then_inc(sig("s_prod"), 1)
            dve.wait_ge(*at("s_egb", 1))
            dve.wait_ge(*at("s_qks", 1))
            for h in range(HC):
                eg, be = egb[:, 0, h, :], egb[:, 1, h, :]
                dve.wait_ge(*at("s_ks", h + 1))
                qS = bank[2 + h % 2][:, 0:2 * TS].rearrange("p (b k) -> p b k", k=2)[:, :, 0]
                kS = bank[2 + h % 2][:, 0:2 * TS].rearrange("p (b k) -> p b k", k=2)[:, :, 1]
                link(V.tensor_tensor(vn_s, kS, eg, ALU.mult))
                link(V.tensor_tensor(vn_s, vT[:, h, TP:T], vn_s, ALU.subtract))
                link(V.tensor_tensor(vn_s, vn_s, be, ALU.mult))
                V.tensor_tensor(vn_t, qS, eg, ALU.mult).then_inc(sig("s_v"), 1)
                link(V.tensor_tensor(prod[:, 0, :], vn_s, qks[:, h, :], ALU.mult))
                V.tensor_tensor(oT[:, h, TP:T], prod[:, 0, :], vn_t, ALU.add).then_inc(sig("s_o"), 1)
                dve.wait_ge(*at("s_vt", h + 1))
                if h:
                    dve.wait_ge(*at("s_outer", h))
                link(V.tensor_copy(k_row, bank[4][0:TS, P:2 * P]))
                V.tensor_tensor(v_diag[0:TS], ident[0:TS, 0:TS].unsqueeze(2).broadcast_to([TS, TS, P]),
                                bank[4][0:TS, 0:P].unsqueeze(1).broadcast_to([TS, TS, P]), ALU.mult).then_inc(sig("s_vd"), 1)
                for b in range(TS):
                    last = V.tensor_scalar(s_ring[h % 4][:, b, :], s_ring[h % 4][:, b, :], eg[:, b:b + 1], None, ALU.mult)
                link(last)
                dve.wait_ge(*at("s_outer", h + 1))
                for k in range(2):
                    n = TS // 2
                    last = V.tensor_tensor(s_ring[h % 4][:, k * n:(k + 1) * n, :], s_ring[h % 4][:, k * n:(k + 1) * n, :], heads(5 + k), ALU.add)
                last.then_inc(sig("s_state"), 1)
            dve.wait_ge(*at("on_root", 1))
            V.reciprocal(inv[0:HC, 0, :], inv[0:HC, 0, :]).then_inc(sig("on_inv"), 1)
            for h in range(HC):
                dve.wait_ge(*at("on_b", h + 1))
                V.scalar_tensor_tensor(oT[:, h, :], oT[:, h, :], col("onorm_g"), bank[h % 4][:, 0:T], ALU.mult, ALU.mult)\
                 .then_inc(sig("on_applied"), 1)
            dve.wait_ge(*at("on_applied", HC))
            for r in range(2):
                part = slice(r * HALF, (r + 1) * HALF)
                V.tensor_tensor(oT[:, part, :], oT[:, part, :], zT[:, part, :], ALU.mult).then_inc(sig("on_done"), 1)
            low_parts(dve, oT, "on_hi", "on_lo")
            for m in range(KD):
                if m % 4 == 0:
                    behind(dense_lo, dve, "w_out_o", m // 4, 0)
                dve.wait_ge(*at("out_o_psum", m + 1))
                V.tensor_tensor(xT[:, m, :], xT[:, m, :], bank[m % 8][:, 0:T], ALU.add).then_inc(sig("out_o_added"), 1)
                if m % 4 == 3:
                    behind(dense_lo, dve, "w_out_o", m // 4, 1)
            norm_dve(dve, 3, "ln_ffn_o", link)
            dve.wait_ge(*at("iota_psum", 1))
            V.tensor_copy(iota, bank[7][:, 0:P]).then_inc(sig("iota"), 1)
            dve.wait_ge(*at("iota", 1))
            dve.wait_ge(*at("logits_psum", 1))
            for i, (t0, n) in enumerate(TOK):
                last = V.tensor_copy(logit[0:n, i, :], bank[5][0:n, i * NE:(i + 1) * NE])
            link(last)
            for i, (t0, n) in enumerate(TOK):
                last = V.max(top[0:n, i, :], logit[0:n, i, :])
            link(last)
            for i, (t0, n) in enumerate(TOK):
                V.max_index(top_i[0:n, i, :], top[0:n, i, :], logit[0:n, i, :])
                last = V.tensor_tensor(gates[0:n, i, 1:2], top[0:n, i, 1:2], top[0:n, i, 0:1], ALU.subtract)
            last.then_inc(sig("top_diff"), 1)
            dve.wait_ge(*at("gate_exp", 1))
            for i, (t0, n) in enumerate(TOK):
                V.tensor_copy(idx_f[0:n, i, :], top_i[0:n, i, 0:2])
                last = V.tensor_scalar(gates[0:n, i, 0:1], gates[0:n, i, 1:2], 1.0, None, ALU.add)
            link(last)
            for i, (t0, n) in enumerate(TOK):
                last = V.reciprocal(gates[0:n, i, 0:1], gates[0:n, i, 0:1])
            link(last)
            for i, (t0, n) in enumerate(TOK):
                last = V.tensor_tensor(gates[0:n, i, 1:2], gates[0:n, i, 1:2], gates[0:n, i, 0:1], ALU.mult)
            link(last)
            for i, (t0, n) in enumerate(TOK):
                io = iota[0:n, 0:NE]
                V.tensor_scalar(mask[0:n, i, :], io, idx_f[0:n, i, 0:1], None, ALU.is_equal)
                V.tensor_scalar(comb[0:n, i, :], io, idx_f[0:n, i, 0:1], gates[0:n, i, 0:1], ALU.is_equal, ALU.mult)
                last = V.tensor_scalar(comb2[0:n, i, :], io, idx_f[0:n, i, 1:2], gates[0:n, i, 1:2], ALU.is_equal, ALU.mult)
            link(last)
            for i, (t0, n) in enumerate(TOK):
                V.tensor_tensor(comb[0:n, i, :], comb[0:n, i, :], comb2[0:n, i, :], ALU.add)
                last = V.scalar_tensor_tensor(mask[0:n, i, :], iota[0:n, 0:NE], idx_f[0:n, i, 1:2], mask[0:n, i, :], ALU.is_equal, ALU.add)
            last.then_inc(sig("masks"), 1)
            dve.wait_ge(*at("ranks_psum", 1))
            V.reduce_max(count, bank[6][:, NTT * NE:(NTT + 1) * NE], X)
            for i, (t0, n) in enumerate(TOK):
                last = V.scalar_tensor_tensor(rank[0:n, i, :], mask[0:n, i, :], -FAR, bank[6][0:n, i * NE:(i + 1) * NE], ALU.mult, ALU.add)
            link(last)
            for i, (t0, n) in enumerate(TOK):
                last = V.tensor_scalar(rank[0:n, i, :], rank[0:n, i, :], FAR, None, ALU.add)
            last.then_inc(sig("ranks"), 1)
            V.tensor_copy(count_i, count).then_inc(sig("flag"), 1)
            dve.wait_ge(*at("flag", 1))
            for i, (name, k) in enumerate((("act_done", 2), ("tr_out", 1), ("y1_out", 1), ("added", NTT * YC))):
                V.memset(spare[:, 2 + i:3 + i], 0.0).then_inc(sig(name), k)

            def column(v, i, n, e):
                return v[0:n, i, e:e + 1] if isinstance(e, int) else v[0:n, i, bass.ds(e, 1)]

            def select(e):
                for i, (t0, n) in enumerate(TOK):
                    V.tensor_scalar(sel[0:n, i, :], iota[0:n, 0:CAP], column(rank, i, n, e), None, ALU.is_equal)
                    last = V.tensor_scalar(selw[0:n, i, :], iota[0:n, 0:CAP], column(rank, i, n, e), column(comb, i, n, e),
                                           ALU.is_equal, ALU.mult)
                last.then_inc(sig("sel"), 1)

            def hte_lo(it):
                for r in range(2):
                    dve.wait_ge(*at("hte_hi", it * 2 + r + 1))
                    n = KD // 2
                    V.tensor_tensor(hte_l[:, r * n:(r + 1) * n, :], bank[(7, 3)[r]][:, :].rearrange("p (j t) -> p j t", j=n),
                                    hte_h[:, r * n:(r + 1) * n, :].bitcast(F32), ALU.subtract).then_inc(sig("hte"), 1)

            def tr_lo(it, c):
                dve.wait_ge(*at("tr_hi", it * NSTEP + c + 1))
                V.tensor_tensor(act_l[:, c % 2], bank[4][:, :].rearrange("p (k t) -> p k t", k=KF), act_h[:, c % 2].bitcast(F32),
                                ALU.subtract).then_inc(sig("tr_out"), 1)

            def dve_expert(it, more, e_next):
                for n, (kind, c, part) in enumerate(order_e):
                    if kind == "g" and part and c:
                        tr_lo(it, c - 1)
                    if kind == "u" and part:
                        dve.wait_ge(*at("sil", it * NSTEP + c + 1))
                        wait_used(dve, it, "u", c)
                        V.tensor_tensor(m_act[:, c % 2, :], m_sil[:, c % 2, :], bank[c % 2 * 2 + 1][:, :], ALU.mult).then_inc(sig("act_done"), 1)
                        if c == 2 and more:
                            dve.wait_ge(*at("moe_w", it + 1))
                            select(e_next)
                    if n == PER - 3:
                        if more:
                            hte_lo(it + 1)
                        tr_lo(it, NSTEP - 1)
                    if more or n + SPLIT < PER:
                        take_lo(dve, it, n + SPLIT)
                wait_used(dve, it, "d", NSTEP - 1)
                V.tensor_copy(y_e[:, CHUNK_COLS:D], bank[6][:, :]).then_inc(sig("y1_out"), 1)
                for k in range(NTT * YC):
                    i, hf = divmod(k, YC)
                    n = TOK[i][1]
                    a = acc[0:n, i, hf * CHUNK_COLS:(hf + 1) * CHUNK_COLS]
                    dve.wait_ge(*at("moe_c", it * (NTT * YC) + k + 1))
                    V.tensor_tensor(a, a, bank[(7, 3, 2)[k % 3]][0:n, :], ALU.add).then_inc(sig("added"), 1)

            select(0)
            hte_lo(0)
            dve.wait_ge(*at("xtok", NTT * YC))
            with dve.Fori(0, NE - 1) as e:
                dve_expert(e, True, e + 1)
            dve_expert(NE - 1, False, 0)
            with dve.If(dve.value_load(count_i[0:1, 0:1], min_val=0, max_val=T) > CAP):
                with dve.Fori(1, PASSES) as p:
                    dve.wait_ge(*at("moe_w", p * NE))
                    for i, (t0, n) in enumerate(TOK):
                        last = V.tensor_scalar(rank[0:n, i, :], rank[0:n, i, :], float(-CAP), None, ALU.add)
                    last.then_inc(sig("rank_pass"), 1)
                    with dve.Fori(0, NE) as e:
                        dve.wait_ge(*at("rank_pass", p))
                        dve.wait_ge(*at("moe_w", p * NE + e))
                        select(e)
                        for n in range(SPLIT):
                            take_lo(dve, p * NE + e, n)
                        hte_lo(p * NE + e)
                        dve_expert(p * NE + e, False, 0)
            V.memset(spare[:, 6:7], 0.0).then_inc(sig("y_ready"), 1)

        @block.tensor
        def _(pe):
            pe.wait_ge(*at("constants", 2))
            pe.wait_ge(*at("par_loaded", 16 * N_PAR))
            PE.transpose(bank[4][:, 0:N_ROWS], par_rows[0:N_ROWS, :], ident[0:N_ROWS, 0:N_ROWS])
            PE.transpose(bank[4][:, P:P + N_CD], cd_rows[0:N_CD, :], ident[0:N_CD, 0:N_CD])
            n = TS * HIST
            for t in range(NL):
                PE.transpose(bank[4][:, 2 * P + t * n:2 * P + (t + 1) * n], hist_rows[:, t * P:(t + 1) * P], ident[0:n, 0:n])
                last = PE.transpose(bank[4][:, 3 * P + t * TS:3 * P + (t + 1) * TS], h0_rows[:, t * P:(t + 1) * P],
                                    ident[0:TS, 0:TS])
            last.then_inc(sig("par_psum"), 1)
            pe.wait_ge(*at("x_loaded", 32))
            for j in range(KD):
                if j >= 4:
                    pe.wait_ge(*at("xT_done", j - 3))
                for i, (t0, n) in enumerate(TOK):
                    last = PE.transpose(bank[j % 4][:, t0:t0 + n], x_tok[0:n, i, j * P:(j + 1) * P], ident[0:n, 0:n])
                last.then_inc(sig("xT_psum"), 1)
            pe.wait_ge(*at("par_done", 1))
            norm_pe(pe, 0)
            pe.wait_ge(*at("norm0_done", 2))
            dense_pe(pe, "w_in_e", IN_E // P, "proj_psum", "proj_done")
            pe.wait_ge(*at("proj_done", IN_E // P))
            pe.wait_ge(*at("xc_done", 1))
            pe.wait_ge(*at("lru_w_loaded", 64))
            for g in range(2):
                for t in range(NL):
                    PE.matmul(bank[g * NL + t][:, 0:T], lru_w[:, g, t, :], xc[:, t, :], start=True, stop=True)\
                      .then_inc(sig("lru_gate_psum"), 1)
            pe.wait_ge(*at("qk_sq", 1))
            for i in range(2 * HB):
                if i >= 4:
                    pe.wait_ge(*at("qk_root", i - 3))
                PE.matmul(bank[i % 4][:, 0:T], halves[:], inv[:, i, :], start=True, stop=True).then_inc(sig("qk_ss"), 1)
            PE.matmul(bank[4][:, 0:2], lamv.broadcast_to([P, P]), half2[:], start=True, stop=True).then_inc(sig("lam_psum"), 1)
            pe.wait_ge(*at("qk_done", 1))
            pe.wait_ge(*at("lam_exp", 1))
            for i, (t0, n) in enumerate(TOK):
                for h in range(HB):
                    last = PE.transpose(bank[i][0:n, h * P:(h + 1) * P], proj[:, K_ + h, t0:t0 + n], ident[:])
                last.then_inc(sig("ktok_psum"), 1)
            for i, (t0, n) in enumerate(TOK):
                for h in range(HB):
                    last = PE.transpose(bank[3 + i][0:n, h * P:(h + 1) * P], proj[:, V_ + h, t0:t0 + n], ident[:])
                last.then_inc(sig("vtok_psum"), 1)
            for h in range(HB):
                last = PE.transpose(bank[6][0:TS, h * P:(h + 1) * P], proj[:, Q_ + h, TP:T], ident[:])
            last.then_inc(sig("qs_psum"), 1)
            for t in range(NL):
                last = PE.transpose(bank[7][0:TAIL, t * P:(t + 1) * P], proj[:, XR + t, T - TAIL:T], ident[:])
            last.then_inc(sig("tail_psum"), 1)
            pe.wait_ge(*at("tail_tok", 1))
            for t in range(NL):
                last = PE.transpose(bank[7][0:TS + 1, t * P:(t + 1) * P], hl[:, t, :], ident[:])
            last.then_inc(sig("hlast_psum"), 1)
            pe.wait_ge(*at("vtok", 3))
            pe.wait_ge(*at("qs_tok", 1))
            for b in range(TS):
                if b >= 2:
                    pe.wait_ge(*at("k_pages_used", b - 1))
                PE.matmul(bank[4 + b % 2][:, 0:AW], ident[0:TS, b:b + 1].broadcast_to([TS, P]), qs_tok, start=True, stop=True)\
                  .then_inc(sig("qb_psum"), 1)
            pe.wait_ge(*at("k_pages_used", TS))
            for i in range(2):
                for g in range(NP_):
                    c = (i * NP_ + g) * P
                    last = PE.transpose(bank[4][0:NB, c:c + P], sc_s[:, g, i].rearrange("p h b -> p (h b)"), ident[:])
            last.then_inc(sig("ss_psum"), 1)
            pe.wait_ge(*at("qk_self", 1))
            PE.matmul(bank[5][0:NB, 0:2], qk_s.rearrange("p h b -> p (h b)"), half2[:], start=True, stop=True).then_inc(sig("self_psum"), 1)
            pe.wait_ge(*at("p_s", 1))
            for g in range(NP_):
                PE.transpose(bank[6][:, g * NB:(g + 1) * NB], ss[:, 0, g * P:(g + 1) * P], ident[0:NB, 0:NB])
            PE.matmul(bank[6][:, NP_ * NB:(NP_ + 1) * NB], ss[:, 0, NP_ * P:NP_ * P + 1].broadcast_to([NB, P]), ident[0:NB, 0:NB],
                      start=True, stop=True).then_inc(sig("pT_s_psum"), 1)
            pe.wait_ge(*at("pT_s", 1))
            pe.wait_ge(*at("hlast", 1))
            for b in range(TS):
                n = TS + b
                pe.wait_ge(*at(f"kv{n % 4}_loaded", 32 * (n // 4 + 1)))
                for h in range(HB):
                    o = bank[7][:, h * TS + b:h * TS + b + 1]
                    for g in range(NP_):
                        last = PE.matmul(o, pages_kv[:, n % 4, g, h * P:(h + 1) * P], pT_s[:, g, h * TS + b:h * TS + b + 1],
                                         start=g == 0, stop=g == NP_ - 1)
                last.then_inc(sig("v_pages_used"), 1)
            pe.wait_ge(*at("v_pages_used", TS))
            for i in range(HH):
                h, k = divmod(i, 2)
                rows_ = slice(k * DH, (k + 1) * DH)
                if i >= 4:
                    pe.wait_ge(*at("scores", i - 3))
                PE.matmul(bank[i % 4][:, 0:P], proj[rows_, Q_ + h, 0:P], proj[rows_, K_ + h, 0:P], start=True, stop=True)
                PE.matmul(bank[i % 4][:, P:3 * P], proj[rows_, Q_ + h, P:2 * P], proj[rows_, K_ + h, 0:2 * P],
                          start=True, stop=True).then_inc(sig("scores_psum"), 1)
            pe.wait_ge(*at("scores", HH))
            for h in range(HB):
                pe.wait_ge(*at("probs", h + 1))
                if h >= 2:
                    pe.wait_ge(*at("pT", h - 1))
                    pe.wait_ge(*at("o_prompt", h - 1))
                for c in range(3):
                    last = PE.transpose(bank[h % 2][:, c * P:(c + 1) * P], sc_p[:, 2 * h, c * P:(c + 1) * P], ident[:])
                last.then_inc(sig("pT_psum"), 1)
                pe.wait_ge(*at("pT", h + 1))
                o = bank[2 + h % 2]
                v = [vtok[:, i, h * P:(h + 1) * P] for i in range(TT)]
                PE.matmul(o[:, 0:P], v[0], pT[h % 2][:, 0:P], start=True, stop=True)
                PE.matmul(o[:, P:2 * P], v[0], pT[h % 2][:, P:2 * P], start=True, stop=False)
                PE.matmul(o[:, P:2 * P], v[1], pT[h % 2][:, 2 * P:3 * P], start=False, stop=True).then_inc(sig("pv_psum"), 1)
            pe.wait_ge(*at("o_sq", 1))
            for h in range(HB):
                PE.matmul(bank[4 + h][:, 0:T], ones[:], osq[:, h, :], start=True, stop=True).then_inc(sig("o_ss"), 1)
            pe.wait_ge(*at("mix_lo", 1))
            dense_pe(pe, "w_out_e", KD, "out_e_psum", "out_e_added")
            norm_pe(pe, 1)
            pe.wait_ge(*at("norm1_done", 2))
            for n in range(NFC):
                tiles = range(n * (CHUNK_COLS // P), min(NF, (n + 1) * (CHUNK_COLS // P)))
                for name, s, b0, free in (("ffn_wg", "ffn_g", 0, "ffn_sil"), ("ffn_wu", "ffn_u", 4, "ffn_act")):
                    def wait_bank(m):
                        if m >= 4:
                            pe.wait_ge(*at(free, m - 3))
                    dense_chunk(pe, name, n, tiles, lambda m: b0 + m % 4, s, wait_bank)
            pe.wait_ge(*at("ffn_act", NF))
            for m in range(KD):
                wait_chunk(pe, place["ffn_wd", m])
                if m >= 4:
                    pe.wait_ge(*at("ffn_added", m - 3))
                for j in range(NF):
                    last = PE.matmul(bank[m % 4][:, 0:T], chunk("ffn_wd", m)[:, j, :], act[:, j, :],
                                     start=j == 0, stop=j == NF - 1)
                last.then_inc(sig("ffn_d_psum"), 1)
                used(pe)

            pe.wait_ge(*at("dhist_loaded", 16))
            n = TS * HIST
            for m in range(NQ):
                k, t = divmod(m, NQ // 2)
                last = PE.transpose(bank[5 + k][:, t * n:(t + 1) * n], dhist_rows[:, m * P:(m + 1) * P], ident[0:n, 0:n])
            last.then_inc(sig("dhist_psum"), 1)
            norm_pe(pe, 2)
            pe.wait_ge(*at("norm2_done", 2))
            pe.wait_ge(*at("small_w", 64))
            for i, (t0, n) in enumerate(TOK):
                for j in range(KD):
                    last = PE.matmul(bank[7][0:n, i * 2 * HC:(i + 1) * 2 * HC], hT[:, j, t0:t0 + n], w_ba[:, j, :],
                                     start=j == 0, stop=j == KD - 1)
            last.then_inc(sig("ba_psum"), 1)
            dense_pe(pe, "w_in_o", NQ + HC, "qkvz_psum", "qkvz_read", before=((7, "ba_read", 1),))
            pe.wait_ge(*at("qkvz_read", NQ + HC))
            for n in range(QKV // CHUNK_COLS):
                if n >= 3:
                    pe.wait_ge(*at("dtail", n - 2))
                if n == 2:
                    pe.wait_ge(*at("g", 1))
                for k in range(CHUNK_COLS // P):
                    m = n * (CHUNK_COLS // P) + k
                    last = PE.transpose(bank[5 + n % 3][0:TAIL, k * P:(k + 1) * P], tailT[:, m, :], ident[:])
                last.then_inc(sig("dtail_psum"), 1)
            for r in range(2):
                pe.wait_ge(*at("l2_sq", r + 1))
                for i in range(HC):
                    k = r * HC + i
                    last = PE.matmul(bank[4][0:2 * HC, 0:T], pick[:, 2 * HC - 1 - k:4 * HC - 1 - k], inv[:, i, :],
                                     start=k == 0, stop=k == 2 * HC - 1)
                last.then_inc(sig("l2_used" if r == 0 else "l2_ss"), 1)
            pe.wait_ge(*at("dtail", QKV // CHUNK_COLS))
            PE.matmul(bank[7][:, 0:TT * HC], le_mask[:], g_t[:, 0:TT, :].rearrange("p c h -> p (c h)"), start=True, stop=True)\
              .then_inc(sig("Gt_psum"), 1)
            pe.wait_ge(*at("l2_inv", 1))
            pe.wait_ge(*at("qkvz_read", NQ + HC))
            for i in range(2 * HC):
                if i >= 4:
                    pe.wait_ge(*at("l2_applied", i - 3))
                PE.matmul(bank[i % 4][:, 0:T], ident[0:2 * HC, i:i + 1].broadcast_to([2 * HC, P]), inv[0:2 * HC, 0, :],
                          start=True, stop=True).then_inc(sig("l2_b"), 1)
            pe.wait_ge(*at("l2_applied", 2 * HC))
            for n in range(NGROUPS):
                c, h0_ = divmod(n * NG, HC)
                tc = slice(c * P, (c + 1) * P)
                hs = range(NG)

                def hb(b, h):
                    return bank[b][:, h * P:(h + 1) * P]
                if n:
                    pe.wait_ge(*at("d_done", 2 * n))
                for h in hs:
                    PE.matmul(hb(0, h), g_t[:, c, h0_ + h:h0_ + h + 1].broadcast_to([P, P]), le_mask[:], start=True, stop=True)
                for h in hs:
                    PE.matmul(hb(1, h), kT[:, h0_ + h, tc], kT[:, h0_ + h, tc], start=True, stop=True)
                for h in hs:
                    PE.matmul(hb(2, h), kT[:, h0_ + h, tc], qT[:, h0_ + h, tc], start=True, stop=True)
                for h in hs:
                    PE.transpose(hb(3, h), kT[:, h0_ + h, tc], ident[:])
                for h in hs:
                    last = PE.transpose(hb(4, h), vT[:, h0_ + h, tc], ident[:])
                last.then_inc(sig("d_in"), 1)
                pe.wait_ge(*at("d_T0", n + 1))
                for h in hs:
                    last = PE.transpose(hb(5, h), Tm[:, h, :], ident[:])
                last.then_inc(sig("d_T0t"), 1)
                for l in range(1, LEVELS):
                    k = n * (LEVELS - 1) + l
                    pe.wait_ge(*at("d_Am", k))
                    pe.wait_ge(*at("d_T", n * LEVELS + l))
                    for h in hs:
                        last = PE.matmul(hb(6, h), Am[:, h, :], Tt[:, h, :], start=True, stop=True)
                    last.then_inc(sig("d_Y"), 1)
                    pe.wait_ge(*at("d_Yc", k))
                    for h in hs:
                        last = PE.matmul(hb(7, h), Tm[:, h, :], Yb[:, h, :], start=True, stop=True)
                    if l < LEVELS - 1:
                        for h in hs:
                            last = PE.matmul(hb(0, h), Yb[:, h, :], Tm[:, h, :], start=True, stop=True)
                    last.then_inc(sig("d_D"), 1)
                pe.wait_ge(*at("d_T", (n + 1) * LEVELS))
                if c:
                    for h in hs:
                        last = PE.matmul(hb(1, h), KB[:, h, :], Tt[:, h, :], start=True, stop=True)
                    last.then_inc(sig("d_w"), 1)
                    pe.wait_ge(*at("d_nw", n - NGROUPS // TT + 1))
                for h in hs:
                    last = PE.matmul(hb(2, h), Tt[:, h, :], VB[:, h, :], start=True, stop=not c)
                    if c:
                        last = PE.matmul(hb(2, h), NW[:, h, :], S_pr[:, h0_ + h, :], start=False, stop=True)
                last.then_inc(sig("d_v"), 1)
                pe.wait_ge(*at("d_vn", n + 1))
                for h in hs:
                    last = PE.matmul(hb(3, h), VN[:, h, :], QK[:, h, :], start=True, stop=not c)
                    if c:
                        last = PE.matmul(hb(3, h), S_pr[:, h0_ + h, :], QD[:, h, :], start=False, stop=True)
                last.then_inc(sig("d_o"), 1)
                for h in hs:
                    last = PE.matmul(hb(4, h), KDc[:, h, :], VN[:, h, :], start=True, stop=True)
                last.then_inc(sig("d_S"), 1)
            pe.wait_ge(*at("d_done", 2 * NGROUPS))
            PE.matmul(bank[0][:, 0:2 * HC * TS], ones[0:TS, :], gd[0:TS].rearrange("p a b c -> p (a b c)"), start=True, stop=True)\
              .then_inc(sig("s_gb"), 1)
            pe.wait_ge(*at("s_prod", 1))
            PE.matmul(bank[1][:, 0:HC * TS], ones[:], inv[:, 0, 0:HC * TS], start=True, stop=True).then_inc(sig("s_qk"), 1)
            for h in range(HC):
                pe.wait_ge(*at(f"state{h % 4}_loaded", 16 * (h // 4 + 1)))
                if h >= 2:
                    pe.wait_ge(*at("s_o", h - 1))
                for b in range(TS):
                    last = PE.matmul(bank[2 + h % 2][:, 2 * b:2 * b + 2], s_ring[h % 4][:, b, :],
                                     qkvT[:, h:h + HC + 1:HC, TP + b], start=True, stop=True)
                last.then_inc(sig("s_ks"), 1)
                pe.wait_ge(*at("s_v", h + 1))
                if h:
                    pe.wait_ge(*at("s_vd", h))
                PE.transpose(bank[4][0:TS, 0:P], vn_s, ident[:])
                PE.transpose(bank[4][0:TS, P:2 * P], kT[:, h, TP:T], ident[:]).then_inc(sig("s_vt"), 1)
                pe.wait_ge(*at("s_vd", h + 1))
                if h:
                    pe.wait_ge(*at("s_state", h))
                for k in range(2):
                    n = TS // 2
                    last = PE.matmul(bank[5 + k][:, :], k_row, v_diag[0:TS, k * n:(k + 1) * n, :].rearrange("p b e -> p (b e)"),
                                     start=True, stop=True)
                last.then_inc(sig("s_outer"), 1)
            pe.wait_ge(*at("on_sq", 1))
            for i in range(HC):
                last = PE.matmul(bank[4][0:HC, 0:T], pick[:, 2 * HC - 1 - i:3 * HC - 1 - i], inv[:, i, :],
                                 start=i == 0, stop=i == HC - 1)
            last.then_inc(sig("on_ss"), 1)
            pe.wait_ge(*at("on_inv", 1))
            for h in range(HC):
                if h >= 4:
                    pe.wait_ge(*at("on_applied", h - 3))
                PE.matmul(bank[h % 4][:, 0:T], ident[0:HC, h:h + 1].broadcast_to([HC, P]), inv[0:HC, 0, :],
                          start=True, stop=True).then_inc(sig("on_b"), 1)
            pe.wait_ge(*at("on_lo", 2))
            dense_pe(pe, "w_out_o", KD, "out_o_psum", "out_o_added")
            norm_pe(pe, 3)
            pe.wait_ge(*at("norm3_done", 1))
            PE.matmul(bank[7][:, 0:P], ones[:], lt_mask[:], start=True, stop=True).then_inc(sig("iota_psum"), 1)
            for i, (t0, n) in enumerate(TOK):
                for j in range(KD):
                    last = PE.matmul(bank[5][0:n, i * NE:(i + 1) * NE], hT[:, j, t0:t0 + n], w_router[:, j, :],
                                     start=j == 0, stop=j == KD - 1)
            last.then_inc(sig("logits_psum"), 1)
            for s, src in (("xtok", xT), ("htok", hT)):
                for i, (t0, n) in enumerate(TOK):
                    for k in range(YC):
                        r = i * YC + k
                        if r >= 4:
                            pe.wait_ge(*at(s, r - 3))
                        elif s == "htok":
                            pe.wait_ge(*at("xtok", NTT * YC))
                        for m in range(KF):
                            last = PE.transpose(bank[r % 4][0:n, m * P:(m + 1) * P], src[:, k * KF + m, t0:t0 + n], ident[:])
                        last.then_inc(sig(s + "_psum"), 1)
            pe.wait_ge(*at("masks", 1))
            for i, (t0, n) in enumerate(TOK):
                for u in range(i + 1):
                    m = TOK[u][1]
                    PE.matmul(bank[6][0:n, i * NE:(i + 1) * NE], (lt_mask if u == i else ones)[0:m, 0:n], mask[0:m, u, :],
                              start=u == 0, stop=u == i)
            for u in range(NTT):
                m = TOK[u][1]
                last = PE.matmul(bank[6][:, NTT * NE:(NTT + 1) * NE], ones[0:m, :], mask[0:m, u, :], start=u == 0, stop=u == NTT - 1)
            last.then_inc(sig("ranks_psum"), 1)
            pe.wait_ge(*at("htok", NTT * YC))
            pe.wait_ge(*at("flag", 1))

            def dispatch(it):
                pe.wait_ge(*at("sel", it + 1))
                for r in range(2):
                    for jj in range(KD // 2):
                        j = r * (KD // 2) + jj
                        for i, (t0, n) in enumerate(TOK):
                            last = PE.matmul(bank[(7, 3)[r]][:, jj * CAP:(jj + 1) * CAP], h_tok[0:n, i, j * P:(j + 1) * P],
                                             sel[0:n, i, :], start=i == 0, stop=i == NTT - 1)
                    last.then_inc(sig("moe_disp"), 1)

            def transposes(it, c):
                pe.wait_ge(*at("act_done", it * NSTEP + c + 3))
                pe.wait_ge(*at("tr_out", it * NSTEP + c + 1))
                if c == 0:
                    pe.wait_ge(*at("wt_out", it + 1))
                for k in range(KF):
                    last = PE.transpose(bank[4][:, k * P:(k + 1) * P], m_act[:, c % 2, k * P:(k + 1) * P], ident[:])
                last.then_inc(sig("moe_tr"), 1)

            def split_piece(it, kind, c, part):
                n = e_at[kind, c, part]
                pe.wait_ge(*at("lo_done", it * PER + (NDP + n + 1)))
                return (piece_view(whi[:, (NDP + n) % SPLIT, :], kind),
                        piece_view(wlo[:, (NDP + n) % SPLIT, :], kind))

            def product(it, kind, c, out):
                for part in range(2):
                    hi, lo = split_piece(it, kind, c, part)
                    for jj in range(KD // 2):
                        j = part * (KD // 2) + jj
                        PE.matmul(out, hte_l[:, j, :], hi[:, jj, :], start=j == 0, stop=False)
                        PE.matmul(out, hte_h[:, j, :], lo[:, jj, :], start=False, stop=False)
                        last = PE.matmul(out, hte_h[:, j, :], hi[:, jj, :], start=False, stop=j == KD - 1)
                    last.then_inc(sig("piece_used"), 1)

            def down(it, c):
                pe.wait_ge(*at("tr_out", it * NSTEP + c + 2))
                if c == 0:
                    pe.wait_ge(*at("y0_out", it + 1))
                    pe.wait_ge(*at("y1_out", it + 1))
                for part in range(2):
                    hi, lo = split_piece(it, "d", c, part)
                    for kk in range(KF // 2):
                        k = part * (KF // 2) + kk
                        for lhs, rhs in ((act_l, hi), (act_h, lo), (act_h, hi)):
                            for hf in range(YC):
                                last = PE.matmul(bank[5 + hf][:, :], lhs[:, c % 2, k, :], rhs[:, kk, hf * CHUNK_COLS:(hf + 1) * CHUNK_COLS],
                                                 start=c == 0 and k == 0 and lhs is act_l,
                                                 stop=c == NSTEP - 1 and k == KF - 1 and lhs is act_h and rhs is hi)
                    last.then_inc(sig("piece_used"), 1)

            def pe_expert(it, more):
                pe.wait_ge(*at("hte", it * 2 + 2))
                for c in range(NSTEP):
                    pe.wait_ge(*at("act_done", it * NSTEP + c + 1))
                    if c == 1:
                        pe.wait_ge(*at("added", (it + 1) * (NTT * YC)))
                    product(it, "g", c, bank[c % 2 * 2][:, :])
                    if c == 0:
                        pe.wait_ge(*at("tr_out", it * NSTEP + 1))
                        for i, (t0, n) in enumerate(TOK):
                            last = PE.transpose(bank[4][:, t0:t0 + n], selw[0:n, i, :], ident[0:n, 0:n])
                        last.then_inc(sig("moe_w"), 1)
                    else:
                        transposes(it, c - 1)
                    product(it, "u", c, bank[c % 2 * 2 + 1][:, :])
                    if c:
                        down(it, c - 1)
                if more:
                    dispatch(it + 1)
                transposes(it, NSTEP - 1)
                down(it, NSTEP - 1)
                pe.wait_ge(*at("y0_out", it + 2))
                pe.wait_ge(*at("y1_out", it + 2))
                if more:
                    pe.wait_ge(*at("hte", it * 2 + 4))
                for k in range(NTT * YC):
                    i, hf = divmod(k, YC)
                    t0, n = TOK[i]
                    if k >= 3:
                        pe.wait_ge(*at("added", (it + 1) * (NTT * YC) + (k - 2)))
                    PE.matmul(bank[(7, 3, 2)[k % 3]][0:n, :], WT[:, t0:t0 + n], y_e[:, hf * CHUNK_COLS:(hf + 1) * CHUNK_COLS],
                              start=True, stop=True).then_inc(sig("moe_c"), 1)

            dispatch(0)
            with pe.Fori(0, NE - 1) as e:
                pe_expert(e, True)
            pe_expert(NE - 1, False)
            with pe.If(pe.value_load(count_i[0:1, 0:1], min_val=0, max_val=T) > CAP):
                with pe.Fori(1, PASSES) as p:
                    with pe.Fori(0, NE) as e:
                        pe.wait_ge(*at("added", (p * NE + e + 1) * (NTT * YC)))
                        dispatch(p * NE + e)
                        pe_expert(p * NE + e, False)


INPUTS = ["x_prompt", "x_sample", "cache_k", "cache_v", "state_lru_conv", "state_lru_h", "state_delta_conv",
          "state_delta_s", "page_table", "ln_mix_e", "w_in_e", "conv_lru_w", "conv_lru_b", "lru_wx", "lru_bx",
          "lru_wa", "lru_ba", "lru_lambda", "qk_gain_q", "qk_gain_k", "lam_q1", "lam_k1", "lam_q2", "lam_k2",
          "subln_g", "w_out_e", "ln_ffn_e", "ffn_wg", "ffn_wu", "ffn_wd", "ln_mix_o", "w_in_o", "conv_delta_w",
          "a_log", "dt_bias", "onorm_g", "w_out_o", "ln_ffn_o", "router_w", "moe_wg", "moe_wu", "moe_wd"]
OUTPUTS = ["y_prompt", "y_sample", "k_prompt", "v_prompt", "lru_conv_prompt", "lru_h_prompt", "delta_conv_prompt",
           "delta_s_prompt", "k_sample", "v_sample", "lru_conv_sample", "lru_h_sample", "delta_conv_sample",
           "delta_s_sample"]


def output_shapes(s):
    _, bp, tp, d = (1,) + s["x_prompt"]
    bs, ts, _ = s["x_sample"]
    hb, e = s["cache_k"][3:]
    hist, lw = s["state_lru_conv"][2:]
    qkv = s["state_delta_conv"][3]
    hc, dk, dv = s["state_delta_s"][2:]
    return {"y_prompt": (bp, tp, d), "y_sample": (bs, ts, d),
            "k_prompt": (1, bp, tp, hb, e), "v_prompt": (1, bp, tp, hb, e),
            "lru_conv_prompt": (1, bp, hist, lw), "lru_h_prompt": (1, bp, lw),
            "delta_conv_prompt": (1, bp, hist, qkv), "delta_s_prompt": (1, bp, hc, dk, dv),
            "k_sample": (1, bs, ts, hb, e), "v_sample": (1, bs, ts, hb, e),
            "lru_conv_sample": (1, bs, hist, lw), "lru_h_sample": (1, bs, lw),
            "delta_conv_sample": (1, bs, hist, qkv), "delta_s_sample": (1, bs, hc, dk, dv)}


def kernel(**inputs):
    import numpy as np
    import concourse.bacc as bacc
    from concourse.bass_utils import run_bass_kernel_spmd

    nc = bacc.Bacc("TRN2", target_bir_lowering=False, num_devices=1)
    arrays = {f"in_{n}": np.ascontiguousarray(inputs[n]) for n in INPUTS}
    A = {n: nc.dram_tensor(f"in_{n}", arrays[f"in_{n}"].shape, mybir.dt.from_np(arrays[f"in_{n}"].dtype),
                           kind="ExternalInput").ap() for n in INPUTS}
    shapes = output_shapes({n: arrays[f"in_{n}"].shape for n in INPUTS})
    O = {n: nc.dram_tensor(f"out_{n}", shapes[n], F32, kind="ExternalOutput").ap() for n in OUTPUTS}
    program(nc, A, O)
    r = run_bass_kernel_spmd(nc, [arrays], core_ids=[0])
    return tuple(r.results[0][f"out_{n}"] for n in OUTPUTS)
```

```python
import math
from contextlib import ExitStack

import concourse.bass as bass
from concourse import mybir

F32 = mybir.dt.float32
F32R = mybir.dt.float32r
I32 = mybir.dt.int32
U32 = mybir.dt.uint32
ACT = mybir.ActivationFunctionType
ALU = mybir.AluOpType
X = mybir.AxisListType.X

P = 128
CHUNK_COLS = 512
SLOTS = 3
EPS = 1e-6
MASKED = -1e30
RG_C = 8.0
LAM_INIT = 0.8 - 0.6 * math.exp(-0.3 * 0)


def program(nc, A, O):
    TP, D = A["x_prompt"].shape[1:]
    TS = A["x_sample"].shape[0]
    T = TP + TS
    KD = D // P
    TT = TP // P
    TOK = [(i * P, P) for i in range(TT)] + [(TP, TS)]
    LW = A["lru_bx"].shape[1]
    NL = LW // P
    HB, E2 = A["cache_k"].shape[3:]
    DH = E2 // 2
    AW = HB * E2
    NP_ = A["page_table"].shape[1]
    NPOOL = A["cache_k"].shape[1]
    CW = A["conv_lru_w"].shape[1]
    HIST = CW - 1
    IN_E = A["w_in_e"].shape[2]
    FF = A["ffn_wg"].shape[2]
    NF = FF // P
    _, _, HC, DK, DV = A["state_delta_s"].shape
    QKV = A["conv_delta_w"].shape[2]
    NQ = QKV // P
    NE = A["router_w"].shape[2]
    FE = A["moe_wg"].shape[3]
    NCH = FE // CHUNK_COLS
    HH = 2 * HB
    NB = TS * HB
    assert D == KD * P and TP == TT * P and TT == 2 and E2 == P and NP_ == 2 and FE % CHUNK_COLS == 0
    TAIL = HIST + TS

    with ExitStack() as ctx:
        def sb(name, shape, dt=F32):
            return ctx.enter_context(nc.sbuf_tensor(name, shape, dt))

        sems, step_at, given = {}, {}, {}

        def sem(name):
            if name not in sems:
                sems[name] = ctx.enter_context(nc.semaphore(name))
            return sems[name]

        def sig(name):
            if name not in step_at:
                return sem(name)
            engine, first, count = step_at[name]
            assert given.get(engine, 0) == first + given.get(name, 0) and given.get(name, 0) < count, (name, given.get(engine, 0), first)
            given[engine] = given.get(engine, 0) + 1
            given[name] = given.get(name, 0) + 1
            return sem(engine)

        def at(name, count=1):
            if name not in step_at:
                return sem(name), count
            engine, first, most = step_at[name]
            assert 0 < count <= most, (name, count)
            return sem(engine), first + count

        def order(engine, *events):
            first = 0
            for name, count in events:
                step_at[name] = (engine, first, count)
                first += count

        order("scalar_steps",
              ("xT_done", KD), ("norm0_sq", 1), ("norm0_root", 1), ("norm0_hi", 2), ("lam_absexp", 1), ("lam_exp", 1), ("proj_done", IN_E // P),
              ("qk_root", 1), ("lru_gates", 2 * NL), ("lru_a", 2), ("gelu", 1), ("lru_root", 1), ("ya_hi", 1), 
              ("ktok", 3), ("vtok", 3), ("qs_tok", 1), ("tail_tok", 1), ("ss", 1), ("exps_s", 2),
              ("exps", 2 * HH), ("o_sq", 1), ("o_root", 1), ("mix_hi", 1), ("norm1_sq", 1), ("norm1_root", 1), ("norm1_hi", 2), ("ffn_sil", NF),
              ("norm2_sq", 1), ("norm2_root", 1), ("norm2_hi", 2), ("beta", 1), ("g_absexp", 1), ("ealog", 1),
              ("l2_sq", 2), ("l2_root", 1), ("eG", 1), ("dtail", QKV // CHUNK_COLS), ("s_egb", 1), ("s_qks", 1),
              ("on_sq", 1), ("on_root", 1), ("on_hi", 2), ("norm3_sq", 1), ("norm3_root", 1), ("gate_exp", 1),
              ("xtok", 6), ("htok", 6))
        order("tensor_steps",
              ("xT_psum", KD), ("norm0_ss", 1), ("par_psum", 1), ("norm0_b", 1), ("lam_psum", 1), ("proj_psum", IN_E // P),
              ("qk_ss", 1), ("lru_gate_psum", 2 * NL), ("qk_b", HH), ("ktok_psum", 3), ("vtok_psum", 3), ("qs_psum", 1), ("tail_psum", 1),
              ("hlast_psum", 1), ("qb_psum", TS), ("ss_psum", 1), ("self_psum", 1), ("pT_s_psum", 1),
              ("scores_psum", HH), ("o_ss", 1), ("o_b", HB), ("out_e_psum", KD), ("norm1_ss", 1), ("norm1_b", 1), ("ffn_d_psum", KD),
              ("dhist_psum", 1), ("norm2_ss", 1), ("norm2_b", 1), ("ba_psum", 1), ("qkvz_psum", NQ + HC),
              ("Gt_psum", 1), ("l2_ss", 1), ("dtail_psum", QKV // CHUNK_COLS), ("l2_b", 2 * HC),
              ("s_gb", 1), ("s_qk", 1), ("on_ss", 1), ("on_b", HC), ("out_o_psum", KD), ("norm3_ss", 1), ("norm3_b", 1),
              ("iota_psum", 1), ("logits_psum", 1), ("xtok_psum", 6), ("htok_psum", 6), ("ranks_psum", 1))
        order("vector_steps",
              ("norm0_inv", 1), ("par_done", 1), ("norm0_h", 2), ("norm0_done", 2), ("lam_abs", 1), ("xc_done", 1), ("qk_inv", 1), ("lru_y", 1), ("lru_m", 1),
              ("qk_done", 1), ("lru_done", 1), ("ya_lo", 1), ("hlast", 1), ("k_pages_used", TS), ("qk_self", 1), ("neg_max_s", 1),
              ("p_s", 1), ("pT_s", 1), ("scores", HH), ("neg_max", 1), ("probs", HB), ("o_sample", 1), ("o_inv", 1),
              ("mix_done", 1), ("mix_lo", 1), ("out_e_added", KD), ("norm1_inv", 1), ("norm1_h", 2), ("norm1_done", 2), ("ffn_act", NF), ("ffn_added", KD),
              ("norm2_inv", 1), ("norm2_h", 2), ("norm2_done", 2), ("ba_read", 1), ("g_abs", 1), ("g", 1), ("dconv", NQ), ("Gt", 1), ("l2_inv", 1),
              ("l2_applied", 2 * HC), ("s_prod", 1), ("on_inv", 1), ("on_applied", HC), ("on_done", 2), ("on_lo", 2),
              ("out_o_added", KD), ("norm3_inv", 1), ("norm3_done", 1), ("iota", 1), ("top_diff", 1), ("masks", 1), ("ranks", 1))

        ring = sb("weight_ring", [P, SLOTS, KD * CHUNK_COLS])
        PIECE = KD * CHUNK_COLS // 2
        SPLIT = 3
        whi = sb("weight_hi", [P, SPLIT, PIECE], F32R)
        wlo = sb("weight_lo", [P, SPLIT, PIECE], F32R)
        h_hi = sb("h_hi", [P, KD, T], F32R)
        h_lo = sb("h_lo", [P, KD, T], F32R)

        def expert_part(t):
            flat = t[:].rearrange("p a b -> p (a b)")
            KC = CHUNK_COLS // P
            return (flat[:, 0:KD * P].rearrange("p (j t) -> p j t", j=KD),
                    flat[:, KD * P:KD * P + 2 * KC * P].rearrange("p (s k t) -> p s k t", s=2, k=KC))

        hte_h, act_h = expert_part(h_hi)
        hte_l, act_l = expert_part(h_lo)
        ident = sb("ident", [P, P])
        ones = sb("ones", [P, P])
        half2 = sb("half2", [P, 2])
        le_mask = sb("le_mask", [P, P])
        lt_mask = sb("lt_mask", [P, P])
        causal = sb("causal", [P, 3 * P])
        eps_t = sb("eps_t", [P, 1])
        par = sb("par", [P, 80])
        cd = sb("cd", [P, 96])
        small = sb("small", [P, 304])
        xT = sb("xT", [P, KD, T])
        hT = sb("hT", [P, KD, T])
        W = 17700
        work = sb("work", [P, W])
        bank = [ctx.enter_context(nc.psum_tensor(f"bank{i}", [P, CHUNK_COLS], F32)) for i in range(8)]

        class Arena:

            def __init__(self):
                self.at = 0

            def take(self, *dims):
                n = math.prod(dims)
                v = work[:, self.at:self.at + n]
                self.at += n
                assert self.at <= W, self.at
                names = "abcd"[:len(dims)]
                if len(dims) > 1:
                    v = v.rearrange(f"p ({' '.join(names)}) -> p {' '.join(names)}", **dict(zip(names, dims)))
                return v

        rows, row = {}, 0
        for name, ap in (("ln_mix_e", A["ln_mix_e"]), ("conv_lru_w", A["conv_lru_w"]), ("conv_lru_b", A["conv_lru_b"]),
                         ("lru_bx", A["lru_bx"]), ("lru_ba", A["lru_ba"]), ("lru_lambda", A["lru_lambda"]),
                         ("ln_ffn_e", A["ln_ffn_e"]), ("ln_mix_o", A["ln_mix_o"]), ("ln_ffn_o", A["ln_ffn_o"]),
                         ("subln_g", A["subln_g"]), ("onorm_g", A["onorm_g"])):
            n = math.prod(ap.shape)
            rows[name] = (row, n // P, ap)
            row += n // P
        r_gq, r_gk, r_lq, r_lk = row, row + 1, row + 2, row + 3
        N_ROWS = row + 4
        N_CD = CW * NQ

        def col(name, i=0):
            return par[:, rows[name][0] + i:rows[name][0] + i + 1]

        sm_at = [0]

        def vec(n):
            v = small[:, sm_at[0]:sm_at[0] + n]
            sm_at[0] += n
            assert sm_at[0] <= 304
            return v

        def cols(ap, c0, n):
            return ap[:, c0:c0 + n].rearrange("(j p) n -> p j n", p=P)

        dense = []
        place = {}

        def stream_cols(name, ap, total, n):
            c0 = n * CHUNK_COLS
            w = min(CHUNK_COLS, total - c0)
            place[name, n] = len(dense)
            dense.append((cols(ap, c0, w), KD, w))

        for n in range(IN_E // CHUNK_COLS):
            stream_cols("w_in_e", A["w_in_e"][0], IN_E, n)
        for n in range(D // CHUNK_COLS):
            stream_cols("w_out_e", A["w_out_e"][0], D, n)
        NFC = -(-FF // CHUNK_COLS)
        for n in range(NFC):
            stream_cols("ffn_wg", A["ffn_wg"][0], FF, n)
            stream_cols("ffn_wu", A["ffn_wu"][0], FF, n)
        for m in range(KD):
            place["ffn_wd", m] = len(dense)
            dense.append((cols(A["ffn_wd"][0], m * P, P), NF, P))
        NQC = (QKV + D) // CHUNK_COLS
        for n in range(NQC):
            stream_cols("w_in_o", A["w_in_o"][0], QKV + D, n)
        for n in range(D // CHUNK_COLS):
            stream_cols("w_out_o", A["w_out_o"][0], D, n)
        ND = len(dense)

        def slot_view(i, k, w):
            return ring[:, i % SLOTS, 0:k * w].rearrange("p (j n) -> p j n", j=k)

        def chunk(name, n):
            i = place[name, n]
            return slot_view(i, dense[i][1], dense[i][2])

        def wait_chunk(eng, i):
            eng.wait_ge(sig(f"slot{i % SLOTS}_loaded"), 16 * (i // SLOTS + 1))

        split_at = {}
        for i in range(ND):
            if i not in [place["ffn_wd", m] for m in range(KD)]:
                split_at[i] = 2 * len(split_at)
        chunk_of = {n: i for i, n in split_at.items()}
        NDP = 2 * len(split_at)

        def dense_piece(p):
            i = chunk_of[p - p % 2]
            half = dense[i][1] * dense[i][2] // 2
            return i, ring[:, i % SLOTS, p % 2 * half:(p % 2 + 1) * half], half

        a0 = Arena()
        proj = a0.take(IN_E // P, T)
        mixT = proj[:, 0:KD, :]
        inv = a0.take(KD, T)
        pages_kv = a0.take(4, NP_, AW)
        scr = a0.take(3 * D)
        ktok = a0.take(3, AW)
        vtok = a0.take(3, AW)
        lru_w = vtok.rearrange("p a b -> p (a b)")[:, 0:2 * NL * P].rearrange(
            "p (a b c) -> p a b c", a=2, b=NL)
        GATE, XR, Q_, K_, V_ = 0, NL, 2 * NL, 2 * NL + HB, 2 * NL + 2 * HB
        x_tok = scr.rearrange("p (t d) -> p t d", t=3)
        kt_flat = ktok.rearrange("p a b -> p (a b)")
        par_rows, cd_rows = kt_flat[:, 0:P], kt_flat[:, P:2 * P]
        hist_rows = kt_flat[0:TS * HIST, 2 * P:2 * P + LW]
        h0_rows = kt_flat[0:TS, 2 * P + LW:2 * P + 2 * LW]
        kv_flat = pages_kv.rearrange("p a b c -> p (a b c)")
        xc = kv_flat[:, 0:NL * T].rearrange("p (a b) -> p a b", a=NL)
        decay_a = kv_flat[:, NL * T:2 * NL * T].rearrange("p (a b) -> p a b", a=NL)
        gate_x = hT[:, 0:NL, :]
        gate_a = hT[:, NL:2 * NL, :]
        tanh_y = scr[:, 0:NL * T].rearrange("p (a b) -> p a b", a=NL)
        tmp_l = scr[:, NL * T:2 * NL * T].rearrange("p (a b) -> p a b", a=NL)
        hist = vec(NL * TS * HIST).rearrange("p (a b c) -> p a b c", a=NL, b=TS)
        h0 = vec(NL * TS).rearrange("p (a b) -> p a b", a=NL)
        sp8 = vec(NL)
        v_s = [vec(NL) for _ in range(3)]
        lamv = vec(1)
        lam_e = vec(2)
        nlam = vec(1)
        mx = vec(2 * HH)
        ssum = vec(2 * HH)
        rsum = vec(2 * HH)
        subg = vec(1)
        mx_s, ssum_s, rsum_s = vec(2), vec(2), vec(2)
        sc_p = scr[:, 0:HH * 3 * P].rearrange("p (i c) -> p i c", i=HH)
        inv_flat = inv.rearrange("p a b -> p (a b)")
        NQK = 4 * HB
        spread = kt_flat[0:NQK, 0:2 * HB * P]
        pT = [inv_flat[:, k * 384:k * 384 + 3 * P] for k in range(2)]
        kv_mul = inv_flat[:, 0:NP_ * AW].rearrange("p (a b) -> p a b", a=NP_)
        qs_tok = inv_flat[0:TS, 1024:1024 + AW]
        tail_tok = inv_flat[0:TAIL, 1536:1536 + LW]
        sc_s = scr[:, 0:NP_ * HH * TS].rearrange("p (g i h b) -> p g i h b", g=NP_, i=2, h=HB)
        qk_s = scr[:, 256:256 + NB].rearrange("p (h b) -> p h b", h=HB)
        NK_S = NP_ * P + 1
        ss = scr[0:NB, 512:512 + 2 * NK_S].rearrange("p (i c) -> p i c", i=2)
        hist_flat = hist.rearrange("p a b c -> p (a b c)")
        pself = hist_flat[:, 0:NB]
        pT_s = hist_flat[:, NB:NB + NP_ * NB].rearrange("p (g n) -> p g n", g=NP_)
        osq = scr[:, 1300:1300 + HB * T].rearrange("p (h t) -> p h t", h=HB)
        hl = vec(NL * (TS + 1)).rearrange("p (a b) -> p a b", a=NL)
        hl_tok = scr[0:TS + 1, 2560:2560 + LW]
        act = work[:, 0:NF * T].rearrange("p (a b) -> p a b", a=NF)
        sil = scr[:, 0:4 * T].rearrange("p (a b) -> p a b", a=4)
        pg_sb = sb("page_numbers", [1, TS * NP_], I32)


        def shaped(v, dims):
            names = "abcd"[:len(dims)]
            return v if len(dims) == 1 else v.rearrange(f"p ({' '.join(names)}) -> p {' '.join(names)}", **dict(zip(names, dims)))

        def cut(o, *dims):
            return shaped(work[:, o:o + math.prod(dims)], dims)

        NGROUPS = TT * HC // 4
        NG = 4
        LEVELS = 7
        GRP = NG * P
        INV0 = (IN_E // P) * T
        QKV0 = INV0 + KD * T
        TMP0 = QKV0 + NQ * T
        A_0 = HC * T + HC * P
        B_0 = TMP0 + LEVELS * P
        zT = cut(0, HC, T)
        pre = cut(HC * T, 8, T)
        S_pr = cut(HC * T, HC, P)
        qkvT = cut(QKV0, NQ, T)
        qT, kT, vT = qkvT[:, 0:HC, :], qkvT[:, HC:2 * HC, :], qkvT[:, 2 * HC:3 * HC, :]
        oT = hT
        dhist_rows = work[0:TS * HIST, TMP0:TMP0 + QKV]
        tail_rows = work[0:TAIL, TMP0:TMP0 + QKV]
        tailT = cut(TMP0 + QKV, NQ, TAIL)
        dhist = cut(TMP0 + QKV + NQ * TAIL, NQ, TS, HIST)
        lvl = cut(TMP0, LEVELS, P)
        Gb, EA, QK, Tm = (cut(A_0 + k * GRP, NG, P) for k in range(4))
        Tt, Am, KB, KDc, VB, QD = (cut(B_0 + k * GRP, NG, P) for k in range(6))
        Yb, NW, VN = Gb, Tm, Am
        halves = (slice(0, NG // 2), slice(NG // 2, NG))
        LV_Y, LV_T, LV_M = (6, 5), (7, 1), (0, 2)

        def half_of(b, u):
            return bank[b][:, 0:GRP].rearrange("p (h t) -> p h t", h=NG)[:, halves[u], :]

        def level_half(n, l, u):
            return 2 * (n * (LEVELS - 1) + l - 1) + u + 1

        s_ring = [cut(A_0, TS, P), cut(A_0 + 2 * GRP, TS, P), cut(B_0, TS, P), cut(B_0 + 2 * GRP, TS, P)]
        v_new_blocks = (inv.rearrange("p a b -> p (a b)")[:, 2 * T:2 * T + TS * P], work[:, B_0 + 4 * GRP:B_0 + 6 * GRP])
        v_diag = [v.rearrange("p (b e) -> p b e", b=TS) for v in v_new_blocks]
        assert A_0 + 4 * GRP <= INV0 and B_0 + 6 * GRP <= W and TMP0 + QKV + NQ * (TAIL + TS * HIST) <= W
        gt_mask = sb("gt_mask", [P, P])
        w_ba = sb("w_ba", [P, KD, 2 * HC])
        w_router = sb("w_router", [P, KD, NE])
        alog_b = sb("alog_b", [P, HC])
        dt_b = sb("dt_b", [P, HC])
        NS1 = 607
        sm1 = sb("sm1", [P, NS1])
        sm1_at = [0]

        def vec1(*dims):
            n = math.prod(dims)
            v = sm1[:, sm1_at[0]:sm1_at[0] + n]
            sm1_at[0] += n
            assert sm1_at[0] <= NS1
            return shaped(v, dims)

        NTT = TT + 1
        pick = vec1(4 * HC - 1)
        ba = vec1(NTT, 2 * HC)
        beta = vec1(NTT, HC)
        g_t = vec1(NTT, HC)
        sp_t = [vec1(NTT, HC) for _ in range(3)]
        Gt = vec1(TT, HC)
        eG = vec1(TT, HC)
        bkb = vec1(TT, HC)
        kd_s = vec1(HC)
        ge = vec1(HC)
        gd = vec1(2, HC, TS)
        egb = vec1(2, HC, TS)
        qks = vec1(HC, TS)
        pick2 = egb.rearrange("p a b c -> p (a b c)")[:, 0:2 * NQK - 2]
        k_row = [inv[0:TS, 1, k * P:(k + 1) * P] for k in range(2)]
        vn_s = [vec1(TS) for _ in range(2)]
        outer_banks = ((5, 6), (0, 1))
        vn_t = vec1(TS)


        NSTEP = FE // CHUNK_COLS
        KF = CHUNK_COLS // P
        CAP = P
        PASSES = -(-T // CAP)
        YC = D // CHUNK_COLS
        acc = cut(0, NTT, D)
        m_act = cut(NTT * D, 2, CHUNK_COLS)
        m_sil = cut(NTT * D + 2 * CHUNK_COLS, 2, CHUNK_COLS)
        assert NTT * D + 4 * CHUNK_COLS <= INV0
        h_tok = cut(QKV0, NTT, D)
        raw_last = cut(QKV0 + NTT * D, PIECE)
        mo = [QKV0 + NTT * D + PIECE]

        def more_of(*dims):
            v = cut(mo[0], *dims)
            mo[0] += math.prod(dims)
            assert mo[0] <= W
            return v

        sel = more_of(NTT, CAP)
        selw = more_of(NTT, CAP)
        WT = more_of(T)
        y_e = more_of(D)
        iota = more_of(P)
        logit = more_of(NTT, NE)
        top = more_of(NTT, NE)
        top_i = more_of(NTT, NE).bitcast(U32)
        idx_f = more_of(NTT, 2)
        gates = more_of(NTT, 2)
        comb = more_of(NTT, NE)
        comb2 = more_of(NTT, NE)
        mask = more_of(NTT, NE)
        rank = more_of(NTT, NE)
        count = more_of(1)
        count_i = more_of(1).bitcast(I32)
        spare = more_of(8)
        FAR = 16384.0
        order_e = [("g", 0), ("u", 0)]
        for c in range(1, NSTEP):
            order_e += [("g", c), ("u", c), ("d", c - 1)]
        order_e.append(("d", NSTEP - 1))
        order_e = [(kind, c, part) for kind, c in order_e for part in range(2)]
        PER = len(order_e)
        RAW = 2 * SLOTS + 1
        assert PER % RAW == 0 and PER % SPLIT == 0
        e_at = {k: i for i, k in enumerate(order_e)}
        FREED = [ND - SLOTS + i for i in range(SLOTS)]
        FFN_END = split_at[place["w_in_o", 0]]

        def raw_piece(n):
            r = n % RAW
            if r == RAW - 1:
                return raw_last
            return ring[:, FREED[r // 2] % SLOTS, r % 2 * PIECE:(r % 2 + 1) * PIECE]

        def piece_view(flat, kind):
            return flat.rearrange("p (j n) -> p j n", n=D if kind == "d" else CHUNK_COLS)

        def hi_part(p, src, size):
            return SC.activation(whi[:, p % SPLIT, 0:size], src, ACT.Copy).then_inc(sig("hi_done"), 1)

        def lo_part(p, src, size):
            V.tensor_tensor(wlo[:, p % SPLIT, 0:size], src, whi[:, p % SPLIT, 0:size].bitcast(F32), ALU.subtract)\
             .then_inc(sig("lo_done"), 1)

        def take_hi(act_e, it, n):
            act_e.wait_ge(*at(f"raw{n % RAW}_loaded", it * (16 * (PER // RAW)) + 16 * (n // RAW + 1)))
            act_e.wait_ge(*at("piece_used", it * PER + (NDP + n - SPLIT + 1)))
            hi_part(NDP + n, raw_piece(n), PIECE)

        def take_lo(dve, it, n):
            dve.wait_ge(*at("hi_done", it * PER + (NDP + n + 1)))
            lo_part(NDP + n, raw_piece(n), PIECE)

        def dense_hi(act_e, p):
            if p >= NDP:
                return take_hi(act_e, 0, p - NDP)
            i, src, size = dense_piece(p)
            wait_chunk(act_e, i)
            if p >= SPLIT:
                act_e.wait_ge(*at("piece_used", p - SPLIT + 1))
            hi_part(p, src, size)

        def dense_lo(dve, p):
            if p >= NDP:
                return take_lo(dve, 0, p - NDP)
            dve.wait_ge(*at("hi_done", p + 1))
            _, src, size = dense_piece(p)
            lo_part(p, src, size)

        def behind(split, eng, name, n, part, last=None):
            p = split_at[place[name, n]] + part + SPLIT
            if last is None or p < last:
                split(eng, p)

        def wait_used(eng, it, kind, c, part=1):
            eng.wait_ge(*at("piece_used", it * PER + (NDP + e_at[kind, c, part] + 1)))

        N_PAR = len(rows) + 11
        OUTS = 8
        block = ctx.enter_context(nc.Block())
        V, SC, PE, GP = nc.vector, nc.scalar, nc.tensor, nc.gpsimd

        def par_load(dst, src):
            return lambda q: q.dma_start(dst, src).then_inc(sig("par_loaded"), 16)

        par_loads = []
        for r0, n, ap in rows.values():
            flat = ap
            while len(flat.shape) > 1:
                flat = flat.rearrange({2: "a b -> (a b)", 3: "a b c -> (a b c)"}[len(flat.shape)])
            par_loads.append(par_load(par_rows[r0:r0 + n, :], flat.rearrange("(r p) -> r p", p=P)))
        for r, a, b in ((r_gq, "qk_gain_q", "qk_gain_q"), (r_gk, "qk_gain_k", "qk_gain_k"),
                        (r_lq, "lam_q1", "lam_q2"), (r_lk, "lam_k1", "lam_k2")):
            par_loads.append(par_load(par_rows[r:r + 1, 0:DH], A[a]))
            par_loads.append(par_load(par_rows[r:r + 1, DH:P], A[b]))
        par_loads.append(par_load(cd_rows[0:N_CD, :], A["conv_delta_w"][0].rearrange("j (t p) -> (j t) p", p=P)))
        par_loads.append(par_load(hist_rows, A["state_lru_conv"][0].rearrange("b j c -> (b j) c")))
        par_loads.append(par_load(h0_rows, A["state_lru_h"][0]))
        assert len(par_loads) == N_PAR

        @block.sync
        def _(sp):
            for i, (src, k, w) in enumerate(dense):
                before = i - SLOTS
                if before in split_at:
                    sp.wait_ge(*at("lo_done", split_at[before] + 2))
                elif before >= 0:
                    sp.wait_ge(*at("chunk_used", before - place["ffn_wd", 0] + 1))
                sp.dma_start(slot_view(i, k, w), src).then_inc(sig(f"slot{i % SLOTS}_loaded"), 16)
                if i == 0:
                    for load in par_loads[0::2]:
                        load(sp)

            def load_expert(e, it, first):
                for n, (kind, c, part) in enumerate(order_e):
                    if not first or n >= RAW:
                        sp.wait_ge(*at("lo_done", it * PER + (NDP + n - RAW + 1)))
                    elif n < RAW - 1:
                        sp.wait_ge(*at("lo_done", split_at[FREED[n // 2]] + n % 2 + 1))
                    else:
                        sp.wait_ge(*at("out_o_psum", KD))
                    if kind == "d":
                        r0 = c * CHUNK_COLS + part * (CHUNK_COLS // 2)
                        src = A["moe_wd"][0, e, r0:r0 + CHUNK_COLS // 2, :]
                    else:
                        src = A["moe_w" + kind][0, e, part * (D // 2):(part + 1) * (D // 2), c * CHUNK_COLS:(c + 1) * CHUNK_COLS]
                    sp.dma_start(piece_view(raw_piece(n), kind), src.rearrange("(j p) n -> p j n", p=P))\
                      .then_inc(sig(f"raw{n % RAW}_loaded"), 16)

            load_expert(0, 0, True)
            with sp.Fori(1, NE) as e:
                load_expert(e, e, False)
            sp.wait_ge(*at("flag", 1))
            with sp.If(sp.value_load(count_i[0:1, 0:1], min_val=0, max_val=T) > CAP):
                with sp.Fori(1, PASSES) as p:
                    with sp.Fori(0, NE) as e:
                        load_expert(e, p * NE + e, False)
            sp.wait_ge(*at("y_ready", 1))
            sp.dma_start(O["y_prompt"][0].rearrange("(t p) d -> p t d", p=P), acc[:, 0:TT, :]).then_inc(sig("y_written"), 16)
            sp.dma_start(O["y_sample"].rearrange("b t d -> (b t) d"), acc[0:TS, TT, :]).then_inc(sig("y_written"), 16)
            sp.wait_ge(*at("y_written", 32))

        @block.gpsimd
        def _(gp):
            GP.memset(ident[:], 0.0)
            GP.memset(ones[:], 1.0)
            GP.memset(half2[:], 0.0)
            GP.memset(le_mask[:], 1.0)
            GP.memset(lt_mask[:], 1.0)
            GP.memset(gt_mask[:], 1.0)
            GP.memset(sm1[:], 0.0)
            GP.memset(causal[:], 0.0)
            GP.memset(eps_t[:], EPS)
            GP.memset(lru_w, 0.0).then_inc(sig("gp_filled"), 1)
            gp.wait_ge(*at("gp_filled", 1))
            GP.affine_select(out=ident[:], in_=ident[:], compare_op=ALU.not_equal, fill=1.0, base=0,
                             pattern=[[-1, P]], channel_multiplier=1)
            for m, base in ((le_mask, 0), (lt_mask, -1)):
                GP.affine_select(out=m[:], in_=m[:], compare_op=ALU.is_ge, fill=0.0, base=base,
                                 pattern=[[1, P]], channel_multiplier=-1)
            GP.affine_select(out=gt_mask[:], in_=gt_mask[:], compare_op=ALU.is_ge, fill=0.0, base=-1,
                             pattern=[[-1, P]], channel_multiplier=1)
            for c in (0, 2):
                last = GP.affine_select(out=causal[:, c * P:(c + 1) * P], in_=causal[:, c * P:(c + 1) * P],
                                        compare_op=ALU.is_ge, fill=MASKED, base=0, pattern=[[-1, P]], channel_multiplier=1)
            last.then_inc(sig("gp_filled"), 1)
            gp.wait_ge(*at("gp_filled", 2))
            for k in range(2):
                GP.memset(half2[k * DH:(k + 1) * DH, k:k + 1], 1.0).then_inc(sig("constants"), 1)
            for g, name in enumerate(("lru_wx", "lru_wa")):
                w = A[name][0].rearrange("(t k) c d -> k c t d", k=2)
                for k in range(2):
                    gp.dma_start(lru_w[k * DH:(k + 1) * DH, g, :, k * DH:(k + 1) * DH], w[k])\
                      .then_inc(sig("lru_w_loaded"), 16)
            gp.wait_ge(*at("par_psum", 1))
            GP.memset(spread, 1.0).then_inc(sig("spread_steps"), 1)
            for k, (base, step, cm) in enumerate(((0, 1, -DH), (DH - 1, -1, DH))):
                gp.wait_ge(*at("spread_steps", k + 1))
                GP.affine_select(out=spread, in_=spread, compare_op=ALU.is_ge, fill=0.0, base=base,
                                 pattern=[[step, 2 * HB * P]], channel_multiplier=cm)\
                  .then_inc(sig("spread_steps" if k == 0 else "spread_made"), 1)
            gp.dma_start(pg_sb[:], A["page_table"].rearrange("(o b) g -> o (b g)", o=1)).then_inc(sig("pages_loaded"), 16)
            gp.wait_ge(*at("pages_loaded", 16))
            gp.wait_ge(*at("lru_done", 1))
            for n in range(2 * TS):
                b, src = n % TS, A["cache_k" if n < TS else "cache_v"]
                if n >= 4:
                    if n - 4 < TS:
                        gp.wait_ge(*at("k_pages_used", n - 3))
                    else:
                        gp.wait_ge(*at("v_pages_used", n - 3 - TS))
                for g in range(NP_):
                    r = gp.value_load(pg_sb[0:1, b * NP_ + g:b * NP_ + g + 1], min_val=0, max_val=NPOOL - 1)
                    gp.dma_start(pages_kv[:, n % 4, g, :], src[0, r].rearrange("t h e -> t (h e)"))\
                      .then_inc(sig(f"kv{n % 4}_loaded"), 16)

            gp.wait_ge(*at("tail_written", 32))
            GP.memset(lvl, 0.0).then_inc(sig("gp_filled"), 1)
            gp.wait_ge(*at("gp_filled", 3))
            for n in range(LEVELS):
                s = 1 << n
                last = GP.memset(lvl[:, n, :].rearrange("p (k c) -> p k c", c=2 * s)[:, :, 0:s], 1.0)
            last.then_inc(sig("gp_filled"), 1)
            for k in range(2):
                gp.wait_ge(*at("gp_filled", 4 + k))
                for n in range(LEVELS):
                    s = 1 << n
                    m = lvl[:, n, :].rearrange("p (k c) -> p k c", c=2 * s)[:, :, 0:s]
                    base, cm = ((-s, 1), (2 * s - 1, -1))[k]
                    last = GP.affine_select(out=m, in_=m, compare_op=ALU.is_ge, fill=0.0, base=base,
                                            pattern=[[-cm * 2 * s, P // (2 * s)], [0, s]], channel_multiplier=cm)
                last.then_inc(sig("gp_filled" if k == 0 else "levels"), 1)
            gp.wait_ge(*at("d_done", 2 * NGROUPS))
            for h in range(HC):
                if h >= 4:
                    gp.wait_ge(*at(f"state{h % 4}_written", 16))
                gp.dma_start(s_ring[h % 4], A["state_delta_s"][0, :, h].rearrange("b d e -> d b e"))\
                  .then_inc(sig(f"state{h % 4}_loaded"), 16)

        def softplus(dve, link, out, z, tmp, abs_sig, exp_sig, sign):
            t, s, s2 = tmp
            V.tensor_scalar(out, z, sign, 0.0, ALU.mult, ALU.max)
            link(V.tensor_scalar(s, z, -1.0, None, ALU.mult))
            V.tensor_tensor(t, s, z, ALU.min).then_inc(sig(abs_sig), 1)
            dve.wait_ge(*at(exp_sig, 1))
            link(V.tensor_scalar(s, t, 2.0, None, ALU.add))
            link(V.reciprocal(s, s))
            link(V.tensor_tensor(s, s, t, ALU.mult))
            link(V.tensor_tensor(s2, s, s, ALU.mult))
            link(V.tensor_scalar(t, s2, 1.0 / 17, 1.0 / 15, ALU.mult, ALU.add))
            for k in (13, 11, 9, 7, 5, 3, 1):
                link(V.tensor_tensor(t, t, s2, ALU.mult))
                link(V.tensor_scalar(t, t, 1.0 / k, None, ALU.add))
            link(V.tensor_tensor(t, t, s, ALU.mult))
            link(V.scalar_tensor_tensor(out, t, 2.0, out, ALU.mult, ALU.add))

        def conv(dve, link, out, x, tap, bias, past, tiles, E, done):
            for t in tiles:
                last = E.tensor_scalar(out[:, t, :], x(t), tap(t, HIST), bias(t), ALU.mult, ALU.add)
            link(last)
            for j in range(HIST - 1, -1, -1):
                back = HIST - j
                for t in tiles:
                    E.scalar_tensor_tensor(out[:, t, back:TP], x(t)[:, 0:TP - back], tap(t, j), out[:, t, back:TP],
                                           ALU.mult, ALU.add)
                    last = E.scalar_tensor_tensor(out[:, t, TP:T], past(t, j), tap(t, j), out[:, t, TP:T], ALU.mult, ALU.add)
                if j:
                    link(last)
            last.then_inc(sig(done), 1)

        def norm_act_squares(eng, n, dep):
            eng.wait_ge(*at(*dep))
            SC.activation(inv[:], xT[:], ACT.Square).then_inc(sig(f"norm{n}_sq"), 1)

        def norm_act_root(eng, n):
            eng.wait_ge(*at(f"norm{n}_ss", 1))
            SC.activation(inv[:, 0, 0:TT], bank[4][:, 0:TT], ACT.Sqrt, bias=eps_t[:], scale=1.0 / D)
            SC.activation(inv[0:TS, 0, TT:TT + 1], bank[4][0:TS, TT:TT + 1], ACT.Sqrt, bias=eps_t[0:TS, :], scale=1.0 / D)\
              .then_inc(sig(f"norm{n}_root"), 1)

        def norm_pe(pe, n, between=None):
            pe.wait_ge(*at(f"norm{n}_sq", 1))
            for i, (t0, m) in enumerate(TOK):
                for j in range(KD):
                    last = PE.matmul(bank[4][0:m, i:i + 1], inv[:, j, t0:t0 + m], ones[:, 0:1], start=j == 0, stop=j == KD - 1)
            last.then_inc(sig(f"norm{n}_ss"), 1)
            if between:
                between()
            pe.wait_ge(*at(f"norm{n}_inv", 1))
            for i, (t0, m) in enumerate(TOK):
                last = PE.matmul(bank[4][:, t0:t0 + m], inv[0:m, 0, i:i + 1].broadcast_to([m, P]), ident[0:m, 0:m], start=True, stop=True)
            last.then_inc(sig(f"norm{n}_b"), 1)

        def norm_dve(dve, n, gain, link, between=None):
            dve.wait_ge(*at(f"norm{n}_root", 1))
            V.reciprocal(inv[:, 0, 0:TT], inv[:, 0, 0:TT])
            V.reciprocal(inv[0:TS, 0, TT:TT + 1], inv[0:TS, 0, TT:TT + 1]).then_inc(sig(f"norm{n}_inv"), 1)
            if between:
                between()
            dve.wait_ge(*at(f"norm{n}_b", 1))
            for j in range(KD):
                last = V.scalar_tensor_tensor(hT[:, j, :], xT[:, j, :], col(gain, j), bank[4][:, 0:T], ALU.mult, ALU.mult)
                if n < 3 and j % HALF == HALF - 1:
                    last.then_inc(sig(f"norm{n}_h"), 1)
            if n < 3:
                low_parts(dve, hT, f"norm{n}_hi", f"norm{n}_done")
            else:
                last.then_inc(sig(f"norm{n}_done"), 1)

        HALF = KD // 2

        def high_parts(act_e, src, ready, done, halves=(0, 1)):
            for k, r in enumerate(halves):
                act_e.wait_ge(*at(ready, k + 1))
                SC.activation(h_hi[:, r * HALF:(r + 1) * HALF, :], src[:, r * HALF:(r + 1) * HALF, :], ACT.Copy).then_inc(sig(done), 1)

        def low_parts(dve, src, ready, done, halves=(0, 1)):
            for k, r in enumerate(halves):
                part = slice(r * HALF, (r + 1) * HALF)
                dve.wait_ge(*at(ready, k + 1))
                V.tensor_tensor(h_lo[:, part, :], src[:, part, :], h_hi[:, part, :].bitcast(F32), ALU.subtract).then_inc(sig(done), 1)

        def dense_chunk(pe, name, n, tiles, bank_of, out_sig, before):
            i = place[name, n]
            k, w = dense[i][1:]
            half = k // 2
            for part in range(2):
                p = split_at[i] + part
                pe.wait_ge(*at("lo_done", p + 1))
                hi, lo = (t[:, p % SPLIT, 0:half * w].rearrange("p (j n) -> p j n", j=half) for t in (whi, wlo))
                for c, m in enumerate(tiles):
                    out = bank[bank_of(m)][:, 0:T]
                    if part == 0:
                        before(m)
                    cols_ = slice(c * P, (c + 1) * P)
                    for jj in range(half):
                        j = part * half + jj
                        PE.matmul(out, lo[:, jj, cols_], h_hi[:, j, :], start=j == 0, stop=False)
                        PE.matmul(out, hi[:, jj, cols_], h_lo[:, j, :], start=False, stop=False)
                        last = PE.matmul(out, hi[:, jj, cols_], h_hi[:, j, :], start=False, stop=j == k - 1)
                    if part == 1:
                        last.then_inc(sig(out_sig), 1)
                if part == 0:
                    last.then_inc(sig("piece_used"), 1)
                else:
                    PE.drain().then_inc(sig("piece_used"), 1)

        def dense_pe(pe, name, tiles, out_sig, free_sig, before=()):
            def wait_bank(m):
                for first, event, count in before:
                    if m == first:
                        pe.wait_ge(*at(event, count))
                if m >= 8:
                    pe.wait_ge(*at(free_sig, m - 7))
            per = CHUNK_COLS // P
            for n in range(-(-tiles // per)):
                dense_chunk(pe, name, n, range(n * per, min(tiles, (n + 1) * per)), lambda m: m % 8, out_sig, wait_bank)

        def used(pe):
            PE.drain().then_inc(sig("chunk_used"), 1)

        @block.scalar
        def _(act_e):
            q = act_e
            q.dma_start(x_tok[:, 0:TT, :], A["x_prompt"][0].rearrange("(t p) d -> p t d", p=P)).then_inc(sig("x_loaded"), 16)
            q.dma_start(x_tok[0:TS, TT, :], A["x_sample"].rearrange("b t d -> (b t) d")).then_inc(sig("x_loaded"), 16)
            for load in par_loads[1::2]:
                load(q)
            q.dma_start(w_ba[:], A["w_in_o"][0][:, QKV + D:QKV + D + 2 * HC].rearrange("(j p) n -> p j n", p=P)).then_inc(sig("small_w"), 16)
            q.dma_start(w_router[:], A["router_w"][0].rearrange("(j p) n -> p j n", p=P)).then_inc(sig("small_w"), 16)
            q.dma_start(alog_b[:], A["a_log"].broadcast_to([P, HC])).then_inc(sig("small_w"), 16)
            q.dma_start(dt_b[:], A["dt_bias"].broadcast_to([P, HC])).then_inc(sig("small_w"), 16)
            dense_hi(act_e, 0)
            dense_hi(act_e, 1)
            for j in range(KD):
                act_e.wait_ge(*at("xT_psum", j + 1))
                SC.activation(xT[:, j, :], bank[j % 4][:, 0:T], ACT.Copy).then_inc(sig("xT_done"), 1)
            norm_act_squares(act_e, 0, ("xT_done", KD))
            norm_act_root(act_e, 0)
            high_parts(act_e, hT, "norm0_h", "norm0_hi")
            dense_hi(act_e, 2)
            act_e.wait_ge(*at("lam_abs", 1))
            SC.activation(v_s[0], v_s[0], ACT.Exp).then_inc(sig("lam_absexp"), 1)
            act_e.wait_ge(*at("lam_psum", 1))
            SC.activation(lam_e, bank[5][:, 0:2], ACT.Exp).then_inc(sig("lam_exp"), 1)
            for m in range(IN_E // P):
                if m % 4 == 0:
                    behind(dense_hi, act_e, "w_in_e", m // 4, 0)
                act_e.wait_ge(*at("proj_psum", m + 1))
                SC.activation(proj[:, m, :], bank[m % 8][:, 0:T], ACT.Copy).then_inc(sig("proj_done"), 1)
                if m % 4 == 3:
                    behind(dense_hi, act_e, "w_in_e", m // 4, 1)
                if m == K_ + HB - 1:
                    act_e.wait_ge(*at("proj_done", K_ + HB))
                    SC.activation(inv[:], proj[:, Q_:Q_ + 2 * HB, :], ACT.Square).then_inc(sig("qk_sq"), 1)
            act_e.wait_ge(*at("qk_ss", 1))
            SC.activation(inv[0:NQK, 0, :], bank[4][0:NQK, 0:T], ACT.Sqrt, bias=eps_t[0:NQK, :], scale=1.0 / DH)\
              .then_inc(sig("qk_root"), 1)
            for g, (dst, bias) in enumerate(((gate_x, "lru_bx"), (gate_a, "lru_ba"))):
                for t in range(NL):
                    act_e.wait_ge(*at("lru_gate_psum", g * NL + t + 1))
                    SC.activation(dst[:, t, :], bank[g * NL + t][:, 0:T], ACT.Sigmoid, bias=col(bias, t))\
                      .then_inc(sig("lru_gates"), 1)
            act_e.wait_ge(*at("lru_y", 1))
            SC.activation(decay_a, gate_a, ACT.Exp, scale=-1.0).then_inc(sig("lru_a"), 1)
            SC.activation(tanh_y, gate_a, ACT.Tanh).then_inc(sig("lru_a"), 1)
            SC.activation(proj[:, GATE:GATE + NL, :], proj[:, GATE:GATE + NL, :], ACT.Gelu_apprx_tanh).then_inc(sig("gelu"), 1)
            act_e.wait_ge(*at("lru_m", 1))
            SC.activation(tanh_y, tanh_y, ACT.Sqrt).then_inc(sig("lru_root"), 1)
            high_parts(act_e, mixT, "lru_done", "ya_hi", halves=(0,))
            for i, (s0, n) in enumerate(TOK):
                act_e.wait_ge(*at("ktok_psum", i + 1))
                SC.activation(ktok[0:n, i, :], bank[i][0:n, :], ACT.Copy).then_inc(sig("ktok"), 1)
            for i, (s0, n) in enumerate(TOK):
                act_e.wait_ge(*at("vtok_psum", i + 1))
                SC.activation(vtok[0:n, i, :], bank[3 + i][0:n, :], ACT.Copy).then_inc(sig("vtok"), 1)
            act_e.wait_ge(*at("qs_psum", 1))
            SC.activation(qs_tok, bank[6][0:TS, :], ACT.Copy).then_inc(sig("qs_tok"), 1)
            act_e.wait_ge(*at("tail_psum", 1))
            SC.activation(tail_tok, bank[7][0:TAIL, 0:LW], ACT.Copy).then_inc(sig("tail_tok"), 1)
            outs = (("ktok", 3, ktok, "k_prompt", "k_sample"), ("vtok", 3, vtok, "v_prompt", "v_sample"))
            for s, k, src, a, b in outs:
                act_e.wait_ge(*at(s, k))
                q.dma_start(O[a][0, 0].rearrange("(t p) h e -> p t (h e)", p=P), src[:, 0:TT, :]).then_inc(sig("out_written"), 16)
                q.dma_start(O[b][0, :, 0].rearrange("b h e -> b (h e)"), src[0:TS, TT, :]).then_inc(sig("out_written"), 16)
            act_e.wait_ge(*at("tail_tok", 1))
            q.dma_start(O["lru_conv_prompt"][0, 0], tail_tok[0:HIST, :]).then_inc(sig("out_written"), 16)
            q.dma_start(O["lru_conv_sample"][0, :, HIST - 1, :], tail_tok[HIST:TAIL, :]).then_inc(sig("out_written"), 16)
            q.dma_start(O["lru_conv_sample"][0, :, 0:HIST - 1, :], A["state_lru_conv"][0, :, 1:HIST, :]).then_inc(sig("out_written"), 16)
            act_e.wait_ge(*at("hlast", 1))
            q.dma_start(O["lru_h_prompt"], hl_tok[0:1, :]).then_inc(sig("h_written"), 16)
            q.dma_start(O["lru_h_sample"][0], hl_tok[1:1 + TS, :]).then_inc(sig("h_written"), 16)
            act_e.wait_ge(*at("ss_psum", 1))
            for i in range(2):
                SC.activation(ss[:, i, 0:NP_ * P], bank[4][0:NB, i * NP_ * P:(i + 1) * NP_ * P], ACT.Copy, scale=DH ** -0.5)
            act_e.wait_ge(*at("self_psum", 1))
            SC.activation(ss[:, :, NP_ * P], bank[5][0:NB, 0:2], ACT.Copy, scale=DH ** -0.5).then_inc(sig("ss"), 1)
            act_e.wait_ge(*at("neg_max_s", 1))
            for i in range(2):
                SC.activation(ss[:, i, :], ss[:, i, :], ACT.Exp, bias=mx_s[0:NB, i:i + 1],
                              accum_out=ssum_s[0:NB, i:i + 1]).then_inc(sig("exps_s"), 1)
            for i in range(HH):
                for s, (c0, c1) in enumerate(((0, P), (P, 3 * P))):
                    act_e.wait_ge(*at("neg_max", 1))
                    SC.activation(sc_p[:, i, c0:c1], sc_p[:, i, c0:c1], ACT.Exp, bias=mx[:, s * HH + i:s * HH + i + 1],
                                  accum_out=ssum[:, s * HH + i:s * HH + i + 1]).then_inc(sig("exps"), 1)
            for h in range(HB):
                act_e.wait_ge(*at("pT_psum", h + 1))
                if h >= 2:
                    act_e.wait_ge(*at("pv_psum", h - 1))
                SC.activation(pT[h % 2], bank[h % 2][:, 0:3 * P], ACT.Copy).then_inc(sig("pT"), 1)
                act_e.wait_ge(*at("pv_psum", h + 1))
                SC.activation(mixT[:, NL + h, 0:TP], bank[2 + h % 2][:, 0:TP], ACT.Copy).then_inc(sig("o_prompt"), 1)
            act_e.wait_ge(*at("o_sample", 1))
            act_e.wait_ge(*at("o_prompt", HB))
            SC.activation(osq, mixT[:, NL:NL + HB, :], ACT.Square).then_inc(sig("o_sq"), 1)
            act_e.wait_ge(*at("o_ss", 1))
            SC.activation(osq[0:HB, 0, :], bank[4][0:HB, 0:T], ACT.Sqrt, bias=eps_t[0:HB, :], scale=1.0 / E2).then_inc(sig("o_root"), 1)
            high_parts(act_e, mixT, "mix_done", "mix_hi", halves=(1,))
            for n in range(D // CHUNK_COLS):
                for part in range(2):
                    behind(dense_hi, act_e, "w_out_e", n, part)
            norm_act_squares(act_e, 1, ("out_e_added", KD))
            norm_act_root(act_e, 1)
            high_parts(act_e, hT, "norm1_h", "norm1_hi")
            for m in range(NF):
                if m % 4 == 0:
                    behind(dense_hi, act_e, "ffn_wg", m // 4, 0, FFN_END)
                act_e.wait_ge(*at("ffn_g", m + 1))
                if m >= 4:
                    act_e.wait_ge(*at("ffn_act", m - 3))
                SC.activation(sil[:, m % 4, :], bank[m % 4][:, 0:T], ACT.Silu).then_inc(sig("ffn_sil"), 1)
                if m % 4 == 3 or m == NF - 1:
                    behind(dense_hi, act_e, "ffn_wg", m // 4, 1, FFN_END)
                    behind(dense_hi, act_e, "ffn_wu", m // 4, 0, FFN_END)
                    behind(dense_hi, act_e, "ffn_wu", m // 4, 1, FFN_END)

            act_e.wait_ge(*at("ffn_act", NF))
            act_e.wait_ge(*at("out_written", 16 * 7))
            q.dma_start(dhist_rows, A["state_delta_conv"][0].rearrange("b j c -> (b j) c")).then_inc(sig("dhist_loaded"), 16)
            norm_act_squares(act_e, 2, ("ffn_added", KD))
            dense_hi(act_e, FFN_END)
            dense_hi(act_e, FFN_END + 1)
            norm_act_root(act_e, 2)
            high_parts(act_e, hT, "norm2_h", "norm2_hi")
            dense_hi(act_e, FFN_END + 2)
            act_e.wait_ge(*at("ba_read", 1))
            SC.activation(beta, ba[:, :, 0:HC], ACT.Sigmoid).then_inc(sig("beta"), 1)
            act_e.wait_ge(*at("g_abs", 1))
            SC.activation(sp_t[0], sp_t[0], ACT.Exp).then_inc(sig("g_absexp"), 1)
            SC.activation(alog_b[:], alog_b[:], ACT.Exp).then_inc(sig("ealog"), 1)
            def silu_qkv(m):
                act_e.wait_ge(*at("dconv", m + 1))
                SC.activation(qkvT[:, m, :], qkvT[:, m, :], ACT.Silu).then_inc(sig("qkv"), 1)

            for m in range(NQ + HC):
                if m % 4 == 0:
                    behind(dense_hi, act_e, "w_in_o", m // 4, 0)
                act_e.wait_ge(*at("qkvz_psum", m + 1))
                if m < NQ:
                    if m >= 8:
                        act_e.wait_ge(*at("dconv", m - 7))
                    SC.activation(pre[:, m % 8, :], bank[m % 8][:, 0:T], ACT.Copy).then_inc(sig("pre"), 1)
                    SC.activation(tailT[:, m, :], bank[m % 8][:, T - TAIL:T], ACT.Copy).then_inc(sig("qkvz_read"), 1)
                else:
                    SC.activation(zT[:, m - NQ, :], bank[m % 8][:, 0:T], ACT.Silu).then_inc(sig("qkvz_read"), 1)
                if 4 <= m < NQ + 4:
                    silu_qkv(m - 4)
                if m % 4 == 3:
                    behind(dense_hi, act_e, "w_in_o", m // 4, 1)
                if m == NQ + 3:
                    act_e.wait_ge(*at("qkv", 2 * HC))
                    SC.activation(inv, qkvT[:, 0:HC, :], ACT.Square).then_inc(sig("l2_sq"), 1)
                    SC.activation(hT[:], qkvT[:, HC:2 * HC, :], ACT.Square).then_inc(sig("l2_sq"), 1)
            act_e.wait_ge(*at("l2_ss", 1))
            SC.activation(inv[0:2 * HC, 0, :], bank[4][0:2 * HC, 0:T], ACT.Sqrt, bias=eps_t[0:2 * HC, :]).then_inc(sig("l2_root"), 1)
            act_e.wait_ge(*at("Gt", 1))
            SC.activation(eG, Gt, ACT.Exp).then_inc(sig("eG"), 1)
            for n in range(QKV // CHUNK_COLS):
                act_e.wait_ge(*at("dtail_psum", n + 1))
                SC.activation(tail_rows[:, n * CHUNK_COLS:(n + 1) * CHUNK_COLS], bank[5 + n % 3][0:TAIL, :], ACT.Copy)\
                  .then_inc(sig("dtail"), 1)
            act_e.wait_ge(*at("dtail", QKV // CHUNK_COLS))
            q.dma_start(O["delta_conv_prompt"][0, 0], tail_rows[0:HIST, :]).then_inc(sig("tail_written"), 16)
            q.dma_start(O["delta_conv_sample"][0, :, HIST - 1, :], tail_rows[HIST:TAIL, :]).then_inc(sig("tail_written"), 16)
            q.dma_start(O["delta_conv_sample"][0, :, 0:HIST - 1, :], A["state_delta_conv"][0, :, 1:HIST, :]).then_inc(sig("out_written"), 16)
            def group_sums(n):
                act_e.wait_ge(*at("d_G", n + 1))
                SC.activation(Gb, bank[0][:, :].rearrange("p (h t) -> p h t", h=NG), ACT.Copy).then_inc(sig("d_gb"), 1)

            for n in range(NGROUPS):
                c, h0_ = divmod(n * NG, HC)
                if n == 0:
                    group_sums(0)
                act_e.wait_ge(*at("d_diff", n + 1))
                SC.activation(EA, EA, ACT.Exp, scale=-1.0)
                SC.activation(QK, QK, ACT.Exp)
                if c:
                    act_e.wait_ge(*at("d_gb", n + 1))
                    SC.activation(ge[:, 0:NG], Gb[:, :, P - 1], ACT.Exp)
                    SC.activation(QD, Gb, ACT.Exp)
                SC.activation(kd_s[:, 0:NG], kd_s[:, 0:NG], ACT.Exp).then_inc(sig("d_exp"), 1)
                for l in range(1, LEVELS):
                    for u in range(2):
                        act_e.wait_ge(*at("d_Y", level_half(n, l, u)))
                        SC.activation(Yb[:, halves[u], :], half_of(LV_Y[u], u), ACT.Copy).then_inc(sig("d_Yc"), 1)
                if c:
                    act_e.wait_ge(*at("d_w", n - NGROUPS // TT + 1))
                    SC.activation(NW, bank[1][:, :].rearrange("p (h t) -> p h t", h=NG), ACT.Copy, scale=-1.0).then_inc(sig("d_nw"), 1)
                act_e.wait_ge(*at("d_v", n + 1))
                SC.activation(VN, bank[2][:, :].rearrange("p (h t) -> p h t", h=NG), ACT.Copy).then_inc(sig("d_vn"), 1)
                if n + 1 < NGROUPS:
                    group_sums(n + 1)
                act_e.wait_ge(*at("d_o", n + 1))
                SC.activation(oT[:, h0_:h0_ + NG, c * P:(c + 1) * P], bank[3][:, :].rearrange("p (h t) -> p h t", h=NG), ACT.Copy)\
                  .then_inc(sig("d_done"), 1)
            act_e.wait_ge(*at("d_done", 2 * NGROUPS))
            q.dma_start(O["delta_s_prompt"][0, 0].rearrange("h d e -> d h e"), S_pr).then_inc(sig("sp_written"), 16)
            act_e.wait_ge(*at("s_gb", 1))
            SC.activation(egb[:, 0], bank[0][:, 0:HC * TS].rearrange("p (h b) -> p h b", h=HC), ACT.Exp)
            SC.activation(egb[:, 1], bank[0][:, HC * TS:2 * HC * TS].rearrange("p (h b) -> p h b", h=HC), ACT.Copy).then_inc(sig("s_egb"), 1)
            act_e.wait_ge(*at("s_qk", 1))
            SC.activation(qks, bank[1][:, 0:HC * TS].rearrange("p (h b) -> p h b", h=HC), ACT.Copy).then_inc(sig("s_qks"), 1)
            for h in range(HC):
                act_e.wait_ge(*at("s_state", h + 1))
                q.dma_start(O["delta_s_sample"][0, :, h].rearrange("b d e -> d b e"), s_ring[h % 4]).then_inc(sig(f"state{h % 4}_written"), 16)
            act_e.wait_ge(*at("s_o", HC))
            SC.activation(inv, oT[:], ACT.Square).then_inc(sig("on_sq"), 1)
            act_e.wait_ge(*at("on_ss", 1))
            SC.activation(inv[0:HC, 0, :], bank[4][0:HC, 0:T], ACT.Sqrt, bias=eps_t[0:HC, :], scale=1.0 / DV).then_inc(sig("on_root"), 1)
            high_parts(act_e, oT, "on_done", "on_hi")
            for k in range(4):
                act_e.wait_ge(*at(f"state{k}_written", 32))
            act_e.wait_ge(*at("sp_written", 16))
            act_e.wait_ge(*at("tail_written", 32))
            for n in range(D // CHUNK_COLS):
                for part in range(2):
                    behind(dense_hi, act_e, "w_out_o", n, part)
            norm_act_squares(act_e, 3, ("out_o_added", KD))
            norm_act_root(act_e, 3)
            act_e.wait_ge(*at("top_diff", 1))
            SC.activation(gates[:, 0:TT, 1:2], gates[:, 0:TT, 1:2], ACT.Exp)
            SC.activation(gates[0:TS, TT, 1:2], gates[0:TS, TT, 1:2], ACT.Exp).then_inc(sig("gate_exp"), 1)
            for s, dst in (("xtok", acc), ("htok", h_tok)):
                for i, (t0, n) in enumerate(TOK):
                    for k in range(YC):
                        act_e.wait_ge(*at(s + "_psum", i * YC + k + 1))
                        SC.activation(dst[0:n, i, k * CHUNK_COLS:(k + 1) * CHUNK_COLS],
                                      bank[(i * YC + k) % 4][0:n, :], ACT.Copy).then_inc(sig(s), 1)
            SC.activation(spare[:, 1:2], eps_t[:], ACT.Copy).then_inc(sig("y0_out"), 1)

            def dispatch_out(it, r):
                act_e.wait_ge(*at("moe_disp", it * 2 + r + 1))
                n = KD // 2
                SC.activation(hte_h[:, r * n:(r + 1) * n, :], bank[(7, 3)[r]][:, :].rearrange("p (j t) -> p j t", j=n), ACT.Copy)\
                  .then_inc(sig("hte_hi"), 1)

            def tr_out(it, c):
                act_e.wait_ge(*at("moe_tr", it * NSTEP + c + 1))
                SC.activation(act_h[:, c % 2], bank[4][:, :].rearrange("p (k t) -> p k t", k=KF), ACT.Copy).then_inc(sig("tr_hi"), 1)

            def act_expert(it, more):
                for n, (kind, c, part) in enumerate(order_e):
                    if kind == "g" and part:
                        wait_used(act_e, it, "g", c)
                        SC.activation(m_sil[:, c % 2, :], bank[c % 2 * 2][:, :], ACT.Silu).then_inc(sig("sil"), 1)
                        if c == 0:
                            act_e.wait_ge(*at("moe_w", it + 1))
                            SC.activation(WT, bank[4][:, 0:T], ACT.Copy).then_inc(sig("wt_out"), 1)
                        else:
                            tr_out(it, c - 1)
                    if n == PER - 3:
                        tr_out(it, NSTEP - 1)
                        if more:
                            dispatch_out(it + 1, 0)
                    if n == PER - 1:
                        wait_used(act_e, it, "d", NSTEP - 1)
                        SC.activation(y_e[:, 0:CHUNK_COLS], bank[5][:, :], ACT.Copy).then_inc(sig("y0_out"), 1)
                        if more:
                            dispatch_out(it + 1, 1)
                    if more or n + SPLIT < PER:
                        take_hi(act_e, it, n + SPLIT)

            for r in range(2):
                dispatch_out(0, r)
            with act_e.Fori(0, NE - 1) as e:
                act_expert(e, True)
            act_expert(NE - 1, False)
            with act_e.If(act_e.value_load(count_i[0:1, 0:1], min_val=0, max_val=T) > CAP):
                with act_e.Fori(1, PASSES) as p:
                    with act_e.Fori(0, NE) as e:
                        for n in range(SPLIT):
                            take_hi(act_e, p * NE + e, n)
                        for r in range(2):
                            dispatch_out(p * NE + e, r)
                        act_expert(p * NE + e, False)
            act_e.wait_ge(*at("out_written", OUTS * 16))
            act_e.wait_ge(*at("h_written", 32))

        @block.vector
        def _(dve):
            chain = [0]

            def link(ins):
                chain[0] += 1
                ins.then_inc(sig("dve_chain"), 1)
                dve.wait_ge(*at("dve_chain", chain[0]))

            dve.wait_ge(*at("constants", 2))
            V.memset(pick[:, 2 * HC - 1:2 * HC], 1.0)
            V.tensor_copy(pick2[:, NQK - 2:NQK], half2[:]).then_inc(sig("pick_halves"), 1)
            def parameters():
                dve.wait_ge(*at("par_psum", 1))
                V.tensor_copy(par[:, 0:N_ROWS], bank[5][:, 0:N_ROWS])
                V.tensor_copy(cd[:, 0:N_CD], bank[5][:, P:P + N_CD])
                V.tensor_copy(hist, bank[5][:, 2 * P:2 * P + NL * TS * HIST].rearrange("p (a b c) -> p a b c", a=NL, b=TS))
                link(V.tensor_copy(h0, bank[5][:, 3 * P:3 * P + NL * TS].rearrange("p (a b) -> p a b", a=NL)))
                V.tensor_tensor(lamv, par[:, r_lq:r_lq + 1], par[:, r_lk:r_lk + 1], ALU.mult).then_inc(sig("par_done"), 1)

            dense_lo(dve, 0)
            dense_lo(dve, 1)
            norm_dve(dve, 0, "ln_mix_e", link, parameters)
            dense_lo(dve, 2)
            softplus(dve, link, sp8, par[:, rows["lru_lambda"][0]:rows["lru_lambda"][0] + NL], v_s, "lam_abs", "lam_absexp", -1.0)
            link(V.tensor_scalar(sp8, sp8, RG_C, None, ALU.mult))
            V.tensor_scalar(subg, col("subln_g"), 1.0 - LAM_INIT, None, ALU.mult)
            for n in range(3):
                for part in range(2):
                    behind(dense_lo, dve, "w_in_e", n, part)

            dve.wait_ge(*at("proj_done", XR + NL))
            conv(dve, link, xc, lambda t: proj[:, XR + t, :], lambda t, j: col("conv_lru_w", j * NL + t),
                 lambda t: col("conv_lru_b", t), lambda t, j: hist[:, t, :, j], range(NL), V, "xc_done")
            for n in range(3, 5):
                for part in range(2):
                    behind(dense_lo, dve, "w_in_e", n, part)
            dve.wait_ge(*at("qk_root", 1))
            V.reciprocal(inv[0:NQK, 0, :], inv[0:NQK, 0, :]).then_inc(sig("qk_inv"), 1)
            dve.wait_ge(*at("lru_gates", 2 * NL))
            for t in range(NL):
                last = V.tensor_scalar(gate_a[:, t, :], gate_a[:, t, :], sp8[:, t:t + 1], None, ALU.mult)
            last.then_inc(sig("lru_y"), 1)
            link(V.tensor_tensor(gate_x, gate_x, xc, ALU.mult))
            dve.wait_ge(*at("lru_a", 2))
            link(V.tensor_tensor(tmp_l, decay_a, decay_a, ALU.mult))
            V.scalar_tensor_tensor(tanh_y, tmp_l, 1.0, tanh_y, ALU.add, ALU.mult).then_inc(sig("lru_m"), 1)
            for i in range(2 * HB):
                g = r_gq if i < HB else r_gk
                dve.wait_ge(*at("qk_b", i + 1))
                last = V.scalar_tensor_tensor(proj[:, Q_ + i, :], proj[:, Q_ + i, :], par[:, g:g + 1], bank[i][:, 0:T],
                                              ALU.mult, ALU.mult)
            last.then_inc(sig("qk_done"), 1)
            dve.wait_ge(*at("lru_root", 1))
            link(V.tensor_tensor(gate_x, gate_x, tanh_y, ALU.mult))
            link(V.tensor_tensor(tmp_l[:, :, 0:TS], decay_a[:, :, TP:T], h0, ALU.mult))
            for t in range(NL):
                V.tensor_tensor_scan(xc[:, t, 0:TP], decay_a[:, t, 0:TP], gate_x[:, t, 0:TP], 0.0, ALU.mult, ALU.add)
            link(V.tensor_tensor(xc[:, :, TP:T], gate_x[:, :, TP:T], tmp_l[:, :, 0:TS], ALU.add))
            dve.wait_ge(*at("gelu", 1))
            V.tensor_copy(hl, xc[:, :, TP - 1:T])
            V.tensor_tensor(mixT[:, 0:NL, :], proj[:, GATE:GATE + NL, :], xc, ALU.mult).then_inc(sig("lru_done"), 1)
            low_parts(dve, mixT, "ya_hi", "ya_lo", halves=(0,))
            dve.wait_ge(*at("lam_exp", 1))
            link(V.tensor_tensor(nlam, lam_e[:, 1:2], lam_e[:, 0:1], ALU.subtract))
            link(V.tensor_scalar(nlam, nlam, -LAM_INIT, None, ALU.add))
            dve.wait_ge(*at("hlast_psum", 1))
            V.tensor_copy(hl_tok, bank[7][0:TS + 1, 0:LW]).then_inc(sig("hlast"), 1)

            for b in range(TS):
                dve.wait_ge(*at("qb_psum", b + 1))
                dve.wait_ge(*at(f"kv{b % 4}_loaded", 32 * (b // 4 + 1)))
                if b:
                    dve.wait_ge(*at("k_pages_used", b))
                for g in range(NP_):
                    last = V.tensor_tensor(kv_mul[:, g, :], pages_kv[:, b % 4, g, :], bank[4 + b % 2][:, :], ALU.mult)
                chain[0] += 1
                last.then_inc(sig("dve_chain"), 1)
                dve.wait_ge(*at("dve_chain", chain[0]))
                for g in range(NP_):
                    last = V.reduce_sum(sc_s[:, g, :, :, b].rearrange("p i h -> p h i"),
                                        kv_mul[:, g, :].rearrange("p (h i d) -> p h i d", i=2, d=DH), X)
                last.then_inc(sig("k_pages_used"), 1)
            dve.wait_ge(*at("qk_done", 1))
            V.tensor_tensor(qk_s, proj[:, Q_:Q_ + HB, TP:T], proj[:, K_:K_ + HB, TP:T], ALU.mult).then_inc(sig("qk_self"), 1)
            dve.wait_ge(*at("ss", 1))
            link(V.reduce_max(mx_s[0:NB, :], ss, X))
            V.tensor_scalar(mx_s[0:NB, :], mx_s[0:NB, :], -1.0, None, ALU.mult).then_inc(sig("neg_max_s"), 1)
            dve.wait_ge(*at("exps_s", 2))
            link(V.reciprocal(rsum_s[0:NB, :], ssum_s[0:NB, :]))
            link(V.tensor_tensor(rsum_s[0:NB, 1:2], rsum_s[0:NB, 1:2], nlam[0:NB, :], ALU.mult))
            link(V.tensor_scalar(ss[:, 0, :], ss[:, 0, :], rsum_s[0:NB, 0:1], None, ALU.mult))
            V.scalar_tensor_tensor(ss[:, 0, :], ss[:, 1, :], rsum_s[0:NB, 1:2], ss[:, 0, :], ALU.mult, ALU.add).then_inc(sig("p_s"), 1)
            dve.wait_ge(*at("pT_s_psum", 1))
            V.tensor_copy(pT_s, bank[6][:, 0:NP_ * NB].rearrange("p (g n) -> p g n", g=NP_))
            V.tensor_copy(pself, bank[6][:, NP_ * NB:(NP_ + 1) * NB]).then_inc(sig("pT_s"), 1)
            dve.wait_ge(*at("pT_s", 1))
            link(V.tensor_tensor(pself.rearrange("p (h b) -> p h b", h=HB), pself.rearrange("p (h b) -> p h b", h=HB),
                                 proj[:, V_:V_ + HB, TP:T], ALU.mult))

            for i in range(HH):
                dve.wait_ge(*at("scores_psum", i + 1))
                if i == 0:
                    dve.wait_ge(*at("pT_s_psum", 1))
                    dve.wait_ge(*at("h_written", 32))
                last = V.scalar_tensor_tensor(sc_p[:, i, :], bank[i % 4][:, 0:3 * P], DH ** -0.5, causal[:], ALU.mult, ALU.add)
                last.then_inc(sig("scores"), 1)
            dve.wait_ge(*at("scores", HH))
            V.reduce_max(mx[:, 0:HH], sc_p[:, :, 0:P], X)
            link(V.reduce_max(mx[:, HH:2 * HH], sc_p[:, :, P:3 * P], X))
            V.tensor_scalar(mx, mx, -1.0, None, ALU.mult).then_inc(sig("neg_max"), 1)
            dve.wait_ge(*at("exps", 2 * HH))
            link(V.reciprocal(rsum, ssum))
            r4 = rsum.rearrange("p (s h i) -> p s h i", s=2, i=2)
            link(V.tensor_scalar(r4[:, :, :, 1], r4[:, :, :, 1], nlam, None, ALU.mult))
            seg = ((0, P), (P, 3 * P))
            for h in range(HB):
                for s, (c0, c1) in enumerate(seg):
                    r = s * HH + 2 * h
                    last = V.tensor_scalar(sc_p[:, 2 * h, c0:c1], sc_p[:, 2 * h, c0:c1], rsum[:, r:r + 1], None, ALU.mult)
            link(last)
            for h in range(HB):
                for s, (c0, c1) in enumerate(seg):
                    r = s * HH + 2 * h + 1
                    last = V.scalar_tensor_tensor(sc_p[:, 2 * h, c0:c1], sc_p[:, 2 * h + 1, c0:c1], rsum[:, r:r + 1],
                                                  sc_p[:, 2 * h, c0:c1], ALU.mult, ALU.add)
                last.then_inc(sig("probs"), 1)
            dve.wait_ge(*at("v_pages_used", TS))
            V.tensor_tensor(mixT[:, NL:NL + HB, TP:T], pself.rearrange("p (h b) -> p h b", h=HB),
                            bank[7][:, 0:NB].rearrange("p (h b) -> p h b", h=HB), ALU.add).then_inc(sig("o_sample"), 1)
            dve.wait_ge(*at("o_root", 1))
            V.reciprocal(osq[0:HB, 0, :], osq[0:HB, 0, :]).then_inc(sig("o_inv"), 1)
            for h in range(HB):
                dve.wait_ge(*at("o_b", h + 1))
                last = V.scalar_tensor_tensor(mixT[:, NL + h, :], mixT[:, NL + h, :], subg, bank[h][:, 0:T], ALU.mult, ALU.mult)
            last.then_inc(sig("mix_done"), 1)
            low_parts(dve, mixT, "mix_hi", "mix_lo", halves=(1,))
            for m in range(KD):
                if m % 4 == 0:
                    behind(dense_lo, dve, "w_out_e", m // 4, 0)
                dve.wait_ge(*at("out_e_psum", m + 1))
                V.tensor_tensor(xT[:, m, :], xT[:, m, :], bank[m % 8][:, 0:T], ALU.add).then_inc(sig("out_e_added"), 1)
                if m % 4 == 3:
                    behind(dense_lo, dve, "w_out_e", m // 4, 1)
            norm_dve(dve, 1, "ln_ffn_e", link)
            for m in range(NF):
                if m % 4 == 0:
                    behind(dense_lo, dve, "ffn_wg", m // 4, 0, FFN_END)
                    behind(dense_lo, dve, "ffn_wg", m // 4, 1, FFN_END)
                    behind(dense_lo, dve, "ffn_wu", m // 4, 0, FFN_END)
                dve.wait_ge(*at("ffn_u", m + 1))
                dve.wait_ge(*at("ffn_sil", m + 1))
                V.tensor_tensor(act[:, m, :], sil[:, m % 4, :], bank[4 + m % 4][:, 0:T], ALU.mult).then_inc(sig("ffn_act"), 1)
                if m % 4 == 3 or m == NF - 1:
                    behind(dense_lo, dve, "ffn_wu", m // 4, 1, FFN_END)
            for m in range(KD):
                dve.wait_ge(*at("ffn_d_psum", m + 1))
                V.tensor_tensor(xT[:, m, :], xT[:, m, :], bank[m % 4][:, 0:T], ALU.add).then_inc(sig("ffn_added"), 1)

            def heads(b, n=NG):
                return bank[b][:, 0:n * P].rearrange("p (h t) -> p h t", h=n)

            dve.wait_ge(*at("dhist_psum", 1))
            half = NQ // 2
            for k in range(2):
                last = V.tensor_copy(dhist[:, k * half:(k + 1) * half],
                                     bank[5 + k][:, 0:half * TS * HIST].rearrange("p (a b c) -> p a b c", a=half, b=TS))
            link(last)
            dense_lo(dve, FFN_END)
            dense_lo(dve, FFN_END + 1)
            norm_dve(dve, 2, "ln_mix_o", link)
            dense_lo(dve, FFN_END + 2)
            dve.wait_ge(*at("ba_psum", 1))
            V.tensor_copy(ba[:, 0:TT, :], bank[7][:, 0:TT * 2 * HC].rearrange("p (t c) -> p t c", t=TT))
            V.tensor_copy(ba[0:TS, TT, :], bank[7][0:TS, TT * 2 * HC:NTT * 2 * HC]).then_inc(sig("ba_read"), 1)
            dve.wait_ge(*at("ba_read", 1))
            dve.wait_ge(*at("small_w", 64))
            dve.wait_ge(*at("beta", 1))
            az = ba[:, :, HC:2 * HC]
            link(V.tensor_tensor(az, az, dt_b[:].unsqueeze(1).broadcast_to([P, NTT, HC]), ALU.add))
            softplus(dve, link, g_t, az, sp_t, "g_abs", "g_absexp", 1.0)
            dve.wait_ge(*at("ealog", 1))
            link(V.scalar_tensor_tensor(g_t, g_t, -1.0, alog_b[:].unsqueeze(1).broadcast_to([P, NTT, HC]), ALU.mult, ALU.mult))
            V.tensor_tensor(gd[0:TS, 0], ident[0:TS, 0:TS].unsqueeze(1).broadcast_to([TS, HC, TS]),
                            g_t[0:TS, TT, :].unsqueeze(2).broadcast_to([TS, HC, TS]), ALU.mult)
            V.tensor_tensor(gd[0:TS, 1], ident[0:TS, 0:TS].unsqueeze(1).broadcast_to([TS, HC, TS]),
                            beta[0:TS, TT, :].unsqueeze(2).broadcast_to([TS, HC, TS]), ALU.mult).then_inc(sig("g"), 1)
            behind(dense_lo, dve, "w_in_o", 0, 0)
            for m0 in range(0, NQ, 2):
                behind(dense_lo, dve, "w_in_o", (m0 + 2) // 4, (m0 + 2) % 4 // 2)
                dve.wait_ge(*at("pre", m0 + 2))
                pair = (m0, m0 + 1)

                def tap(m, j):
                    return cd[:, j * NQ + m:j * NQ + m + 1]
                for m in pair:
                    last = V.tensor_scalar(qkvT[:, m, :], pre[:, m % 8, :], tap(m, HIST), None, ALU.mult)
                link(last)
                for j in range(HIST - 1, -1, -1):
                    back = HIST - j
                    for m in pair:
                        x, o = pre[:, m % 8, :], qkvT[:, m, :]
                        V.scalar_tensor_tensor(o[:, back:TP], x[:, 0:TP - back], tap(m, j), o[:, back:TP], ALU.mult, ALU.add)
                        last = V.scalar_tensor_tensor(o[:, TP:T], dhist[:, m, :, j], tap(m, j), o[:, TP:T], ALU.mult, ALU.add)
                        if j == 0:
                            last.then_inc(sig("dconv"), 1)
                    if j:
                        link(last)
            for n in range(NQ * P // CHUNK_COLS, (QKV + D) // CHUNK_COLS):
                for part in range(2):
                    if (n, part) != (NQ * P // CHUNK_COLS, 0):
                        behind(dense_lo, dve, "w_in_o", n, part)
            dve.wait_ge(*at("Gt_psum", 1))
            V.tensor_copy(Gt, bank[0][:, 0:TT * HC].rearrange("p (c h) -> p c h", c=TT)).then_inc(sig("Gt"), 1)
            dve.wait_ge(*at("eG", 1))
            link(V.tensor_tensor(bkb, beta[:, 0:TT, :], eG, ALU.mult))
            dve.wait_ge(*at("l2_root", 1))
            V.reciprocal(inv[0:2 * HC, 0, :], inv[0:2 * HC, 0, :]).then_inc(sig("l2_inv"), 1)
            for i in range(2 * HC):
                dve.wait_ge(*at("l2_b", i + 1))
                V.scalar_tensor_tensor(qkvT[:, i, :], qkvT[:, i, :], DK ** -0.5 if i < HC else 1.0, bank[i % 4][:, 0:T],
                                       ALU.mult, ALU.mult).then_inc(sig("l2_applied"), 1)
            for n in range(NGROUPS):
                c, h0_ = divmod(n * NG, HC)
                hs = range(NG)

                def per_head(v, h):
                    return v[:, c, h0_ + h:h0_ + h + 1]
                dve.wait_ge(*at("d_gb", n + 1))
                if n == 0:
                    dve.wait_ge(*at("levels", 1))
                for h in hs:
                    V.tensor_scalar(EA[:, h, :], Gb[:, h, :], per_head(Gt, h), 0.0, ALU.subtract, ALU.max)
                    V.tensor_scalar(QK[:, h, :], Gb[:, h, :], per_head(Gt, h), 0.0, ALU.subtract, ALU.min)
                V.tensor_tensor(kd_s[:, 0:NG], Gb[:, :, P - 1], Gt[:, c, h0_:h0_ + NG], ALU.subtract).then_inc(sig("d_diff"), 1)
                dve.wait_ge(*at("d_exp", n + 1))
                dve.wait_ge(*at("d_in", n + 1))
                V.tensor_tensor(EA, EA, heads(7), ALU.mult)
                link(V.tensor_tensor(QK, QK, heads(6), ALU.mult))
                for h in hs:
                    last = V.scalar_tensor_tensor(EA[:, h, :], EA[:, h, :], per_head(beta, h), gt_mask[:], ALU.mult, ALU.mult)
                link(last)
                link(V.tensor_tensor(Am, EA, lvl[:, 0, :].unsqueeze(1).broadcast_to([P, NG, P]), ALU.mult))
                V.tensor_tensor(Tm, ident[:].unsqueeze(1).broadcast_to([P, NG, P]), Am, ALU.subtract).then_inc(sig("d_T0"), 1)
                dve.wait_ge(*at("d_T0t", n + 1))
                V.tensor_copy(Tt, heads(5)).then_inc(sig("d_T"), 1)
                dve.wait_ge(*at("d_T0", n + 1))

                def update(l, u):
                    dve.wait_ge(*at("d_D", level_half(n, l, u)))
                    for t, b in ((Tm, LV_M[u]), (Tt, LV_T[u])):
                        if t is Tt or l < LEVELS - 1:
                            last = V.tensor_tensor(t[:, halves[u], :], t[:, halves[u], :], half_of(b, u), ALU.subtract)
                    last.then_inc(sig("d_T"), 1)

                for l in range(1, LEVELS):
                    for u in range(2):
                        if l > 1:
                            dve.wait_ge(*at("d_Y", level_half(n, l - 1, u)))
                        V.tensor_tensor(Am[:, halves[u], :], EA[:, halves[u], :], lvl[:, l, :].unsqueeze(1).broadcast_to([P, NG // 2, P]),
                                        ALU.mult).then_inc(sig("d_Am"), 1)
                    if l > 1:
                        for u in range(2):
                            update(l - 1, u)
                    if l == 1:
                        V.tensor_tensor(QK, QK, le_mask[:].unsqueeze(1).broadcast_to([P, NG, P]), ALU.mult)
                        if c:
                            V.tensor_tensor(QD, QD, qT[:, h0_:h0_ + NG, c * P:(c + 1) * P], ALU.mult)
                    for h in hs:
                        if l == 2:
                            V.tensor_scalar(KDc[:, h, :], bank[3][:, h * P:(h + 1) * P], kd_s[:, h:h + 1], None, ALU.mult)
                        if l == 3:
                            V.tensor_scalar(KB[:, h, :], bank[3][:, h * P:(h + 1) * P], per_head(bkb, h), None, ALU.mult)
                        if l == 4:
                            V.tensor_scalar(VB[:, h, :], bank[4][:, h * P:(h + 1) * P], per_head(beta, h), None, ALU.mult)
                for u in range(2):
                    update(LEVELS - 1, u)
                dve.wait_ge(*at("d_S", n + 1))
                for h in hs:
                    if c:
                        last = V.scalar_tensor_tensor(S_pr[:, h0_ + h, :], S_pr[:, h0_ + h, :], ge[:, h:h + 1],
                                                      bank[4][:, h * P:(h + 1) * P], ALU.mult, ALU.add)
                    else:
                        last = V.tensor_copy(S_pr[:, h0_ + h, :], bank[4][:, h * P:(h + 1) * P])
                last.then_inc(sig("d_done"), 1)
            dve.wait_ge(*at("d_done", 2 * NGROUPS))
            prod = inv[:, 0, 0:HC * TS].rearrange("p (h b) -> p h b", h=HC)
            V.tensor_tensor(prod, qT[:, :, TP:T], kT[:, :, TP:T], ALU.mult).then_inc(sig("s_prod"), 1)
            dve.wait_ge(*at("s_egb", 1))
            dve.wait_ge(*at("s_qks", 1))

            def sample_out(h):
                eg, be = egb[:, 0, h, :], egb[:, 1, h, :]
                vn = vn_s[h % 2]
                dve.wait_ge(*at("s_ks", h + 1))
                qS = bank[2 + h % 2][:, 0:2 * TS].rearrange("p (b k) -> p b k", k=2)[:, :, 0]
                kS = bank[2 + h % 2][:, 0:2 * TS].rearrange("p (b k) -> p b k", k=2)[:, :, 1]
                link(V.tensor_tensor(vn, kS, eg, ALU.mult))
                link(V.tensor_tensor(vn, vT[:, h, TP:T], vn, ALU.subtract))
                link(V.tensor_tensor(vn, vn, be, ALU.mult))
                V.tensor_tensor(vn_t, qS, eg, ALU.mult).then_inc(sig("s_v"), 1)
                link(V.tensor_tensor(prod[:, 0, :], vn, qks[:, h, :], ALU.mult))
                V.tensor_tensor(oT[:, h, TP:T], prod[:, 0, :], vn_t, ALU.add).then_inc(sig("s_o"), 1)

            def sample_outer_in(h):
                dve.wait_ge(*at("s_vt", h + 1))
                if h >= 2:
                    dve.wait_ge(*at("s_outer", h - 1))
                vt = bank[(4, 7)[h % 2]]
                link(V.tensor_copy(k_row[h % 2], vt[0:TS, P:2 * P]))
                V.tensor_tensor(v_diag[h % 2][0:TS], ident[0:TS, 0:TS].unsqueeze(2).broadcast_to([TS, TS, P]),
                                vt[0:TS, 0:P].unsqueeze(1).broadcast_to([TS, TS, P]), ALU.mult).then_inc(sig("s_vd"), 1)
                for b in range(TS):
                    last = V.tensor_scalar(s_ring[h % 4][:, b, :], s_ring[h % 4][:, b, :], egb[:, 0, h, b:b + 1], None, ALU.mult)
                link(last)

            def sample_state(h):
                dve.wait_ge(*at("s_outer", h + 1))
                for k in range(2):
                    n = TS // 2
                    last = V.tensor_tensor(s_ring[h % 4][:, k * n:(k + 1) * n, :], s_ring[h % 4][:, k * n:(k + 1) * n, :],
                                           heads(outer_banks[h % 2][k]), ALU.add)
                last.then_inc(sig("s_state"), 1)

            sample_out(0)
            for h in range(HC):
                if h + 1 < HC:
                    sample_out(h + 1)
                sample_outer_in(h)
                if h:
                    sample_state(h - 1)
            sample_state(HC - 1)
            dve.wait_ge(*at("on_root", 1))
            V.reciprocal(inv[0:HC, 0, :], inv[0:HC, 0, :]).then_inc(sig("on_inv"), 1)
            for h in range(HC):
                dve.wait_ge(*at("on_b", h + 1))
                V.scalar_tensor_tensor(oT[:, h, :], oT[:, h, :], col("onorm_g"), bank[h % 4][:, 0:T], ALU.mult, ALU.mult)\
                 .then_inc(sig("on_applied"), 1)
            dve.wait_ge(*at("on_applied", HC))
            for r in range(2):
                part = slice(r * HALF, (r + 1) * HALF)
                V.tensor_tensor(oT[:, part, :], oT[:, part, :], zT[:, part, :], ALU.mult).then_inc(sig("on_done"), 1)
            low_parts(dve, oT, "on_hi", "on_lo")
            for m in range(KD):
                if m % 4 == 0:
                    behind(dense_lo, dve, "w_out_o", m // 4, 0)
                dve.wait_ge(*at("out_o_psum", m + 1))
                V.tensor_tensor(xT[:, m, :], xT[:, m, :], bank[m % 8][:, 0:T], ALU.add).then_inc(sig("out_o_added"), 1)
                if m % 4 == 3:
                    behind(dense_lo, dve, "w_out_o", m // 4, 1)
            norm_dve(dve, 3, "ln_ffn_o", link)
            dve.wait_ge(*at("iota_psum", 1))
            V.tensor_copy(iota, bank[7][:, 0:P]).then_inc(sig("iota"), 1)
            dve.wait_ge(*at("iota", 1))
            dve.wait_ge(*at("logits_psum", 1))
            for i, (t0, n) in enumerate(TOK):
                last = V.tensor_copy(logit[0:n, i, :], bank[5][0:n, i * NE:(i + 1) * NE])
            link(last)
            for i, (t0, n) in enumerate(TOK):
                last = V.max(top[0:n, i, :], logit[0:n, i, :])
            link(last)
            for i, (t0, n) in enumerate(TOK):
                V.max_index(top_i[0:n, i, :], top[0:n, i, :], logit[0:n, i, :])
                last = V.tensor_tensor(gates[0:n, i, 1:2], top[0:n, i, 1:2], top[0:n, i, 0:1], ALU.subtract)
            last.then_inc(sig("top_diff"), 1)
            dve.wait_ge(*at("gate_exp", 1))
            for i, (t0, n) in enumerate(TOK):
                V.tensor_copy(idx_f[0:n, i, :], top_i[0:n, i, 0:2])
                last = V.tensor_scalar(gates[0:n, i, 0:1], gates[0:n, i, 1:2], 1.0, None, ALU.add)
            link(last)
            for i, (t0, n) in enumerate(TOK):
                last = V.reciprocal(gates[0:n, i, 0:1], gates[0:n, i, 0:1])
            link(last)
            for i, (t0, n) in enumerate(TOK):
                last = V.tensor_tensor(gates[0:n, i, 1:2], gates[0:n, i, 1:2], gates[0:n, i, 0:1], ALU.mult)
            link(last)
            for i, (t0, n) in enumerate(TOK):
                io = iota[0:n, 0:NE]
                V.tensor_scalar(mask[0:n, i, :], io, idx_f[0:n, i, 0:1], None, ALU.is_equal)
                V.tensor_scalar(comb[0:n, i, :], io, idx_f[0:n, i, 0:1], gates[0:n, i, 0:1], ALU.is_equal, ALU.mult)
                last = V.tensor_scalar(comb2[0:n, i, :], io, idx_f[0:n, i, 1:2], gates[0:n, i, 1:2], ALU.is_equal, ALU.mult)
            link(last)
            for i, (t0, n) in enumerate(TOK):
                V.tensor_tensor(comb[0:n, i, :], comb[0:n, i, :], comb2[0:n, i, :], ALU.add)
                last = V.scalar_tensor_tensor(mask[0:n, i, :], iota[0:n, 0:NE], idx_f[0:n, i, 1:2], mask[0:n, i, :], ALU.is_equal, ALU.add)
            last.then_inc(sig("masks"), 1)
            dve.wait_ge(*at("ranks_psum", 1))
            V.reduce_max(count, bank[6][:, NTT * NE:(NTT + 1) * NE], X)
            for i, (t0, n) in enumerate(TOK):
                last = V.scalar_tensor_tensor(rank[0:n, i, :], mask[0:n, i, :], -FAR, bank[6][0:n, i * NE:(i + 1) * NE], ALU.mult, ALU.add)
            link(last)
            for i, (t0, n) in enumerate(TOK):
                last = V.tensor_scalar(rank[0:n, i, :], rank[0:n, i, :], FAR, None, ALU.add)
            last.then_inc(sig("ranks"), 1)
            V.tensor_copy(count_i, count).then_inc(sig("flag"), 1)
            dve.wait_ge(*at("flag", 1))
            for i, (name, k) in enumerate((("act_done", 2), ("tr_out", 1), ("y1_out", 1), ("added", NTT * YC))):
                V.memset(spare[:, 2 + i:3 + i], 0.0).then_inc(sig(name), k)

            def column(v, i, n, e):
                return v[0:n, i, e:e + 1] if isinstance(e, int) else v[0:n, i, bass.ds(e, 1)]

            def select(e):
                for i, (t0, n) in enumerate(TOK):
                    V.tensor_scalar(sel[0:n, i, :], iota[0:n, 0:CAP], column(rank, i, n, e), None, ALU.is_equal)
                    last = V.tensor_scalar(selw[0:n, i, :], iota[0:n, 0:CAP], column(rank, i, n, e), column(comb, i, n, e),
                                           ALU.is_equal, ALU.mult)
                last.then_inc(sig("sel"), 1)

            def hte_lo(it, r):
                dve.wait_ge(*at("hte_hi", it * 2 + r + 1))
                n = KD // 2
                V.tensor_tensor(hte_l[:, r * n:(r + 1) * n, :], bank[(7, 3)[r]][:, :].rearrange("p (j t) -> p j t", j=n),
                                hte_h[:, r * n:(r + 1) * n, :].bitcast(F32), ALU.subtract).then_inc(sig("hte"), 1)

            def tr_lo(it, c):
                dve.wait_ge(*at("tr_hi", it * NSTEP + c + 1))
                V.tensor_tensor(act_l[:, c % 2], bank[4][:, :].rearrange("p (k t) -> p k t", k=KF), act_h[:, c % 2].bitcast(F32),
                                ALU.subtract).then_inc(sig("tr_out"), 1)

            def dve_expert(it, more, e_next):
                for n, (kind, c, part) in enumerate(order_e):
                    if kind == "g" and part and c:
                        tr_lo(it, c - 1)
                    if kind == "u" and part:
                        dve.wait_ge(*at("sil", it * NSTEP + c + 1))
                        wait_used(dve, it, "u", c)
                        V.tensor_tensor(m_act[:, c % 2, :], m_sil[:, c % 2, :], bank[c % 2 * 2 + 1][:, :], ALU.mult).then_inc(sig("act_done"), 1)
                        if c == 2 and more:
                            dve.wait_ge(*at("moe_w", it + 1))
                            select(e_next)
                    if n == PER - 3:
                        tr_lo(it, NSTEP - 1)
                        if more:
                            hte_lo(it + 1, 0)
                    if n == PER - 1:
                        wait_used(dve, it, "d", NSTEP - 1)
                        V.tensor_copy(y_e[:, CHUNK_COLS:D], bank[6][:, :]).then_inc(sig("y1_out"), 1)
                        if more:
                            hte_lo(it + 1, 1)
                    if more or n + SPLIT < PER:
                        take_lo(dve, it, n + SPLIT)
                for k in range(NTT * YC):
                    i, hf = divmod(k, YC)
                    n = TOK[i][1]
                    a = acc[0:n, i, hf * CHUNK_COLS:(hf + 1) * CHUNK_COLS]
                    dve.wait_ge(*at("moe_c", it * (NTT * YC) + k + 1))
                    V.tensor_tensor(a, a, bank[(7, 3, 2)[k % 3]][0:n, :], ALU.add).then_inc(sig("added"), 1)

            select(0)
            for r in range(2):
                hte_lo(0, r)
            dve.wait_ge(*at("xtok", NTT * YC))
            with dve.Fori(0, NE - 1) as e:
                dve_expert(e, True, e + 1)
            dve_expert(NE - 1, False, 0)
            with dve.If(dve.value_load(count_i[0:1, 0:1], min_val=0, max_val=T) > CAP):
                with dve.Fori(1, PASSES) as p:
                    dve.wait_ge(*at("moe_w", p * NE))
                    for i, (t0, n) in enumerate(TOK):
                        last = V.tensor_scalar(rank[0:n, i, :], rank[0:n, i, :], float(-CAP), None, ALU.add)
                    last.then_inc(sig("rank_pass"), 1)
                    with dve.Fori(0, NE) as e:
                        dve.wait_ge(*at("rank_pass", p))
                        dve.wait_ge(*at("moe_w", p * NE + e))
                        select(e)
                        for n in range(SPLIT):
                            take_lo(dve, p * NE + e, n)
                        for r in range(2):
                            hte_lo(p * NE + e, r)
                        dve_expert(p * NE + e, False, 0)
            V.memset(spare[:, 6:7], 0.0).then_inc(sig("y_ready"), 1)

        @block.tensor
        def _(pe):
            pe.wait_ge(*at("constants", 2))
            pe.wait_ge(*at("x_loaded", 32))
            for j in range(KD):
                if j >= 4:
                    pe.wait_ge(*at("xT_done", j - 3))
                for i, (t0, n) in enumerate(TOK):
                    last = PE.transpose(bank[j % 4][:, t0:t0 + n], x_tok[0:n, i, j * P:(j + 1) * P], ident[0:n, 0:n])
                last.then_inc(sig("xT_psum"), 1)
            def parameters():
                pe.wait_ge(*at("par_loaded", 16 * N_PAR))
                PE.transpose(bank[5][:, 0:N_ROWS], par_rows[0:N_ROWS, :], ident[0:N_ROWS, 0:N_ROWS])
                PE.transpose(bank[5][:, P:P + N_CD], cd_rows[0:N_CD, :], ident[0:N_CD, 0:N_CD])
                n = TS * HIST
                for t in range(NL):
                    PE.transpose(bank[5][:, 2 * P + t * n:2 * P + (t + 1) * n], hist_rows[:, t * P:(t + 1) * P], ident[0:n, 0:n])
                    last = PE.transpose(bank[5][:, 3 * P + t * TS:3 * P + (t + 1) * TS], h0_rows[:, t * P:(t + 1) * P],
                                        ident[0:TS, 0:TS])
                last.then_inc(sig("par_psum"), 1)

            norm_pe(pe, 0, parameters)
            pe.wait_ge(*at("norm0_done", 2))
            PE.matmul(bank[5][:, 0:2], lamv.broadcast_to([P, P]), half2[:], start=True, stop=True).then_inc(sig("lam_psum"), 1)
            dense_pe(pe, "w_in_e", IN_E // P, "proj_psum", "proj_done", before=((5, "lam_exp", 1),))
            pe.wait_ge(*at("qk_sq", 1))
            pe.wait_ge(*at("pick_halves", 1))
            for i in range(2 * HB):
                last = PE.matmul(bank[4][0:NQK, 0:T], pick2[:, NQK - 2 - 2 * i:2 * NQK - 2 - 2 * i], inv[:, i, :],
                                 start=i == 0, stop=i == 2 * HB - 1)
            last.then_inc(sig("qk_ss"), 1)
            pe.wait_ge(*at("proj_done", IN_E // P))
            pe.wait_ge(*at("xc_done", 1))
            pe.wait_ge(*at("lru_w_loaded", 64))
            for g in range(2):
                if g:
                    pe.wait_ge(*at("qk_root", 1))
                for t in range(NL):
                    PE.matmul(bank[g * NL + t][:, 0:T], lru_w[:, g, t, :], xc[:, t, :], start=True, stop=True)\
                      .then_inc(sig("lru_gate_psum"), 1)
            pe.wait_ge(*at("qk_inv", 1))
            pe.wait_ge(*at("spread_made", 1))
            pe.wait_ge(*at("lru_gates", 2 * NL))
            for i in range(2 * HB):
                PE.matmul(bank[i][:, 0:T], spread[:, i * P:(i + 1) * P], inv[0:NQK, 0, :], start=True, stop=True).then_inc(sig("qk_b"), 1)
            pe.wait_ge(*at("lru_done", 1))
            pe.wait_ge(*at("qk_done", 1))
            for i, (t0, n) in enumerate(TOK):
                for h in range(HB):
                    last = PE.transpose(bank[i][0:n, h * P:(h + 1) * P], proj[:, K_ + h, t0:t0 + n], ident[:])
                last.then_inc(sig("ktok_psum"), 1)
            for i, (t0, n) in enumerate(TOK):
                for h in range(HB):
                    last = PE.transpose(bank[3 + i][0:n, h * P:(h + 1) * P], proj[:, V_ + h, t0:t0 + n], ident[:])
                last.then_inc(sig("vtok_psum"), 1)
            for h in range(HB):
                last = PE.transpose(bank[6][0:TS, h * P:(h + 1) * P], proj[:, Q_ + h, TP:T], ident[:])
            last.then_inc(sig("qs_psum"), 1)
            for t in range(NL):
                last = PE.transpose(bank[7][0:TAIL, t * P:(t + 1) * P], proj[:, XR + t, T - TAIL:T], ident[:])
            last.then_inc(sig("tail_psum"), 1)
            pe.wait_ge(*at("tail_tok", 1))
            for t in range(NL):
                last = PE.transpose(bank[7][0:TS + 1, t * P:(t + 1) * P], hl[:, t, :], ident[:])
            last.then_inc(sig("hlast_psum"), 1)
            pe.wait_ge(*at("vtok", 3))
            pe.wait_ge(*at("qs_tok", 1))
            for b in range(TS):
                if b >= 2:
                    pe.wait_ge(*at("k_pages_used", b - 1))
                PE.matmul(bank[4 + b % 2][:, 0:AW], ident[0:TS, b:b + 1].broadcast_to([TS, P]), qs_tok, start=True, stop=True)\
                  .then_inc(sig("qb_psum"), 1)
            pe.wait_ge(*at("k_pages_used", TS))
            for i in range(2):
                for g in range(NP_):
                    c = (i * NP_ + g) * P
                    last = PE.transpose(bank[4][0:NB, c:c + P], sc_s[:, g, i].rearrange("p h b -> p (h b)"), ident[:])
            last.then_inc(sig("ss_psum"), 1)
            pe.wait_ge(*at("qk_self", 1))
            PE.matmul(bank[5][0:NB, 0:2], qk_s.rearrange("p h b -> p (h b)"), half2[:], start=True, stop=True).then_inc(sig("self_psum"), 1)
            pe.wait_ge(*at("p_s", 1))
            for g in range(NP_):
                PE.transpose(bank[6][:, g * NB:(g + 1) * NB], ss[:, 0, g * P:(g + 1) * P], ident[0:NB, 0:NB])
            PE.matmul(bank[6][:, NP_ * NB:(NP_ + 1) * NB], ss[:, 0, NP_ * P:NP_ * P + 1].broadcast_to([NB, P]), ident[0:NB, 0:NB],
                      start=True, stop=True).then_inc(sig("pT_s_psum"), 1)
            pe.wait_ge(*at("pT_s", 1))
            pe.wait_ge(*at("hlast", 1))

            def sample_values(b):
                n = TS + b
                pe.wait_ge(*at(f"kv{n % 4}_loaded", 32 * (n // 4 + 1)))
                for h in range(HB):
                    o = bank[7][:, h * TS + b:h * TS + b + 1]
                    for g in range(NP_):
                        last = PE.matmul(o, pages_kv[:, n % 4, g, h * P:(h + 1) * P], pT_s[:, g, h * TS + b:h * TS + b + 1],
                                         start=g == 0, stop=g == NP_ - 1)
                last.then_inc(sig("v_pages_used"), 1)

            for i in range(HH):
                h, k = divmod(i, 2)
                rows_ = slice(k * DH, (k + 1) * DH)
                if i >= 4:
                    pe.wait_ge(*at("scores", i - 3))
                PE.matmul(bank[i % 4][:, 0:P], proj[rows_, Q_ + h, 0:P], proj[rows_, K_ + h, 0:P], start=True, stop=True)
                PE.matmul(bank[i % 4][:, P:3 * P], proj[rows_, Q_ + h, P:2 * P], proj[rows_, K_ + h, 0:2 * P],
                          start=True, stop=True).then_inc(sig("scores_psum"), 1)
            for b in range(4):
                sample_values(b)
            pe.wait_ge(*at("scores", HH))
            for h in range(HB):
                pe.wait_ge(*at("probs", h + 1))
                if h >= 2:
                    pe.wait_ge(*at("pT", h - 1))
                    pe.wait_ge(*at("o_prompt", h - 1))
                for c in range(3):
                    last = PE.transpose(bank[h % 2][:, c * P:(c + 1) * P], sc_p[:, 2 * h, c * P:(c + 1) * P], ident[:])
                last.then_inc(sig("pT_psum"), 1)
                pe.wait_ge(*at("pT", h + 1))
                o = bank[2 + h % 2]
                v = [vtok[:, i, h * P:(h + 1) * P] for i in range(TT)]
                PE.matmul(o[:, 0:P], v[0], pT[h % 2][:, 0:P], start=True, stop=True)
                PE.matmul(o[:, P:2 * P], v[0], pT[h % 2][:, P:2 * P], start=True, stop=False)
                PE.matmul(o[:, P:2 * P], v[1], pT[h % 2][:, 2 * P:3 * P], start=False, stop=True).then_inc(sig("pv_psum"), 1)
            for b in range(4, TS):
                sample_values(b)
            pe.wait_ge(*at("o_sq", 1))
            for h in range(HB):
                last = PE.matmul(bank[4][0:HB, 0:T], pick[:, 2 * HC - 1 - h:2 * HC - 1 - h + HB], osq[:, h, :],
                                 start=h == 0, stop=h == HB - 1)
            last.then_inc(sig("o_ss"), 1)
            pe.wait_ge(*at("o_inv", 1))
            for h in range(HB):
                PE.matmul(bank[h][:, 0:T], ident[0:HB, h:h + 1].broadcast_to([HB, P]), osq[0:HB, 0, :],
                          start=True, stop=True).then_inc(sig("o_b"), 1)
            pe.wait_ge(*at("mix_lo", 1))
            dense_pe(pe, "w_out_e", KD, "out_e_psum", "out_e_added")
            norm_pe(pe, 1)
            pe.wait_ge(*at("norm1_done", 2))
            for n in range(NFC):
                tiles = range(n * (CHUNK_COLS // P), min(NF, (n + 1) * (CHUNK_COLS // P)))
                for name, s, b0, free in (("ffn_wg", "ffn_g", 0, "ffn_sil"), ("ffn_wu", "ffn_u", 4, "ffn_act")):
                    def wait_bank(m):
                        if m >= 4:
                            pe.wait_ge(*at(free, m - 3))
                    dense_chunk(pe, name, n, tiles, lambda m: b0 + m % 4, s, wait_bank)
            pe.wait_ge(*at("ffn_act", NF))
            for m in range(KD):
                wait_chunk(pe, place["ffn_wd", m])
                if m >= 4:
                    pe.wait_ge(*at("ffn_added", m - 3))
                for j in range(NF):
                    last = PE.matmul(bank[m % 4][:, 0:T], chunk("ffn_wd", m)[:, j, :], act[:, j, :],
                                     start=j == 0, stop=j == NF - 1)
                last.then_inc(sig("ffn_d_psum"), 1)
                used(pe)

            pe.wait_ge(*at("dhist_loaded", 16))
            n = TS * HIST
            for m in range(NQ):
                k, t = divmod(m, NQ // 2)
                last = PE.transpose(bank[5 + k][:, t * n:(t + 1) * n], dhist_rows[:, m * P:(m + 1) * P], ident[0:n, 0:n])
            last.then_inc(sig("dhist_psum"), 1)
            norm_pe(pe, 2)
            pe.wait_ge(*at("norm2_done", 2))
            pe.wait_ge(*at("small_w", 64))
            for i, (t0, n) in enumerate(TOK):
                for j in range(KD):
                    last = PE.matmul(bank[7][0:n, i * 2 * HC:(i + 1) * 2 * HC], hT[:, j, t0:t0 + n], w_ba[:, j, :],
                                     start=j == 0, stop=j == KD - 1)
            last.then_inc(sig("ba_psum"), 1)
            dense_pe(pe, "w_in_o", NQ + HC, "qkvz_psum", "qkvz_read", before=((7, "ba_read", 1),))
            pe.wait_ge(*at("qkvz_read", NQ + HC))
            pe.wait_ge(*at("g", 1))
            PE.matmul(bank[0][:, 0:TT * HC], le_mask[:], g_t[:, 0:TT, :].rearrange("p c h -> p (c h)"), start=True, stop=True)\
              .then_inc(sig("Gt_psum"), 1)
            for r, src in enumerate((inv, hT)):
                pe.wait_ge(*at("l2_sq", r + 1))
                for i in range(HC):
                    k = r * HC + i
                    last = PE.matmul(bank[4][0:2 * HC, 0:T], pick[:, 2 * HC - 1 - k:4 * HC - 1 - k], src[:, i, :],
                                     start=k == 0, stop=k == 2 * HC - 1)
            last.then_inc(sig("l2_ss"), 1)
            for n in range(QKV // CHUNK_COLS):
                if n >= 3:
                    pe.wait_ge(*at("dtail", n - 2))
                for k in range(CHUNK_COLS // P):
                    m = n * (CHUNK_COLS // P) + k
                    last = PE.transpose(bank[5 + n % 3][0:TAIL, k * P:(k + 1) * P], tailT[:, m, :], ident[:])
                last.then_inc(sig("dtail_psum"), 1)
            pe.wait_ge(*at("l2_inv", 1))
            for i in range(2 * HC):
                if i >= 4:
                    pe.wait_ge(*at("l2_applied", i - 3))
                PE.matmul(bank[i % 4][:, 0:T], ident[0:2 * HC, i:i + 1].broadcast_to([2 * HC, P]), inv[0:2 * HC, 0, :],
                          start=True, stop=True).then_inc(sig("l2_b"), 1)
            pe.wait_ge(*at("l2_applied", 2 * HC))
            pe.wait_ge(*at("dtail", QKV // CHUNK_COLS))
            hs = range(NG)

            def hb(b, h):
                return bank[b][:, h * P:(h + 1) * P]

            def group_products(n):
                c, h0_ = divmod(n * NG, HC)
                tc = slice(c * P, (c + 1) * P)
                for h in hs:
                    last = PE.matmul(hb(0, h), g_t[:, c, h0_ + h:h0_ + h + 1].broadcast_to([P, P]), le_mask[:], start=True, stop=True)
                last.then_inc(sig("d_G"), 1)
                for h in hs:
                    PE.matmul(hb(7, h), kT[:, h0_ + h, tc], kT[:, h0_ + h, tc], start=True, stop=True)
                for h in hs:
                    PE.matmul(hb(6, h), kT[:, h0_ + h, tc], qT[:, h0_ + h, tc], start=True, stop=True)

            group_products(0)
            for n in range(NGROUPS):
                c, h0_ = divmod(n * NG, HC)
                tc = slice(c * P, (c + 1) * P)
                if n:
                    pe.wait_ge(*at("d_done", 2 * n))
                for h in hs:
                    PE.transpose(hb(3, h), kT[:, h0_ + h, tc], ident[:])
                for h in hs:
                    last = PE.transpose(hb(4, h), vT[:, h0_ + h, tc], ident[:])
                last.then_inc(sig("d_in"), 1)
                pe.wait_ge(*at("d_T0", n + 1))
                for h in hs:
                    last = PE.transpose(hb(5, h), Tm[:, h, :], ident[:])
                last.then_inc(sig("d_T0t"), 1)
                for l in range(1, LEVELS):
                    for u in range(2):
                        pe.wait_ge(*at("d_Am", level_half(n, l, u)))
                        pe.wait_ge(*at("d_T", n * (2 * LEVELS - 1) + 1 + (2 * (l - 2) + u + 1 if l > 1 else 0)))
                        for h in hs[halves[u]]:
                            last = PE.matmul(hb(LV_Y[u], h), Am[:, h, :], Tt[:, h, :], start=True, stop=True)
                        last.then_inc(sig("d_Y"), 1)
                    for u in range(2):
                        pe.wait_ge(*at("d_Yc", level_half(n, l, u)))
                        for h in hs[halves[u]]:
                            last = PE.matmul(hb(LV_T[u], h), Tm[:, h, :], Yb[:, h, :], start=True, stop=True)
                        if l < LEVELS - 1:
                            for h in hs[halves[u]]:
                                last = PE.matmul(hb(LV_M[u], h), Yb[:, h, :], Tm[:, h, :], start=True, stop=True)
                        last.then_inc(sig("d_D"), 1)
                pe.wait_ge(*at("d_T", (n + 1) * (2 * LEVELS - 1)))
                if c:
                    for h in hs:
                        last = PE.matmul(hb(1, h), KB[:, h, :], Tt[:, h, :], start=True, stop=True)
                    last.then_inc(sig("d_w"), 1)
                    pe.wait_ge(*at("d_nw", n - NGROUPS // TT + 1))
                for h in hs:
                    last = PE.matmul(hb(2, h), Tt[:, h, :], VB[:, h, :], start=True, stop=not c)
                    if c:
                        last = PE.matmul(hb(2, h), NW[:, h, :], S_pr[:, h0_ + h, :], start=False, stop=True)
                last.then_inc(sig("d_v"), 1)
                if n + 1 < NGROUPS:
                    group_products(n + 1)
                pe.wait_ge(*at("d_vn", n + 1))
                for h in hs:
                    last = PE.matmul(hb(3, h), VN[:, h, :], QK[:, h, :], start=True, stop=not c)
                    if c:
                        last = PE.matmul(hb(3, h), S_pr[:, h0_ + h, :], QD[:, h, :], start=False, stop=True)
                last.then_inc(sig("d_o"), 1)
                for h in hs:
                    last = PE.matmul(hb(4, h), KDc[:, h, :], VN[:, h, :], start=True, stop=True)
                last.then_inc(sig("d_S"), 1)
            pe.wait_ge(*at("d_done", 2 * NGROUPS))
            PE.matmul(bank[0][:, 0:2 * HC * TS], ones[0:TS, :], gd[0:TS].rearrange("p a b c -> p (a b c)"), start=True, stop=True)\
              .then_inc(sig("s_gb"), 1)
            pe.wait_ge(*at("s_prod", 1))
            PE.matmul(bank[1][:, 0:HC * TS], ones[:], inv[:, 0, 0:HC * TS], start=True, stop=True).then_inc(sig("s_qk"), 1)

            def state_products(h):
                pe.wait_ge(*at(f"state{h % 4}_loaded", 16 * (h // 4 + 1)))
                if h >= 2:
                    pe.wait_ge(*at("s_o", h - 1))
                for b in range(TS):
                    last = PE.matmul(bank[2 + h % 2][:, 2 * b:2 * b + 2], s_ring[h % 4][:, b, :],
                                     qkvT[:, h:h + HC + 1:HC, TP + b], start=True, stop=True)
                last.then_inc(sig("s_ks"), 1)

            def state_rows(h):
                pe.wait_ge(*at("s_v", h + 1))
                if h >= 2:
                    pe.wait_ge(*at("s_vd", h - 1))
                vt = bank[(4, 7)[h % 2]]
                PE.transpose(vt[0:TS, 0:P], vn_s[h % 2], ident[:])
                PE.transpose(vt[0:TS, P:2 * P], kT[:, h, TP:T], ident[:]).then_inc(sig("s_vt"), 1)

            def state_outer(h):
                pe.wait_ge(*at("s_vd", h + 1))
                if h >= 2:
                    pe.wait_ge(*at("s_state", h - 1))
                for k in range(2):
                    n = TS // 2
                    last = PE.matmul(bank[outer_banks[h % 2][k]][:, :], k_row[h % 2],
                                     v_diag[h % 2][0:TS, k * n:(k + 1) * n, :].rearrange("p b e -> p (b e)"), start=True, stop=True)
                last.then_inc(sig("s_outer"), 1)

            state_products(0)
            for h in range(HC):
                if h + 1 < HC:
                    state_products(h + 1)
                state_rows(h)
                if h:
                    state_outer(h - 1)
            state_outer(HC - 1)
            pe.wait_ge(*at("on_sq", 1))
            for i in range(HC):
                last = PE.matmul(bank[4][0:HC, 0:T], pick[:, 2 * HC - 1 - i:3 * HC - 1 - i], inv[:, i, :],
                                 start=i == 0, stop=i == HC - 1)
            last.then_inc(sig("on_ss"), 1)
            pe.wait_ge(*at("on_inv", 1))
            for h in range(HC):
                if h >= 4:
                    pe.wait_ge(*at("on_applied", h - 3))
                PE.matmul(bank[h % 4][:, 0:T], ident[0:HC, h:h + 1].broadcast_to([HC, P]), inv[0:HC, 0, :],
                          start=True, stop=True).then_inc(sig("on_b"), 1)
            pe.wait_ge(*at("on_lo", 2))
            dense_pe(pe, "w_out_o", KD, "out_o_psum", "out_o_added")
            norm_pe(pe, 3)
            pe.wait_ge(*at("norm3_done", 1))
            PE.matmul(bank[7][:, 0:P], ones[:], lt_mask[:], start=True, stop=True).then_inc(sig("iota_psum"), 1)
            for i, (t0, n) in enumerate(TOK):
                for j in range(KD):
                    last = PE.matmul(bank[5][0:n, i * NE:(i + 1) * NE], hT[:, j, t0:t0 + n], w_router[:, j, :],
                                     start=j == 0, stop=j == KD - 1)
            last.then_inc(sig("logits_psum"), 1)
            for s, src in (("xtok", xT), ("htok", hT)):
                for i, (t0, n) in enumerate(TOK):
                    for k in range(YC):
                        r = i * YC + k
                        if r >= 4:
                            pe.wait_ge(*at(s, r - 3))
                        elif s == "htok":
                            pe.wait_ge(*at("xtok", NTT * YC))
                        for m in range(KF):
                            last = PE.transpose(bank[r % 4][0:n, m * P:(m + 1) * P], src[:, k * KF + m, t0:t0 + n], ident[:])
                        last.then_inc(sig(s + "_psum"), 1)
            pe.wait_ge(*at("masks", 1))
            for i, (t0, n) in enumerate(TOK):
                for u in range(i + 1):
                    m = TOK[u][1]
                    PE.matmul(bank[6][0:n, i * NE:(i + 1) * NE], (lt_mask if u == i else ones)[0:m, 0:n], mask[0:m, u, :],
                              start=u == 0, stop=u == i)
            for u in range(NTT):
                m = TOK[u][1]
                last = PE.matmul(bank[6][:, NTT * NE:(NTT + 1) * NE], ones[0:m, :], mask[0:m, u, :], start=u == 0, stop=u == NTT - 1)
            last.then_inc(sig("ranks_psum"), 1)
            pe.wait_ge(*at("htok", NTT * YC))
            pe.wait_ge(*at("flag", 1))

            def dispatch(it, r):
                pe.wait_ge(*at("sel", it + 1))
                for jj in range(KD // 2):
                    j = r * (KD // 2) + jj
                    for i, (t0, n) in enumerate(TOK):
                        last = PE.matmul(bank[(7, 3)[r]][:, jj * CAP:(jj + 1) * CAP], h_tok[0:n, i, j * P:(j + 1) * P],
                                         sel[0:n, i, :], start=i == 0, stop=i == NTT - 1)
                last.then_inc(sig("moe_disp"), 1)

            def transposes(it, c):
                pe.wait_ge(*at("act_done", it * NSTEP + c + 3))
                pe.wait_ge(*at("tr_out", it * NSTEP + c + 1))
                if c == 0:
                    pe.wait_ge(*at("wt_out", it + 1))
                for k in range(KF):
                    last = PE.transpose(bank[4][:, k * P:(k + 1) * P], m_act[:, c % 2, k * P:(k + 1) * P], ident[:])
                last.then_inc(sig("moe_tr"), 1)

            def split_piece(it, kind, c, part):
                n = e_at[kind, c, part]
                pe.wait_ge(*at("lo_done", it * PER + (NDP + n + 1)))
                return (piece_view(whi[:, (NDP + n) % SPLIT, :], kind),
                        piece_view(wlo[:, (NDP + n) % SPLIT, :], kind))

            def product(it, kind, c, out):
                for part in range(2):
                    hi, lo = split_piece(it, kind, c, part)
                    for jj in range(KD // 2):
                        j = part * (KD // 2) + jj
                        PE.matmul(out, hte_l[:, j, :], hi[:, jj, :], start=j == 0, stop=False)
                        PE.matmul(out, hte_h[:, j, :], lo[:, jj, :], start=False, stop=False)
                        last = PE.matmul(out, hte_h[:, j, :], hi[:, jj, :], start=False, stop=j == KD - 1)
                    last.then_inc(sig("piece_used"), 1)

            def down(it, c):
                pe.wait_ge(*at("tr_out", it * NSTEP + c + 2))
                if c == 0:
                    pe.wait_ge(*at("y0_out", it + 1))
                    pe.wait_ge(*at("y1_out", it + 1))
                for part in range(2):
                    hi, lo = split_piece(it, "d", c, part)
                    for kk in range(KF // 2):
                        k = part * (KF // 2) + kk
                        for lhs, rhs in ((act_l, hi), (act_h, lo), (act_h, hi)):
                            for hf in range(YC):
                                last = PE.matmul(bank[5 + hf][:, :], lhs[:, c % 2, k, :], rhs[:, kk, hf * CHUNK_COLS:(hf + 1) * CHUNK_COLS],
                                                 start=c == 0 and k == 0 and lhs is act_l,
                                                 stop=c == NSTEP - 1 and k == KF - 1 and lhs is act_h and rhs is hi)
                    last.then_inc(sig("piece_used"), 1)

            def pe_expert(it, more):
                pe.wait_ge(*at("hte", it * 2 + 2))
                for c in range(NSTEP):
                    pe.wait_ge(*at("act_done", it * NSTEP + c + 1))
                    if c == 1:
                        pe.wait_ge(*at("added", (it + 1) * (NTT * YC)))
                    product(it, "g", c, bank[c % 2 * 2][:, :])
                    if c == 0:
                        pe.wait_ge(*at("tr_out", it * NSTEP + 1))
                        for i, (t0, n) in enumerate(TOK):
                            last = PE.transpose(bank[4][:, t0:t0 + n], selw[0:n, i, :], ident[0:n, 0:n])
                        last.then_inc(sig("moe_w"), 1)
                    else:
                        transposes(it, c - 1)
                    product(it, "u", c, bank[c % 2 * 2 + 1][:, :])
                    if c:
                        down(it, c - 1)
                transposes(it, NSTEP - 1)
                if more:
                    dispatch(it + 1, 0)
                down(it, NSTEP - 1)
                if more:
                    dispatch(it + 1, 1)
                pe.wait_ge(*at("y0_out", it + 2))
                pe.wait_ge(*at("y1_out", it + 2))
                if more:
                    pe.wait_ge(*at("hte", it * 2 + 4))
                for k in range(NTT * YC):
                    i, hf = divmod(k, YC)
                    t0, n = TOK[i]
                    if k >= 3:
                        pe.wait_ge(*at("added", (it + 1) * (NTT * YC) + (k - 2)))
                    PE.matmul(bank[(7, 3, 2)[k % 3]][0:n, :], WT[:, t0:t0 + n], y_e[:, hf * CHUNK_COLS:(hf + 1) * CHUNK_COLS],
                              start=True, stop=True).then_inc(sig("moe_c"), 1)

            for r in range(2):
                dispatch(0, r)
            with pe.Fori(0, NE - 1) as e:
                pe_expert(e, True)
            pe_expert(NE - 1, False)
            with pe.If(pe.value_load(count_i[0:1, 0:1], min_val=0, max_val=T) > CAP):
                with pe.Fori(1, PASSES) as p:
                    with pe.Fori(0, NE) as e:
                        pe.wait_ge(*at("added", (p * NE + e + 1) * (NTT * YC)))
                        for r in range(2):
                            dispatch(p * NE + e, r)
                        pe_expert(p * NE + e, False)


INPUTS = ["x_prompt", "x_sample", "cache_k", "cache_v", "state_lru_conv", "state_lru_h", "state_delta_conv",
          "state_delta_s", "page_table", "ln_mix_e", "w_in_e", "conv_lru_w", "conv_lru_b", "lru_wx", "lru_bx",
          "lru_wa", "lru_ba", "lru_lambda", "qk_gain_q", "qk_gain_k", "lam_q1", "lam_k1", "lam_q2", "lam_k2",
          "subln_g", "w_out_e", "ln_ffn_e", "ffn_wg", "ffn_wu", "ffn_wd", "ln_mix_o", "w_in_o", "conv_delta_w",
          "a_log", "dt_bias", "onorm_g", "w_out_o", "ln_ffn_o", "router_w", "moe_wg", "moe_wu", "moe_wd"]
OUTPUTS = ["y_prompt", "y_sample", "k_prompt", "v_prompt", "lru_conv_prompt", "lru_h_prompt", "delta_conv_prompt",
           "delta_s_prompt", "k_sample", "v_sample", "lru_conv_sample", "lru_h_sample", "delta_conv_sample",
           "delta_s_sample"]


def output_shapes(s):
    _, bp, tp, d = (1,) + s["x_prompt"]
    bs, ts, _ = s["x_sample"]
    hb, e = s["cache_k"][3:]
    hist, lw = s["state_lru_conv"][2:]
    qkv = s["state_delta_conv"][3]
    hc, dk, dv = s["state_delta_s"][2:]
    return {"y_prompt": (bp, tp, d), "y_sample": (bs, ts, d),
            "k_prompt": (1, bp, tp, hb, e), "v_prompt": (1, bp, tp, hb, e),
            "lru_conv_prompt": (1, bp, hist, lw), "lru_h_prompt": (1, bp, lw),
            "delta_conv_prompt": (1, bp, hist, qkv), "delta_s_prompt": (1, bp, hc, dk, dv),
            "k_sample": (1, bs, ts, hb, e), "v_sample": (1, bs, ts, hb, e),
            "lru_conv_sample": (1, bs, hist, lw), "lru_h_sample": (1, bs, lw),
            "delta_conv_sample": (1, bs, hist, qkv), "delta_s_sample": (1, bs, hc, dk, dv)}


def kernel(**inputs):
    import numpy as np
    import concourse.bacc as bacc
    from concourse.bass_utils import run_bass_kernel_spmd

    nc = bacc.Bacc("TRN2", target_bir_lowering=False, num_devices=1)
    arrays = {f"in_{n}": np.ascontiguousarray(inputs[n]) for n in INPUTS}
    A = {n: nc.dram_tensor(f"in_{n}", arrays[f"in_{n}"].shape, mybir.dt.from_np(arrays[f"in_{n}"].dtype),
                           kind="ExternalInput").ap() for n in INPUTS}
    shapes = output_shapes({n: arrays[f"in_{n}"].shape for n in INPUTS})
    O = {n: nc.dram_tensor(f"out_{n}", shapes[n], F32, kind="ExternalOutput").ap() for n in OUTPUTS}
    program(nc, A, O)
    r = run_bass_kernel_spmd(nc, [arrays], core_ids=[0])
    return tuple(r.results[0][f"out_{n}"] for n in OUTPUTS)
```
